# Optimizing a Trainium2 kernel written in Bass

```python
import math
import jax
import jax.numpy as jnp
from jax import lax
import numpy as np

D_MODEL = 1024
BATCH = 1
SEQ = 2048
DEPTH = 1

CTX_LEN = 256
GRID_W = 64
D_MIX = D_MODEL
CHUNK = 128
EPS = 1e-6
RET_HEADS = 4
RET_WIDTH = D_MIX // 2
RET_DK = RET_WIDTH // RET_HEADS
RET_DV = RET_WIDTH // RET_HEADS
ROPE_BASE = 10000.0
SSD_WIDTH = D_MIX - RET_WIDTH
SSD_HEADDIM = 64
SSD_HEADS = SSD_WIDTH // SSD_HEADDIM
SSD_GROUPS = 2
SSD_HPG = SSD_HEADS // SSD_GROUPS
SSD_STATE = 128
SSD_CONV = 5
SSD_CONV_CH = SSD_WIDTH + 2 * SSD_GROUPS * SSD_STATE
D_PROJ = 4 * RET_WIDTH + SSD_WIDTH + SSD_CONV_CH + 2 * SSD_HEADS
MOE_GROUPS = 4
EXPERTS_PER_GROUP = 8
N_EXPERTS = MOE_GROUPS * EXPERTS_PER_GROUP
TOP_K = 2
D_EXPERT = D_MODEL // 2
MOE_BLOCK = 128

kernel_name = "hybrid_retention_ssd_hmoe_prefix_dit"

def rmsnorm(x, w):
    xf = x.astype(jnp.float32)
    y = xf * lax.rsqrt(jnp.mean(xf * xf, axis=-1, keepdims=True) + EPS)
    return (y * w.astype(jnp.float32)).astype(x.dtype)

def head_norm(y, w):
    b, L, H, d = y.shape
    yf = y.astype(jnp.float32)
    mu = jnp.mean(yf, axis=-1, keepdims=True)
    var = jnp.mean(jnp.square(yf - mu), axis=-1, keepdims=True)
    yn = ((yf - mu) * lax.rsqrt(var + EPS)).reshape(b, L, H * d)
    return (yn * w.astype(jnp.float32)).astype(y.dtype)

def split_proj(p):
    parts = []
    start = 0
    for size in (RET_WIDTH, RET_WIDTH, RET_WIDTH, RET_WIDTH, SSD_WIDTH, SSD_CONV_CH, SSD_HEADS, SSD_HEADS):
        parts.append(p[..., start:start + size])
        start += size
    return parts

def axial_rope(t, row_id, col_id):
    half = t.shape[-1] // 2
    quarter = half // 2
    freqs = ROPE_BASE ** (-jnp.arange(quarter, dtype=jnp.float32) / quarter)

    def rotate(u, pos):
        ang = pos.astype(jnp.float32)[:, None] * freqs
        cos = jnp.cos(ang)[None, :, None, :]
        sin = jnp.sin(ang)[None, :, None, :]
        u1 = u[..., :quarter].astype(jnp.float32)
        u2 = u[..., quarter:].astype(jnp.float32)
        return jnp.concatenate([u1 * cos - u2 * sin, u1 * sin + u2 * cos], axis=-1).astype(u.dtype)

    return jnp.concatenate([rotate(t[..., :half], row_id), rotate(t[..., half:], col_id)], axis=-1)

def to_chunks(t):
    b, L = t.shape[:2]
    return jnp.moveaxis(t.reshape(b, L // CHUNK, CHUNK, *t.shape[2:]), 1, 0)

def from_chunks(t):
    n, b, c = t.shape[:3]
    return jnp.moveaxis(t, 0, 1).reshape(b, n * c, *t.shape[3:])

def flip_seq(t):
    return jnp.flip(t, axis=1)

def retention_scan(q, k, v, log_g, s0, strict):
    dt = q.dtype
    idx = jnp.arange(CHUNK, dtype=jnp.float32)
    rel = idx[:, None] - idx[None, :]
    mask = (rel > 0) if strict else (rel >= 0)
    decay_in = jnp.where(mask[..., None], jnp.exp(jnp.maximum(rel, 0.0)[..., None] * log_g), 0.0)
    decay_in = jnp.moveaxis(decay_in, -1, 0).astype(dt)
    decay_q = jnp.exp((idx + 1.0)[:, None] * log_g).astype(dt)
    decay_k = jnp.exp((CHUNK - 1.0 - idx)[:, None] * log_g).astype(dt)
    decay_chunk = jnp.exp(CHUNK * log_g).astype(dt)

    def step(s, inp):
        qc, kc, vc = inp
        scores = jnp.einsum('bnhd,bmhd->bhnm', qc, kc) * decay_in
        inner = jnp.einsum('bhnm,bmhe->bnhe', scores, vc)
        cross = jnp.einsum('bnhd,bhde->bnhe', qc, s) * decay_q[None, :, :, None]
        s_new = decay_chunk[None, :, None, None] * s + jnp.einsum('bmhd,bmhe,mh->bhde', kc, vc, decay_k)
        return s_new.astype(dt), inner + cross

    s_fin, y = lax.scan(step, s0.astype(dt), (to_chunks(q), to_chunks(k), to_chunks(v)))
    return from_chunks(y), s_fin

def retention_state(k, v, log_g):
    L = k.shape[1]
    w = jnp.exp((L - 1.0 - jnp.arange(L, dtype=jnp.float32))[:, None] * log_g).astype(k.dtype)
    return jnp.einsum('bmhd,bmhe,mh->bhde', k, v, w)

def retention_group(q, k, v, g, qc, kc, vc, gc, decay_f, decay_b, gn_w, need_ctx):
    b = q.shape[0]
    lg_f = -jnp.exp(decay_f.astype(jnp.float32))
    lg_b = -jnp.exp(decay_b.astype(jnp.float32))
    if need_ctx:
        s0 = jnp.zeros((b, RET_HEADS, RET_DK, RET_DV), q.dtype)
        yc_f, s_f = retention_scan(qc, kc, vc, lg_f, s0, False)
        yc_b, s_b = retention_scan(flip_seq(qc), flip_seq(kc), flip_seq(vc), lg_b, s0, True)
        yc = head_norm(yc_f + flip_seq(yc_b), gn_w) * jax.nn.silu(gc)
    else:
        s_f = retention_state(kc, vc, lg_f)
        s_b = retention_state(flip_seq(kc), flip_seq(vc), lg_b)
        yc = None
    y_f, _ = retention_scan(q, k, v, lg_f, s_f, False)
    y_b, _ = retention_scan(flip_seq(q), flip_seq(k), flip_seq(v), lg_b, s_b, True)
    y = head_norm(y_f + flip_seq(y_b), gn_w) * jax.nn.silu(g)
    return y, yc

def short_conv(u, w, bias):
    pad = SSD_CONV // 2
    out = lax.conv_general_dilated(u, w[:, None, :].astype(u.dtype), window_strides=(1,),
                                   padding=[(pad, pad)], dimension_numbers=('NWC', 'WIO', 'NWC'),
                                   feature_group_count=u.shape[-1])
    return out + bias

def ssd_inputs(xbc, dt_f_raw, dt_b_raw, conv_w, conv_b, dt_bias_f, dt_bias_b, a_f, a_b):
    u = jax.nn.silu(short_conv(xbc, conv_w, conv_b))
    b, L, _ = u.shape
    gn = SSD_GROUPS * SSD_STATE
    xs = u[..., :SSD_WIDTH].reshape(b, L, SSD_GROUPS, SSD_HPG, SSD_HEADDIM)
    bm = u[..., SSD_WIDTH:SSD_WIDTH + gn].reshape(b, L, SSD_GROUPS, SSD_STATE)
    cm = u[..., SSD_WIDTH + gn:].reshape(b, L, SSD_GROUPS, SSD_STATE)

    def discretise(raw, bias, a):
        dt = jax.nn.softplus(raw.astype(jnp.float32) + bias.astype(jnp.float32))
        dt = dt.reshape(b, L, SSD_GROUPS, SSD_HPG)
        return dt, dt * a

    dt_f, da_f = discretise(dt_f_raw, dt_bias_f, a_f)
    dt_b, da_b = discretise(dt_b_raw, dt_bias_b, a_b)
    return xs, bm, cm, dt_f, da_f, dt_b, da_b

def ssd_scan(xs, dt, da, bm, cm, s0, strict):
    dtype = xs.dtype
    idx = jnp.arange(CHUNK)
    mask = (idx[:, None] > idx[None, :]) if strict else (idx[:, None] >= idx[None, :])
    dtx = dt.astype(dtype)[..., None] * xs

    def step(s, inp):
        xc, ac, bc, cc = inp
        acum = jnp.cumsum(ac, axis=1)
        seg = acum[:, :, None] - acum[:, None, :]
        lmat = jnp.exp(jnp.where(mask[None, :, :, None, None], seg, -jnp.inf)).astype(dtype)
        cb = jnp.einsum('bngs,bmgs->bgnm', cc, bc)
        y_in = jnp.einsum('bgnm,bnmgr,bmgrp->bngrp', cb, lmat, xc)
        y_st = jnp.einsum('bngs,bgrps->bngrp', cc, s) * jnp.exp(acum).astype(dtype)[..., None]
        w = jnp.exp(acum[:, -1:] - acum).astype(dtype)
        s_new = jnp.exp(acum[:, -1]).astype(dtype)[..., None, None] * s + jnp.einsum('bmgs,bmgr,bmgrp->bgrps', bc, w, xc)
        return s_new.astype(dtype), y_in + y_st

    s_fin, y = lax.scan(step, s0.astype(dtype), (to_chunks(dtx), to_chunks(da), to_chunks(bm), to_chunks(cm)))
    return from_chunks(y), s_fin

def ssd_state(xs, dt, da, bm):
    dtx = dt.astype(xs.dtype)[..., None] * xs
    acum = jnp.cumsum(da, axis=1)
    w = jnp.exp(acum[:, -1:] - acum).astype(xs.dtype)
    return jnp.einsum('bmgs,bmgr,bmgrp->bgrps', bm, w, dtx)

def ssd_output(y, xs, z, d_skip, norm_w):
    b, L = y.shape[:2]
    y = (y + d_skip.reshape(SSD_GROUPS, SSD_HPG)[:, :, None].astype(y.dtype) * xs).reshape(b, L, SSD_WIDTH)
    return rmsnorm(y * jax.nn.silu(z), norm_w)

def ssd_group(z, xbc, dtf, dtb, zc, xbcc, dtfc, dtbc, conv_w, conv_b, dt_bias_f, dt_bias_b,
              a_log_f, a_log_b, d_skip, norm_w, need_ctx):
    a_f = -jnp.exp(a_log_f.astype(jnp.float32)).reshape(SSD_GROUPS, SSD_HPG)
    a_b = -jnp.exp(a_log_b.astype(jnp.float32)).reshape(SSD_GROUPS, SSD_HPG)
    xs, bm, cm, dt_f, da_f, dt_b, da_b = ssd_inputs(xbc, dtf, dtb, conv_w, conv_b, dt_bias_f, dt_bias_b, a_f, a_b)
    xsc, bmc, cmc, dtc_f, dac_f, dtc_b, dac_b = ssd_inputs(xbcc, dtfc, dtbc, conv_w, conv_b, dt_bias_f, dt_bias_b, a_f, a_b)
    if need_ctx:
        b = xs.shape[0]
        s0 = jnp.zeros((b, SSD_GROUPS, SSD_HPG, SSD_HEADDIM, SSD_STATE), xs.dtype)
        yc_f, s_f = ssd_scan(xsc, dtc_f, dac_f, bmc, cmc, s0, False)
        yc_b, s_b = ssd_scan(flip_seq(xsc), flip_seq(dtc_b), flip_seq(dac_b), flip_seq(bmc), flip_seq(cmc), s0, True)
        yc = ssd_output(yc_f + flip_seq(yc_b), xsc, zc, d_skip, norm_w)
    else:
        s_f = ssd_state(xsc, dtc_f, dac_f, bmc)
        s_b = ssd_state(flip_seq(xsc), flip_seq(dtc_b), flip_seq(dac_b), flip_seq(bmc))
        yc = None
    y_f, _ = ssd_scan(xs, dt_f, da_f, bm, cm, s_f, False)
    y_b, _ = ssd_scan(flip_seq(xs), flip_seq(dt_b), flip_seq(da_b), flip_seq(bm), flip_seq(cm), s_b, True)
    y = ssd_output(y_f + flip_seq(y_b), xs, z, d_skip, norm_w)
    return y, yc

def token_mixing(h, hc, w_in, w_out, ret_decay_f, ret_decay_b, ret_gn_w, conv_w, conv_b,
                 dt_bias_f, dt_bias_b, a_log_f, a_log_b, d_skip, ssd_norm_w, row_id, col_id, need_ctx):
    b, L, _ = h.shape
    lc = hc.shape[1]
    q, k, v, g, z, xbc, dtf, dtb = split_proj(h @ w_in)
    qc, kc, vc, gc, zc, xbcc, dtfc, dtbc = split_proj(hc @ w_in)
    scale = RET_DK ** -0.5
    q = axial_rope(q.reshape(b, L, RET_HEADS, RET_DK), row_id, col_id)
    k = axial_rope(k.reshape(b, L, RET_HEADS, RET_DK), row_id, col_id) * scale
    v = v.reshape(b, L, RET_HEADS, RET_DV)
    qc = qc.reshape(b, lc, RET_HEADS, RET_DK)
    kc = kc.reshape(b, lc, RET_HEADS, RET_DK) * scale
    vc = vc.reshape(b, lc, RET_HEADS, RET_DV)
    yr, yrc = retention_group(q, k, v, g, qc, kc, vc, gc, ret_decay_f, ret_decay_b, ret_gn_w, need_ctx)
    ys, ysc = ssd_group(z, xbc, dtf, dtb, zc, xbcc, dtfc, dtbc, conv_w, conv_b, dt_bias_f, dt_bias_b,
                        a_log_f, a_log_b, d_skip, ssd_norm_w, need_ctx)
    y = jnp.concatenate([yr, ys], axis=-1) @ w_out
    yc = jnp.concatenate([yrc, ysc], axis=-1) @ w_out if need_ctx else None
    return y, yc

def hier_moe(h, w_rg, b_rg, w_re, b_re, w_gate, w_up, w_down):
    T, d = h.shape
    lg = (h @ w_rg + b_rg).astype(jnp.float32)
    grp = jnp.argmax(lg, axis=-1)
    gate_g = jnp.take_along_axis(jax.nn.softmax(lg, axis=-1), grp[:, None], axis=1)[:, 0]
    le = (jnp.einsum('td,gde->tge', h, w_re) + b_re).astype(jnp.float32)
    le_sel = jnp.take_along_axis(le, grp[:, None, None], axis=1)[:, 0]
    top_v, top_i = lax.top_k(le_sel, TOP_K)
    w_top = jax.nn.softmax(top_v, axis=-1) * gate_g[:, None]
    expert = grp[:, None] * EXPERTS_PER_GROUP + top_i

    tk = T * TOP_K
    flat_e = expert.reshape(-1)
    flat_t = jnp.repeat(jnp.arange(T, dtype=jnp.int32), TOP_K)
    flat_w = w_top.reshape(-1)
    order = jnp.argsort(flat_e)
    se, st, sw = flat_e[order], flat_t[order], flat_w[order]
    counts = jnp.bincount(flat_e, length=N_EXPERTS)
    starts = jnp.cumsum(counts) - counts
    padded = (counts + MOE_BLOCK - 1) // MOE_BLOCK * MOE_BLOCK
    pad_end = jnp.cumsum(padded)
    pad_start = pad_end - padded
    dest = pad_start[se] + (jnp.arange(tk) - starts[se])
    n_blocks = -(-(tk + N_EXPERTS * (MOE_BLOCK - 1)) // MOE_BLOCK)
    cap = n_blocks * MOE_BLOCK
    slot_tok = jnp.full((cap,), T, jnp.int32).at[dest].set(st)
    slot_w = jnp.zeros((cap,), h.dtype).at[dest].set(sw.astype(h.dtype))
    blk_expert = jnp.minimum(jnp.searchsorted(pad_end, jnp.arange(n_blocks) * MOE_BLOCK, side='right'), N_EXPERTS - 1)
    h_pad = jnp.concatenate([h, jnp.zeros((1, d), h.dtype)], axis=0)

    def expert_block(args):
        tok, e = args
        xb = h_pad[tok]
        hid = jax.nn.silu(xb @ w_gate[e]) * (xb @ w_up[e])
        return hid @ w_down[e]

    yb = lax.map(expert_block, (slot_tok.reshape(n_blocks, MOE_BLOCK), blk_expert))
    out = jnp.zeros((T + 1, d), h.dtype).at[slot_tok].add(yb.reshape(cap, d) * slot_w[:, None])
    return out[:T]

def setup_inputs(seed: int = 0) -> dict:
    key = jax.random.key(seed)
    ks = iter(jax.random.split(key, 48))
    f32 = jnp.float32

    def nrm(shape, scale):
        return jax.random.normal(next(ks), shape, f32) * scale

    def gain(shape):
        return 1.0 + 0.05 * jax.random.normal(next(ks), shape, f32)

    ret_base = jnp.log(-jnp.log1p(-(2.0 ** (-5.0 - jnp.arange(RET_HEADS, dtype=f32)))))

    def dt_bias():
        dt = jnp.exp(jax.random.uniform(next(ks), (DEPTH, SSD_HEADS), f32, math.log(1e-3), math.log(1e-1)))
        return dt + jnp.log(-jnp.expm1(-dt))

    def a_log():
        return jnp.log(jax.random.uniform(next(ks), (DEPTH, SSD_HEADS), f32, 1.0, 16.0))

    return {
        'x': nrm((BATCH, SEQ, D_MODEL), 1.0),
        'c': nrm((BATCH, D_MODEL), 1.0),
        'ctx': nrm((BATCH, CTX_LEN, D_MODEL), 1.0),
        'c_ctx': nrm((D_MODEL,), 1.0),
        'w_mod': nrm((DEPTH, D_MODEL, 6 * D_MODEL), 0.5 * D_MODEL ** -0.5),
        'b_mod': nrm((DEPTH, 6 * D_MODEL), 0.02),
        'norm_pre_mix': gain((DEPTH, D_MODEL)),
        'norm_post_mix': gain((DEPTH, D_MODEL)),
        'norm_pre_ffn': gain((DEPTH, D_MODEL)),
        'norm_post_ffn': gain((DEPTH, D_MODEL)),
        'w_in': nrm((DEPTH, D_MODEL, D_PROJ), D_MODEL ** -0.5),
        'w_out': nrm((DEPTH, D_MIX, D_MODEL), D_MIX ** -0.5),
        'ret_decay_f': ret_base + nrm((DEPTH, RET_HEADS), 0.1),
        'ret_decay_b': ret_base + nrm((DEPTH, RET_HEADS), 0.1),
        'ret_gn_w': gain((DEPTH, RET_WIDTH)),
        'ssd_conv_w': nrm((DEPTH, SSD_CONV, SSD_CONV_CH), SSD_CONV ** -0.5),
        'ssd_conv_b': nrm((DEPTH, SSD_CONV_CH), 0.02),
        'ssd_dt_bias_f': dt_bias(),
        'ssd_dt_bias_b': dt_bias(),
        'ssd_a_log_f': a_log(),
        'ssd_a_log_b': a_log(),
        'ssd_d': gain((DEPTH, SSD_HEADS)),
        'ssd_norm_w': gain((DEPTH, SSD_WIDTH)),
        'moe_w_rg': nrm((DEPTH, D_MODEL, MOE_GROUPS), D_MODEL ** -0.5),
        'moe_b_rg': nrm((DEPTH, MOE_GROUPS), 0.01),
        'moe_w_re': nrm((DEPTH, MOE_GROUPS, D_MODEL, EXPERTS_PER_GROUP), D_MODEL ** -0.5),
        'moe_b_re': nrm((DEPTH, MOE_GROUPS, EXPERTS_PER_GROUP), 0.01),
        'moe_w_gate': nrm((DEPTH, N_EXPERTS, D_MODEL, D_EXPERT), D_MODEL ** -0.5),
        'moe_w_up': nrm((DEPTH, N_EXPERTS, D_MODEL, D_EXPERT), D_MODEL ** -0.5),
        'moe_w_down': nrm((DEPTH, N_EXPERTS, D_EXPERT, D_MODEL), D_EXPERT ** -0.5),
    }

def reference(x, c, ctx, c_ctx, w_mod, b_mod, norm_pre_mix, norm_post_mix, norm_pre_ffn, norm_post_ffn,
              w_in, w_out, ret_decay_f, ret_decay_b, ret_gn_w, ssd_conv_w, ssd_conv_b,
              ssd_dt_bias_f, ssd_dt_bias_b, ssd_a_log_f, ssd_a_log_b, ssd_d, ssd_norm_w,
              moe_w_rg, moe_b_rg, moe_w_re, moe_b_re, moe_w_gate, moe_w_up, moe_w_down):
    b, L, d = x.shape
    lc = ctx.shape[1]
    rows = L // GRID_W
    row_id = jnp.repeat(jnp.arange(rows), GRID_W)
    col_id = jnp.tile(jnp.arange(GRID_W), rows)
    act_c = jax.nn.silu(c)
    act_cc = jax.nn.silu(c_ctx)
    for l in range(DEPTH):
        need_ctx = l < DEPTH - 1
        mod = act_c @ w_mod[l] + b_mod[l]
        modc = act_cc @ w_mod[l] + b_mod[l]
        sh1, sc1, g1, sh2, sc2, g2 = [m[:, None, :] for m in jnp.split(mod, 6, axis=-1)]
        sh1c, sc1c, g1c, sh2c, sc2c, g2c = jnp.split(modc, 6, axis=-1)

        h = rmsnorm(x, norm_pre_mix[l]) * (1.0 + sc1) + sh1
        hc = rmsnorm(ctx, norm_pre_mix[l]) * (1.0 + sc1c) + sh1c
        y, yc = token_mixing(h, hc, w_in[l], w_out[l], ret_decay_f[l], ret_decay_b[l], ret_gn_w[l],
                             ssd_conv_w[l], ssd_conv_b[l], ssd_dt_bias_f[l], ssd_dt_bias_b[l],
                             ssd_a_log_f[l], ssd_a_log_b[l], ssd_d[l], ssd_norm_w[l], row_id, col_id, need_ctx)
        x = x + g1 * rmsnorm(y, norm_post_mix[l])

        h = rmsnorm(x, norm_pre_ffn[l]) * (1.0 + sc2) + sh2
        tokens = h.reshape(b * L, d)
        if need_ctx:
            ctx = ctx + g1c * rmsnorm(yc, norm_post_mix[l])
            hc = rmsnorm(ctx, norm_pre_ffn[l]) * (1.0 + sc2c) + sh2c
            tokens = jnp.concatenate([tokens, hc.reshape(b * lc, d)], axis=0)
        out = hier_moe(tokens, moe_w_rg[l], moe_b_rg[l], moe_w_re[l], moe_b_re[l],
                       moe_w_gate[l], moe_w_up[l], moe_w_down[l])
        x = x + g2 * rmsnorm(out[:b * L].reshape(b, L, d), norm_post_ffn[l])
        if need_ctx:
            ctx = ctx + g2c * rmsnorm(out[b * L:].reshape(b, lc, d), norm_post_ffn[l])
    return x


_drawn_inputs = setup_inputs


def setup_inputs(seed=0):
    import zlib

    import numpy as np

    out = dict(_drawn_inputs(seed))
    spreads = {}
    factors = {'norm_post_ffn': 3.783, 'ssd_d': 3.389, 'moe_b_re': 3.19}
    for name, (base, spread) in spreads.items():
        noise = np.random.default_rng([zlib.crc32(name.encode()), seed]).standard_normal(out[name].shape)
        drawn = base * np.exp(spread * noise) if base else spread * noise
        out[name] = jnp.asarray(drawn.astype(out[name].dtype))
    for name, factor in factors.items():
        out[name] = (out[name] * factor).astype(out[name].dtype)
    return out
```

```python
from contextlib import ExitStack

import numpy as np
import concourse.bass as bass
from concourse import mybir

F32 = mybir.dt.float32
I32 = mybir.dt.int32
ALU = mybir.AluOpType
ACT = mybir.ActivationFunctionType
AX = mybir.AxisListType.X

P = 128
D = 1024
KD = D // P
SEQ = 2048
CTX = 256
NT = (SEQ + CTX) // P
NCT = CTX // P
NL = SEQ // P
RH = 4
RW = 512
SH = 8
SP_ = 64
SG = 2
DPROJ = 3600
NTOK = 5 * 512 + 16
NCH = 8
CONV = 5
NG = 4
EPG = 8
NE = 32
DE = 512
ROWS = 2 * SEQ + P
EPS = 1e-6
EPS_OF = {1: 0, 512: 4, D: 8}


class Counter:

    def __init__(self, sem, per=1, credit=0):
        self.sem, self.per, self.credit = sem, per, credit

    def at(self, turn, n=None):
        return turn * self.per + (self.credit + (self.per if n is None else n))


class Landing:

    def __init__(self, sems, dmas=1, credit=0):
        self.sems, self.dmas, self.credit = sems, dmas, credit

    def sem(self, slot):
        return self.sems[slot]

    def at(self, use):
        return use * (16 * self.dmas) + (16 * self.dmas + self.credit)


class Kit:

    def __init__(self, nc):
        self.nc = nc
        self.keep = ExitStack()
        self.sems = []

    def semaphore(self, name):
        self.sems.append(self.nc.alloc_semaphore(name))
        return self.sems[-1]

    def counter(self, name, per=1, credit=0):
        return Counter(self.semaphore(name), per, credit)

    def landing(self, name, slots=1, dmas=1, credit=0):
        return Landing([self.semaphore(f"{name}{s}") for s in range(slots)], dmas, credit)

    def retire(self):
        self.nc.clear_and_free_semaphores(self.sems)
        self.nc.all_engine_barrier()
        self.sems = []

    def sb(self, name, shape, dt=F32, stack=None):
        return (stack or self.keep).enter_context(self.nc.sbuf_tensor(name, shape, dt))

    def ps(self, name, shape, stack):
        return stack.enter_context(self.nc.psum_tensor(name, shape, F32))


def pairs(eng, first, last):
    with eng.Fori(0, (last - first) // 2) as i:
        for s in range(2):
            yield i * 2 + (first + s), i, s


def globals_of(kit):
    return {
        "ident": kit.sb("ident", [P, P]),
        "mod": kit.sb("mod", [P, 6 * D]),
        "cols": kit.sb("cols", [P, 2, KD, 2]),
        "neghalf": kit.sb("neghalf", [P, 16]),
        "eps": kit.sb("eps", [P, 12]),
    }


def mixing_globals_of(kit, st):
    return {
        "E": kit.sb("E", [P, NT, 6, SH], stack=st),
        "dd": kit.sb("dd", [P, NT, 4, SH], stack=st),
        "dskip": kit.sb("dskip", [P, SH], stack=st),
        "wn": kit.sb("wn", [P, KD], stack=st),
        "DT": kit.sb("DT", [P, RH, P], stack=st),
        "Dq": kit.sb("Dq", [P, 2, RH, P], stack=st),
        "Dk": kit.sb("Dk", [P, 2, RH], stack=st),
        "Dtot": kit.sb("Dtot", [P, 2, RH], stack=st),
        "sf": kit.sb("sf", [P, 2, 2, 512], stack=st),
    }


def routing_globals_of(kit):
    return {
        "tri": kit.sb("tri", [P, 5, P]),
        "logits": kit.sb("logits", [P, NL, NG + NE]),
        "slots": kit.sb("slots", [P, 2, NL], I32),
        "wtop": kit.sb("wtop", [P, 2, NL]),
        "spans": kit.sb("spans", [1, 2, NE], I32),
    }


def tile_of(dram, t, lo=None, hi=None):
    v = dram[bass.ds(t, 1), :, :] if lo is None else dram[bass.ds(t, 1), :, lo:hi]
    return v.rearrange("o p f -> p (o f)")


def modulation(nc, kit, io, g, dram):
    NMOD = 12
    with ExitStack() as st:
        ccol = kit.sb("ccol", [P, 2, KD], stack=st)
        csil = kit.sb("csil", [P, 2, KD], stack=st)
        both = kit.sb("both", [P, KD, P], stack=st)
        lat = kit.sb("lat", [P, KD, P], stack=st)
        wm = kit.sb("wm", [P, 2, KD, 512], stack=st)
        bm = kit.sb("bm", [P, 2, 512], stack=st)
        nrow = kit.sb("nrow", [P, 3, D], stack=st)
        ncol = kit.sb("ncol", [P, KD], stack=st)
        acc = kit.ps("mod_acc", [P, 2, 512], st)
        colT = kit.ps("mod_colT", [P, 4, 4, P], st)
        c_in = kit.landing("c_in", dmas=2)
        w_in = kit.landing("wmod_in", 2, dmas=2)
        n_in = kit.landing("norm_rows_in", dmas=5)
        silu = kit.counter("c_silu")
        spread = kit.counter("c_spread", 3)
        row_acc = kit.counter("mod_row_acc", 1, credit=2)
        row = kit.counter("mod_row", 1, credit=2)
        cols_t = kit.counter("mod_cols_t")
        fin = kit.counter("mod_final", 2)
        block = st.enter_context(nc.Block())

        @block.sync
        def _(sp):
            for n, src in enumerate((io["c"].rearrange("a d -> (a d)"), io["c_ctx"])):
                sp.dma_start(ccol[:, n, :], src.rearrange("(k p) -> p k", p=P), allow_slow_non_contiguous=True).then_inc(c_in.sem(0), 16)
            for n, src in enumerate(("norm_post_mix", "norm_pre_ffn", "norm_post_ffn")):
                sp.dma_start(nrow[:, n, :], io[src].to_broadcast([P, D])).then_inc(n_in.sem(0), 16)
            sp.dma_start(ncol[:, :], io["norm_pre_mix"].rearrange("o (k p) -> p (o k)", p=P), allow_slow_non_contiguous=True).then_inc(n_in.sem(0), 16)
            sp.dma_start(g["ident"][:, :], io["ident"]).then_inc(n_in.sem(0), 16)
            wsrc = io["w_mod"].rearrange("o (k p) (n f) -> n p (o k) f", p=P, f=512)
            bsrc = io["b_mod"].rearrange("o (n f) -> n o f", f=512)
            for t, use, s in pairs(sp, 0, NMOD):
                sp.wait_ge(row_acc.sem, row_acc.at(t - 2))
                sp.wait_ge(row.sem, row.at(t - 2))
                sp.dma_start(wm[:, s], wsrc[bass.ds(t, 1)].rearrange("o p k f -> p (o k) f")).then_inc(w_in.sem(s), 16)
                sp.dma_start(bm[:, s], bsrc[bass.ds(t, 1)].rearrange("a o f -> (a o) f").to_broadcast([P, 512])).then_inc(w_in.sem(s), 16)

        @block.gpsimd
        def _(pool):
            nc.gpsimd.memset(g["neghalf"][:], -0.5)
            for count, at in EPS_OF.items():
                nc.gpsimd.memset(g["eps"][:, at:at + 4], count * EPS)

        @block.scalar
        def _(act):
            act.wait_ge(c_in.sem(0), c_in.at(0))
            nc.scalar.activation(csil[:], ccol[:], ACT.Silu).then_inc(silu.sem, 1)

        @block.tensor
        def _(pe):
            pe.sem_inc(row_acc.sem, row_acc.credit)
            pe.wait_ge(spread.sem, spread.at(0))

            def rows(span, stationary):
                for t, use, s in pairs(pe, *span):
                    pe.wait_ge(w_in.sem(s), w_in.at(use + span[0] // 2))
                    pe.wait_ge(row.sem, row.at(t - 2))
                    for k in range(KD):
                        m = nc.tensor.matmul(acc[:, s], stationary[:, k], wm[:, s, k], start=(k == 0), stop=(k == KD - 1))
                    m.then_inc(row_acc.sem, 1)

            rows((0, 4), both)
            rows((4, NMOD), lat)
            pe.wait_ge(row.sem, row.at(NMOD - 1))
            pe.wait_ge(n_in.sem(0), n_in.at(0))
            for b in range(16):
                m = nc.tensor.transpose(colT[:, b // 4, b % 4], g["mod"][:, b * P:(b + 1) * P], g["ident"][:, :])
            m.then_inc(cols_t.sem, 1)

        @block.vector
        def _(dve):
            dve.sem_inc(row.sem, row.credit)
            dve.wait_ge(silu.sem, silu.at(0))
            nc.vector.tensor_copy(both[:, :, 0:64], csil[:, 0, :, None].to_broadcast([P, KD, 64])).then_inc(spread.sem, 1)
            nc.vector.tensor_copy(both[:, :, 64:P], csil[:, 1, :, None].to_broadcast([P, KD, 64])).then_inc(spread.sem, 1)
            nc.vector.tensor_copy(lat[:, :, :], csil[:, 0, :, None].to_broadcast([P, KD, P])).then_inc(spread.sem, 1)
            for t, use, s in pairs(dve, 0, NMOD):
                dve.wait_ge(row_acc.sem, row_acc.at(t))
                dve.wait_ge(w_in.sem(s), w_in.at(use))
                nc.vector.tensor_tensor(g["mod"][:, bass.ds(t * 512, 512)], acc[:, s], bm[:, s], ALU.add).then_inc(row.sem, 1)
            dve.wait_ge(n_in.sem(0), n_in.at(0))
            dve.wait_ge(row.sem, row.at(NMOD - 1))
            g1, sc2, g2 = (g["mod"][:, n * D:(n + 1) * D] for n in (2, 4, 5))
            root = float(D) ** 0.5
            nc.vector.scalar_tensor_tensor(out=g1, in0=g1, scalar=root, in1=nrow[:, 0], op0=ALU.mult, op1=ALU.mult)
            nc.vector.tensor_scalar(sc2, sc2, root, root, ALU.mult, ALU.add).then_inc(fin.sem, 1)
            nc.vector.scalar_tensor_tensor(out=g2, in0=g2, scalar=root, in1=nrow[:, 2], op0=ALU.mult, op1=ALU.mult)
            dve.wait_ge(fin.sem, fin.at(0, 1))
            nc.vector.tensor_tensor(sc2, sc2, nrow[:, 1], ALU.mult)
            dve.wait_ge(cols_t.sem, cols_t.at(0))
            nc.vector.tensor_copy(g["cols"][:, 0], colT[:, 0:2, :, 0:65:64].rearrange("p a b c -> p (a b) c"))
            nc.vector.tensor_copy(g["cols"][:, 1], colT[:, 2:4, :, 0:65:64].rearrange("p a b c -> p (a b) c")).then_inc(fin.sem, 1)
            dve.wait_ge(fin.sem, fin.at(0))
            nc.vector.scalar_tensor_tensor(out=g["cols"][:, 1], in0=g["cols"][:, 1], scalar=1.0,
                                           in1=ncol[:, :, None].to_broadcast([P, KD, 2]), op0=ALU.add, op1=ALU.mult)


def rstd_root(nc, g, pool, eps_added, turn, n, out, ssq, count):
    w = out.shape[-1]
    nc.gpsimd.tensor_tensor(out, ssq, g["eps"][:, EPS_OF[count]:EPS_OF[count] + w], ALU.add).then_inc(eps_added.sem, 1)
    pool.wait_ge(eps_added.sem, eps_added.at(turn, n))
    return nc.gpsimd.tensor_tensor(out, out, g["neghalf"][:, 0:w], ALU.pow)


def projection(nc, kit, io, g, dram):
    NGR = NT // 2
    NO = 15
    OUTS = [("tok", j, n) for j in range(2) for n in range(5)] + [("ch", 0, n) for n in range(4)] + [("dt", 0, 0)]
    ON_DVE = [k == "tok" and n < 2 or k == "ch" and n < 2 for k, _, n in OUTS]
    ORD = [sum(ON_DVE[:o]) if ON_DVE[o] else o - sum(ON_DVE[:o]) for o in range(NO)]
    NDVE = sum(ON_DVE)
    NACT = NO - NDVE
    with ExitStack() as st:
        w = kit.sb("w_in_sb", [P, KD, DPROJ], stack=st)
        xt = kit.sb("xt", [P, 2, D], stack=st)
        xn = kit.sb("xn", [P, 2, D], stack=st)
        hT = kit.sb("hT", [P, KD, 2 * P], stack=st)
        rope = kit.sb("rope", [P, 2, 4, P], stack=st)
        tok = kit.sb("tok", [P, 2, NTOK], stack=st)
        ch = kit.sb("ch", [P, NCH, 2 * P], stack=st)
        ra = kit.sb("ra", [P, 2, 512], stack=st)
        stat = kit.sb("stat", [P, 2, 2], stack=st)
        xT = kit.ps("xT", [P, KD, P], st)
        acc = kit.ps("proj_acc", [P, 5, 512], st)
        wl = kit.landing("w_in_in", dmas=KD)
        x_in = kit.landing("x_in", 2)
        rope_in = kit.landing("rope_in", 2)
        tok_out = kit.landing("tok_out", 2, credit=16)
        ch_out = kit.landing("ch_out", 1, credit=16)
        ssq = kit.counter("x_ssq", 2)
        rstd = kit.counter("x_rstd", 2)
        eps_added = kit.counter("x_eps_added", 2)
        xnorm = kit.counter("x_normed", 2, credit=2)
        xTd = kit.counter("x_transposed", 2, credit=2)
        hTd = kit.counter("hT_ready", 2, credit=2)
        accd = kit.counter("proj_acc_ready", NO, credit=NO)
        rtmp = kit.counter("rope_products", 4)
        edve = kit.counter("proj_out_dve", NDVE, credit=NDVE)
        eact = kit.counter("proj_out_act", NACT, credit=NACT)
        block = st.enter_context(nc.Block())

        def turns(eng, body):
            body(0, True)
            with eng.Fori(1, NGR) as t:
                body(t, False)

        @block.sync
        def _(sp):
            for k in range(KD):
                sp.dma_start(w[:, k], io["w_in"][0, k * P:(k + 1) * P, :]).then_inc(wl.sem(0), 16)

            def load(t, ctx):
                for j in range(2):
                    sp.wait_ge(xnorm.sem, xnorm.at(t - 1, j + 1))
                    src = io["ctx"][0, j * P:(j + 1) * P, :] if ctx else tile_of(io["x"].rearrange("o (t p) d -> (o t) p d", p=P), t * 2 + (j - NCT))
                    sp.dma_start(xt[:, j], src).then_inc(x_in.sem(j), 16)
                    sp.wait_ge(edve.sem, edve.at(t - 1, 2 * j + 2))
                    sp.dma_start(rope[:, j].rearrange("p a b -> p (a b)"), tile_of(io["rope"], t * 2 + j)).then_inc(rope_in.sem(j), 16)

            def store(t):
                sp.wait_ge(edve.sem, edve.at(t, NDVE))
                sp.wait_ge(eact.sem, eact.at(t, NACT))
                sp.dma_start(dram["ch"][:, :, bass.ds(t * (2 * P), 2 * P)].rearrange("c p t -> p c t"), ch[:]).then_inc(ch_out.sem(0), 16)
                for j in range(2):
                    sp.dma_start(tile_of(dram["tok"], t * 2 + j), tok[:, j]).then_inc(tok_out.sem(j), 16)

            for j in range(2):
                sp.sem_inc(tok_out.sem(j), tok_out.credit)
            sp.sem_inc(ch_out.sem(0), ch_out.credit)
            load(0, True)
            with sp.Fori(0, NGR - 1) as t:
                load(t + 1, False)
                store(t)
            store(NGR - 1)
            for j in range(2):
                sp.wait_ge(tok_out.sem(j), tok_out.at(NGR - 1))
            sp.wait_ge(ch_out.sem(0), ch_out.at(NGR - 1))

        @block.gpsimd
        def _(pool):
            with pool.Fori(0, NGR) as t:
                for j in range(2):
                    pool.wait_ge(ssq.sem, ssq.at(t, j + 1))
                    rstd_root(nc, g, pool, eps_added, t, j + 1, stat[:, j, 1:2], stat[:, j, 0:1], D).then_inc(rstd.sem, 1)

        @block.scalar
        def _(act):
            act.sem_inc(hTd.sem, hTd.credit)
            act.sem_inc(eact.sem, eact.credit)

            def body(t, ctx):
                for j in range(2):
                    act.wait_ge(x_in.sem(j), x_in.at(t))
                    act.wait_ge(xTd.sem, xTd.at(t - 1, j + 1))
                    nc.scalar.activation(xn[:, j], xt[:, j], ACT.Square, accum_out=stat[:, j, 0:1]).then_inc(ssq.sem, 1)
                act.wait_ge(accd.sem, accd.at(t - 1, NO))
                for j in range(2):
                    act.wait_ge(xTd.sem, xTd.at(t, j + 1))
                    for k in range(KD):
                        c = 1 if ctx else 0
                        m = nc.scalar.activation(hT[:, k, j * P:(j + 1) * P], xT[:, k], ACT.Identity,
                                                 bias=g["cols"][:, 0, k, c:c + 1], scale=g["cols"][:, 1, k, c:c + 1])
                    m.then_inc(hTd.sem, 1)
                for o, (kind, j, n) in enumerate(OUTS):
                    if ON_DVE[o]:
                        continue
                    act.wait_ge(accd.sem, accd.at(t, o + 1))
                    if kind == "tok":
                        if n == 2:
                            act.wait_ge(tok_out.sem(j), tok_out.at(t - 1))
                        m = nc.scalar.activation(tok[:, j, n * 512:(n + 1) * 512], acc[:, o % 5], ACT.Copy if n == 2 else ACT.Silu)
                    elif kind == "ch":
                        act.wait_ge(ch_out.sem(0), ch_out.at(t - 1))
                        m = nc.scalar.activation(ch[:, 2 * n:2 * n + 2], acc[:, o % 5].rearrange("p (a b) -> p a b", a=2), ACT.Copy)
                    else:
                        m = nc.scalar.activation(tok[:, :, 5 * 512:NTOK], acc[:, o % 5, 0:32].rearrange("p (a b) -> p a b", a=2), ACT.Copy)
                    m.then_inc(eact.sem, 1)
            turns(act, body)

        @block.tensor
        def _(pe):
            pe.sem_inc(xTd.sem, xTd.credit)
            pe.sem_inc(accd.sem, accd.credit)
            pe.wait_ge(wl.sem(0), wl.at(0))

            def free(t, o):
                q, tt = (o - 5, t) if o >= 5 else (o - 5 + NO, t - 1)
                e = edve if ON_DVE[q] else eact
                pe.wait_ge(e.sem, e.at(tt, ORD[q] + 1))

            def body(t, ctx):
                for j in range(2):
                    pe.wait_ge(xnorm.sem, xnorm.at(t, j + 1))
                    pe.wait_ge(hTd.sem, hTd.at(t, j) if j else hTd.at(t - 1, 2))
                    for k in range(KD):
                        m = nc.tensor.transpose(xT[:, k], xn[:, j, k * P:(k + 1) * P], g["ident"][:, :])
                    m.then_inc(xTd.sem, 1)
                pe.wait_ge(hTd.sem, hTd.at(t, 2))
                for o, (kind, j, n) in enumerate(OUTS):
                    free(t, o)
                    bank = acc[:, o % 5]
                    if kind == "tok":
                        for k in range(KD):
                            m = nc.tensor.matmul(bank, hT[:, k, j * P:(j + 1) * P], w[:, k, n * 512:(n + 1) * 512], start=(k == 0), stop=(k == KD - 1))
                    elif kind == "ch":
                        for b in range(2):
                            c0 = 5 * 512 + (2 * n + b) * P
                            for k in range(KD):
                                m = nc.tensor.matmul(bank[:, b * 2 * P:(b + 1) * 2 * P], w[:, k, c0:c0 + P], hT[:, k], start=(k == 0), stop=(k == KD - 1))
                    else:
                        for j in range(2):
                            for k in range(KD):
                                m = nc.tensor.matmul(bank[:, j * 16:(j + 1) * 16], hT[:, k, j * P:(j + 1) * P], w[:, k, DPROJ - 16:DPROJ], start=(k == 0), stop=(k == KD - 1))
                    m.then_inc(accd.sem, 1)
            turns(pe, body)

        @block.vector
        def _(dve):
            dve.sem_inc(xnorm.sem, xnorm.credit)
            dve.sem_inc(edve.sem, edve.credit)

            def body(t, ctx):
                for j in range(2):
                    dve.wait_ge(rstd.sem, rstd.at(t, j + 1))
                    nc.vector.tensor_scalar(xn[:, j], xt[:, j], stat[:, j, 1:2], float(D) ** 0.5, ALU.mult, ALU.mult).then_inc(xnorm.sem, 1)
                for o, (kind, j, n) in enumerate(OUTS):
                    if not ON_DVE[o]:
                        continue
                    dve.wait_ge(accd.sem, accd.at(t, o + 1))
                    if kind == "ch":
                        dve.wait_ge(ch_out.sem(0), ch_out.at(t - 1))
                        nc.vector.tensor_copy(ch[:, 2 * n:2 * n + 2], acc[:, o % 5].rearrange("p (a b) -> p a b", a=2)).then_inc(edve.sem, 1)
                        continue
                    dve.wait_ge(rope_in.sem(j), rope_in.at(t))
                    prev = 2 * j + n
                    dve.wait_ge(edve.sem, edve.at(t, prev) if prev else edve.at(t - 1, NDVE))
                    a = acc[:, o % 5].rearrange("p (h e q i) -> p h e q i", h=RH, e=2, q=2)
                    cos = rope[:, j, 2 * n].rearrange("p (o e i) -> p o e i", o=1, e=2).to_broadcast([P, RH, 2, 64])
                    sin = rope[:, j, 2 * n + 1].rearrange("p (e q i) -> p e q i", e=2, q=2)
                    nc.vector.tensor_tensor(ra[:, 0].rearrange("p (h f) -> p h f", h=RH), acc[:, o % 5].rearrange("p (h f) -> p h f", h=RH),
                                            rope[:, j, 2 * n].unsqueeze(1).to_broadcast([P, RH, P]), ALU.mult)
                    b = ra[:, 1].rearrange("p (h e q i) -> p h e q i", h=RH, e=2, q=2)
                    for q in range(2):
                        m = nc.vector.tensor_tensor(b[:, :, :, q], a[:, :, :, 1 - q], sin[:, :, q].unsqueeze(1).to_broadcast([P, RH, 2, 32]), ALU.mult)
                    m.then_inc(rtmp.sem, 1)
                    dve.wait_ge(rtmp.sem, rtmp.at(t, 2 * j + n + 1))
                    if n == 0:
                        dve.wait_ge(tok_out.sem(j), tok_out.at(t - 1))
                    nc.vector.tensor_tensor(tok[:, j, n * 512:(n + 1) * 512], ra[:, 0], ra[:, 1], ALU.add).then_inc(edve.sem, 1)
            turns(dve, body)


def convolution(nc, kit, io, g, dram):
    W = CTX + SEQ + 8
    LAT = CTX + 4
    NS = NT * SH
    with ExitStack() as st:
        u = kit.sb("cu", [P, 2, W], stack=st)
        v = kit.sb("cv", [P, 2, W], stack=st)
        cw = kit.sb("cw", [P, CONV, NCH], stack=st)
        cb = kit.sb("cb", [P, NCH], stack=st)
        raw = kit.sb("dt_raw", [P, NT, 2, SH], stack=st)
        bias = kit.sb("dt_bias", [P, 2, SH], stack=st)
        alog = kit.sb("a_log", [P, 2, SH], stack=st)
        y = kit.sb("dt_y", [P, NT, 2, SH], stack=st)
        z = kit.sb("dt_z", [P, NT, 2, SH], stack=st)
        r = kit.sb("dt_r", [P, NT, 2, SH], stack=st)
        dt = kit.sb("dt_dt", [P, NT, 2, SH], stack=st)
        da = kit.sb("dt_da", [P, 2, NT, SH], stack=st)
        rel = kit.sb("rel", [P, 4, P], stack=st)
        relk = kit.sb("relk", [P, 2], stack=st)
        lg = kit.sb("lg", [P, 2, RH], stack=st)
        dec = kit.sb("ret_decay", [P, 2, RH], stack=st)
        acc = kit.ps("dt_sums", [P, 2, 512], st)
        small_in = kit.landing("conv_small_in", dmas=18)
        raw_in = kit.landing("dt_raw_in")
        u_in = kit.landing("conv_in", 2, dmas=2)
        u_out = kit.landing("conv_out", 2, dmas=2, credit=32)
        padded = kit.counter("conv_padded", 6)
        tap = kit.counter("conv_tap", CONV, credit=CONV)
        silu = kit.counter("conv_silu", 1, credit=1)
        dstep = kit.counter("dt_step", 20)
        dact = kit.counter("dt_act", 4)
        sums = kit.counter("dt_sums_ready")
        tabs = kit.counter("decay_tables", 5)
        block = st.enter_context(nc.Block())

        @block.sync
        def _(sp):
            for s in range(2):
                sp.sem_inc(u_out.sem(s), u_out.credit)
            one = small_in.sem(0)
            for k in range(CONV):
                sp.dma_start(cw[:, k], io["ssd_conv_w"][0, k, :].rearrange("(c p) -> p c", p=P), allow_slow_non_contiguous=True).then_inc(one, 16)
            sp.dma_start(cb[:], io["ssd_conv_b"].rearrange("o (c p) -> p (o c)", p=P), allow_slow_non_contiguous=True).then_inc(one, 16)
            for n, d in enumerate("fb"):
                sp.dma_start(bias[:, n], io[f"ssd_dt_bias_{d}"].to_broadcast([P, SH])).then_inc(one, 16)
                sp.dma_start(alog[:, n], io[f"ssd_a_log_{d}"].to_broadcast([P, SH])).then_inc(one, 16)
                sp.dma_start(dec[:, n], io[f"ret_decay_{d}"].to_broadcast([P, RH])).then_inc(one, 16)
            sp.dma_start(g["tri"][:], io["tri"]).then_inc(one, 16)
            sp.dma_start(rel[:], io["rel"]).then_inc(one, 16)
            sp.dma_start(relk[:], io["relk"]).then_inc(one, 16)
            sp.dma_start(g["dskip"][:], io["ssd_d"].to_broadcast([P, SH])).then_inc(one, 16)
            sp.dma_start(g["wn"][:, 0:4], io["ret_gn_w"].rearrange("o (k p) -> p (o k)", p=P), allow_slow_non_contiguous=True).then_inc(one, 16)
            sp.dma_start(g["wn"][:, 4:8], io["ssd_norm_w"].rearrange("o (k p) -> p (o k)", p=P), allow_slow_non_contiguous=True).then_inc(one, 16)
            sp.dma_start(raw[:].rearrange("p t d h -> p t (d h)"), dram["tok"][:, :, 5 * 512:NTOK].rearrange("t p f -> p t f")).then_inc(raw_in.sem(0), 16)
            sp.wait_ge(padded.sem, padded.at(0))

            def load(t, use, s):
                sp.wait_ge(tap.sem, tap.at(t - 2 + 1, 0))
                src = tile_of(dram["ch"], t)
                sp.dma_start(u[:, s, 2:2 + CTX], src[:, 0:CTX]).then_inc(u_in.sem(s), 16)
                sp.dma_start(u[:, s, LAT + 2:LAT + 2 + SEQ], src[:, CTX:CTX + SEQ]).then_inc(u_in.sem(s), 16)

            def store(t, use, s):
                sp.wait_ge(silu.sem, silu.at(t))
                dst = tile_of(dram["u"], t)
                sp.dma_start(dst[:, 0:CTX], v[:, s, 2:2 + CTX]).then_inc(u_out.sem(s), 16)
                sp.dma_start(dst[:, CTX:CTX + SEQ], v[:, s, LAT + 2:LAT + 2 + SEQ]).then_inc(u_out.sem(s), 16)

            for s in range(2):
                src = tile_of(dram["ch"], s)
                sp.dma_start(u[:, s, 2:2 + CTX], src[:, 0:CTX]).then_inc(u_in.sem(s), 16)
                sp.dma_start(u[:, s, LAT + 2:LAT + 2 + SEQ], src[:, CTX:CTX + SEQ]).then_inc(u_in.sem(s), 16)
            with sp.Fori(0, NCH // 2 - 1) as i:
                for s in range(2):
                    store(i * 2 + s, i, s)
                    load(i * 2 + (s + 2), i, s)
            for s in range(2):
                store(NCH - 2 + s, NCH // 2 - 1, s)
                sp.wait_ge(u_out.sem(s), u_out.at(NCH // 2 - 1))

        @block.gpsimd
        def _(pool):
            for s in range(2):
                for a, b in ((0, 2), (CTX + 2, LAT + 2), (W - 2, W)):
                    nc.gpsimd.memset(u[:, s, a:b], 0.0).then_inc(padded.sem, 1)

        @block.tensor
        def _(pe):
            pe.wait_ge(small_in.sem(0), small_in.at(0))
            pe.wait_ge(dstep.sem, 15)
            for d, tris in enumerate(((0, 1, 4), (2, 3, 4))):
                for n, tri in enumerate(tris):
                    m = nc.tensor.matmul(acc[:, d, n * NS:(n + 1) * NS], g["tri"][:, tri], da[:, d].rearrange("p t h -> p (t h)"), start=True, stop=True)
            m.then_inc(sums.sem, 1)

        @block.scalar
        def _(act):
            act.sem_inc(silu.sem, silu.credit)
            act.wait_ge(dstep.sem, 1)
            nc.scalar.activation(z[:], y[:], ACT.Abs).then_inc(dact.sem, 1)
            act.wait_ge(dact.sem, 1)
            nc.scalar.activation(r[:], z[:], ACT.Exp, scale=-1.0).then_inc(dact.sem, 1)
            act.wait_ge(small_in.sem(0), small_in.at(0))
            nc.scalar.activation(alog[:], alog[:], ACT.Exp).then_inc(dact.sem, 1)
            nc.scalar.activation(dec[:], dec[:], ACT.Exp).then_inc(dact.sem, 1)
            act.wait_ge(sums.sem, sums.at(0))
            for d in range(2):
                m = nc.scalar.activation(g["E"][:, :, 3 * d:3 * d + 3, :].rearrange("p t k h -> p k t h"),
                                         acc[:, d, 0:3 * NS].rearrange("p (k t h) -> p k t h", k=3, t=NT), ACT.Exp)
            m.then_inc(tabs.sem, 1)
            act.wait_ge(dstep.sem, 21)
            nc.scalar.activation(g["DT"][:], g["DT"][:], ACT.Exp)
            for h in range(RH):
                nc.scalar.activation(g["Dq"][:, 0, h], rel[:, 2], ACT.Exp, scale=lg[:, 0, h:h + 1])
                nc.scalar.activation(g["Dq"][:, 1, h], rel[:, 3], ACT.Exp, scale=lg[:, 1, h:h + 1])
            for d in range(2):
                nc.scalar.activation(g["Dk"][:, d], lg[:, d], ACT.Exp, scale=relk[:, d:d + 1])
                nc.scalar.activation(g["Dtot"][:, d], lg[:, d], ACT.Exp, scale=float(P)).then_inc(tabs.sem, 1)
            with act.Fori(0, NCH // 2) as i:
                for s in range(2):
                    t = i * 2 + s
                    act.wait_ge(tap.sem, tap.at(t))
                    act.wait_ge(u_out.sem(s), i * 32 + 32)
                    nc.scalar.activation(v[:, s, 2:W - 2], v[:, s, 2:W - 2], ACT.Silu).then_inc(silu.sem, 1)

        @block.vector
        def _(dve):
            dve.sem_inc(tap.sem, tap.credit)
            dve.wait_ge(small_in.sem(0), small_in.at(0))
            dve.wait_ge(raw_in.sem(0), raw_in.at(0))
            count = [0]

            def step(ins):
                count[0] += 1
                ins.then_inc(dstep.sem, 1)
                dve.wait_ge(dstep.sem, count[0])

            step(nc.vector.tensor_tensor(y[:], raw[:], bias[:].unsqueeze(1).to_broadcast([P, NT, 2, SH]), ALU.add))
            dve.wait_ge(dact.sem, 2)
            step(nc.vector.tensor_scalar(z[:], r[:], 2.0, None, ALU.add))
            step(nc.vector.reciprocal(z[:], z[:]))
            step(nc.vector.tensor_tensor(z[:], z[:], r[:], ALU.mult))
            step(nc.vector.tensor_tensor(raw[:], z[:], z[:], ALU.mult))
            step(nc.vector.tensor_scalar(r[:], raw[:], 1.0 / 15, None, ALU.mult))
            for k in range(6, 0, -1):
                step(nc.vector.scalar_tensor_tensor(out=r[:], in0=r[:], scalar=1.0 / (2 * k + 1), in1=raw[:], op0=ALU.add, op1=ALU.mult))
            step(nc.vector.scalar_tensor_tensor(out=r[:], in0=r[:], scalar=1.0, in1=z[:], op0=ALU.add, op1=ALU.mult))
            nc.vector.tensor_scalar(y[:], y[:], 0.0, None, ALU.max)
            dve.wait_ge(dact.sem, 4)
            step(nc.vector.tensor_scalar(alog[:], alog[:], -1.0, None, ALU.mult))
            dve.wait_ge(dstep.sem, count[0])
            nc.vector.scalar_tensor_tensor(out=dt[:], in0=r[:], scalar=2.0, in1=y[:], op0=ALU.mult, op1=ALU.add).then_inc(tabs.sem, 1)
            dve.wait_ge(tabs.sem, 1)
            step(nc.vector.tensor_tensor(da[:].rearrange("p d t h -> p t d h"), dt[:], alog[:].unsqueeze(1).to_broadcast([P, NT, 2, SH]), ALU.mult))
            dd = g["dd"]
            nc.vector.tensor_tensor(dd[:, :, 0], dt[:, :, 0], dt[:, :, 1], ALU.subtract)
            nc.vector.tensor_copy(dd[:, :, 1], dt[:, :, 1])
            nc.vector.tensor_copy(dd[:, :, 2:4], da[:].rearrange("p d t h -> p t d h"))
            step(nc.vector.tensor_scalar(lg[:], dec[:], -1.0, None, ALU.mult))
            for h in range(RH):
                step(nc.vector.tensor_scalar(g["DT"][:, h], rel[:, 1], lg[:, 1, h:h + 1], None, ALU.mult))
            for h in range(RH):
                last = nc.vector.scalar_tensor_tensor(out=g["DT"][:, h], in0=rel[:, 0], scalar=lg[:, 0, h:h + 1], in1=g["DT"][:, h], op0=ALU.mult, op1=ALU.add)
            step(last)
            dve.wait_ge(tabs.sem, 2)
            for d in range(2):
                w = g["E"][:, :, 3 * d + 1, :]
                m = nc.vector.tensor_tensor(w, w, dt[:, :, d], ALU.mult)
            m.then_inc(tabs.sem, 1)
            with dve.Fori(0, NCH // 2) as i:
                for s in range(2):
                    t = i * 2 + s
                    dve.wait_ge(u_in.sem(s), u_in.at(i))
                    dve.wait_ge(u_out.sem(s), i * 32 + 32)
                    n = W - 4
                    for k in range(CONV):
                        wk = conv_w(cw, t, k)
                        if k == 0:
                            nc.vector.tensor_scalar(v[:, s, 2:2 + n], u[:, s, 0:n], wk, conv_w(cb, t, None), ALU.mult, ALU.add).then_inc(tap.sem, 1)
                        else:
                            dve.wait_ge(tap.sem, tap.at(t, k))
                            nc.vector.scalar_tensor_tensor(out=v[:, s, 2:2 + n], in0=u[:, s, k:k + n], scalar=wk, in1=v[:, s, 2:2 + n], op0=ALU.mult, op1=ALU.add).then_inc(tap.sem, 1)


def conv_w(w, t, k):
    if k is None:
        return w[:, bass.ds(t, 1)]
    return w[:, k, bass.ds(t, 1)]


def heads(v, n):
    return v.unsqueeze(2).to_broadcast([P, v.shape[1], n])


def tile_row(t4, t, k):
    return t4[:, bass.ds(t, 1), k, :].rearrange("p o h -> p (o h)")


def states(nc, kit, io, g, dram):
    TURNS = NT + NCT
    with ExitStack() as st:
        kv = kit.sb("s_kv", [P, 2, D], stack=st)
        uc = kit.sb("s_u", [P, 2, 6, P], stack=st)
        kd = kit.sb("s_kd", [P, 2, 512], stack=st)
        xw = kit.sb("s_xw", [P, 2, 512], stack=st)
        bt = kit.sb("s_bt", [P, 2, SG * P], stack=st)
        sb = kit.sb("s_sb", [P, 2, 2, 512], stack=st)
        sd = kit.sb("s_sd", [P, 2, 512], stack=st)
        xT = kit.ps("s_xT", [P, 2, 512], st)
        bT = kit.ps("s_bT", [P, 2, 512], st)
        up = kit.ps("s_up", [P, 2, 2, 512], st)
        kv_in = kit.landing("s_kv_in", 2)
        u_in = kit.landing("s_u_in", 2)
        s_out = kit.landing("s_out", 2)
        turned = kit.counter("s_transposed", 2, credit=4)
        bts = kit.counter("s_b_ready", 1, credit=2)
        kds = kit.counter("s_k_decayed", 1, credit=2)
        xws = kit.counter("s_x_weighted", 1, credit=2)
        dec = kit.counter("s_decayed", 2, credit=4)
        ups = kit.counter("s_update_ready", 1, credit=2)
        news = kit.counter("s_state_ready", 2, credit=4)
        zero = kit.counter("s_zero")
        block = st.enter_context(nc.Block())

        def turns(eng, body):
            for t in range(NCT):
                body(t, t // 2, t % 2, NCT - 1 - t, True, sb, False)
            with eng.Fori(0, NL // 2) as i:
                for s in range(2):
                    t = i * 2 + (NCT + s)
                    body(t, i + 1, s, i * -2 + (NT - 1 - s), True, sb, True)
            for t in range(NT, TURNS):
                body(t, t // 2, t % 2, t - NT, False, g["sf"], False)

        @block.sync
        def _(sp):
            def load(t, use, s, tile, back, state, stored):
                sp.wait_ge(ups.sem, ups.at(t - 2))
                sp.wait_ge(kds.sem, kds.at(t - 2))
                sp.dma_start(kv[:, s], tile_of(dram["tok"], tile, 512, 3 * 512)).then_inc(kv_in.sem(s), 16)
                sp.wait_ge(turned.sem, turned.at(t - 2))
                sp.dma_start(uc[:, s], dram["u"][0:6, :, bass.ds(tile * P, P)].rearrange("c p t -> p c t")).then_inc(u_in.sem(s), 16)
            turns(sp, load)

        @block.gpsimd
        def _(pool):
            pool.sem_inc(kds.sem, kds.credit)
            pool.sem_inc(dec.sem, dec.credit)
            nc.gpsimd.memset(sb[:, 0], 0.0)
            nc.gpsimd.memset(g["sf"][:, 0], 0.0).then_inc(zero.sem, 1)
            pool.wait_ge(zero.sem, zero.at(0))

            def body(t, use, s, tile, back, state, stored):
                pool.wait_ge(kv_in.sem(s), kv_in.at(use))
                pool.wait_ge(ups.sem, ups.at(t - 2))
                nc.gpsimd.tensor_tensor(kd[:, s].rearrange("p (h e) -> p h e", h=RH), kv[:, s, 0:512].rearrange("p (h e) -> p h e", h=RH),
                                                heads(g["Dk"][:, int(back)], P), ALU.mult).then_inc(kds.sem, 1)
                pool.wait_ge(news.sem, news.at(t - 1))
                nc.gpsimd.tensor_tensor(sd[:, 0].rearrange("p (h e) -> p h e", h=RH), state[:, s, 0].rearrange("p (h e) -> p h e", h=RH),
                                                heads(g["Dtot"][:, int(back)], P), ALU.mult).then_inc(dec.sem, 1)
                nc.gpsimd.tensor_tensor(sd[:, 1].rearrange("p (h e) -> p h e", h=SH), state[:, s, 1].rearrange("p (h e) -> p h e", h=SH),
                                                heads(tile_row(g["E"], tile, 5 if back else 2), SP_), ALU.mult).then_inc(dec.sem, 1)
            turns(pool, body)

        @block.tensor
        def _(pe):
            pe.sem_inc(turned.sem, turned.credit)
            pe.sem_inc(ups.sem, ups.credit)

            def body(t, use, s, tile, back, state, stored):
                pe.wait_ge(u_in.sem(s), u_in.at(use))
                pe.wait_ge(xws.sem, xws.at(t - 2))
                for c in range(4):
                    m = nc.tensor.transpose(xT[:, s, c * P:(c + 1) * P], uc[:, s, c], g["ident"][:, :])
                m.then_inc(turned.sem, 1)
                pe.wait_ge(bts.sem, bts.at(t - 2))
                for c in range(SG):
                    m = nc.tensor.transpose(bT[:, s, c * P:(c + 1) * P], uc[:, s, 4 + c], g["ident"][:, :])
                m.then_inc(turned.sem, 1)
                pe.wait_ge(kds.sem, kds.at(t))
                pe.wait_ge(news.sem, news.at(t - 2))
                for h in range(RH):
                    nc.tensor.matmul(up[:, s, 0, h * P:(h + 1) * P], kd[:, s, h * P:(h + 1) * P], kv[:, s, 512 + h * P:512 + (h + 1) * P], start=True, stop=True)
                pe.wait_ge(xws.sem, xws.at(t))
                pe.wait_ge(bts.sem, bts.at(t))
                for c in range(SG):
                    m = nc.tensor.matmul(up[:, s, 1, c * 256:(c + 1) * 256], bt[:, s, c * P:(c + 1) * P], xw[:, s, c * 256:(c + 1) * 256], start=True, stop=True)
                m.then_inc(ups.sem, 1)
            turns(pe, body)

        @block.scalar
        def _(act):
            act.sem_inc(bts.sem, bts.credit)

            def body(t, use, s, tile, back, state, stored):
                if stored:
                    act.wait_ge(news.sem, news.at(t - 1))
                    act.dma_start(tile_of(dram["sb"], tile), state[:, s].rearrange("p a b -> p (a b)")).then_inc(s_out.sem(s), 16)
                act.wait_ge(turned.sem, turned.at(t, 2))
                act.wait_ge(ups.sem, ups.at(t - 2))
                nc.scalar.activation(bt[:, s], bT[:, s, 0:SG * P], ACT.Copy).then_inc(bts.sem, 1)
            turns(act, body)
            for s in range(2):
                act.wait_ge(s_out.sem(s), 16 * NL // 2)

        @block.vector
        def _(dve):
            dve.sem_inc(xws.sem, xws.credit)
            dve.sem_inc(news.sem, news.credit)

            def body(t, use, s, tile, back, state, stored):
                dve.wait_ge(turned.sem, turned.at(t, 1))
                dve.wait_ge(ups.sem, ups.at(t - 2))
                nc.vector.tensor_tensor(xw[:, s].rearrange("p (h e) -> p h e", h=SH), xT[:, s].rearrange("p (h e) -> p h e", h=SH),
                                                heads(tile_row(g["E"], tile, 4 if back else 1), SP_), ALU.mult).then_inc(xws.sem, 1)
                dve.wait_ge(dec.sem, dec.at(t))
                dve.wait_ge(ups.sem, ups.at(t))
                if stored:
                    dve.wait_ge(s_out.sem(1 - s), s_out.at(use - 1 if s else use - 2))
                for n in range(2):
                    nc.vector.tensor_tensor(state[:, 1 - s, n], sd[:, n], up[:, s, n], ALU.add).then_inc(news.sem, 1)
            turns(dve, body)


def mixing(nc, kit, io, g, dram):
    with ExitStack() as st:
        tok = kit.sb("m_tok", [P, 2, 5 * 512], stack=st)
        uc = kit.sb("m_u", [P, 2, NCH, P], stack=st)
        sb = kit.sb("m_sb", [P, 2, 2, 512], stack=st)
        qk = kit.sb("m_qk", [P, 2, 512], stack=st)
        qd = kit.sb("m_qd", [P, 2, 512], stack=st)
        xs = kit.sb("m_xs", [P, 512], stack=st)
        bt = kit.sb("m_bt", [P, SG * P], stack=st)
        kd = kit.sb("m_kd", [P, 512], stack=st)
        xw = kit.sb("m_xw", [P, 512], stack=st)
        dav = kit.sb("m_dav", [P, 2, SH * P], stack=st)
        sT = kit.sb("m_sT", [P, 512], stack=st)
        L = kit.sb("m_L", [P, SH, P], stack=st)
        G = kit.sb("m_G", [P, SH, P], stack=st)
        sd = kit.sb("m_sd", [P, 2, 512], stack=st)
        xd = kit.sb("m_xd", [P, 512], stack=st)
        t1 = kit.sb("m_t1", [P, 512], stack=st)
        t2 = kit.sb("m_t2", [P, 512], stack=st)
        t3 = kit.sb("m_t3", [P, 512], stack=st)
        yr = kit.sb("m_yr", [P, 512], stack=st)
        bn = kit.sb("m_bn", [P, RH, 6], stack=st)
        mv = kit.sb("m_mv", [P, RH, 2], stack=st)
        rs = kit.sb("m_rs", [P, 8], stack=st)
        sq = kit.sb("m_sq", [P, 512], stack=st)
        yc = kit.sb("m_y", [P, 2, D], stack=st)
        bank = kit.ps("m_bank", [P, 8, 512], st)
        tok_in = kit.landing("m_tok_in", 2)
        u_in = kit.landing("m_u_in", 2)
        sb_in = kit.landing("m_sb_in", 2)
        y_out = kit.landing("m_y_out", 2, credit=16)
        turned = kit.counter("m_transposed", 4, credit=4)
        left = kit.counter("m_transposed_copied", 4, credit=4)
        qdec = kit.counter("m_q_decayed", 2, credit=2)
        davs = kit.counter("m_da_spread", 2, credit=2)
        kds = kit.counter("m_k_decayed", 1, credit=1)
        xws = kit.counter("m_x_weighted", 1, credit=1)
        prod = kit.counter("m_products", 3, credit=3)
        exps = kit.counter("m_decays_exp", 1, credit=1)
        sTs = kit.counter("m_scores_decayed", 1, credit=1)
        gate = kit.counter("m_steps_spread", 3, credit=3)
        yret = kit.counter("m_y_ret", 1, credit=1)
        yssd = kit.counter("m_y_ssd", 2, credit=2)
        ups = kit.counter("m_update_ready", 1, credit=1)
        dec = kit.counter("m_state_decayed", 2, credit=2)
        news = kit.counter("m_state_ready", 2, credit=2)
        skip = kit.counter("m_skip_ready", 1, credit=1)
        stats = kit.counter("m_head_stats", 2)
        rstd = kit.counter("m_rstd", 2)
        eps_added = kit.counter("m_eps_added", 2)
        yrs = kit.counter("m_ret_normed", 2, credit=2)
        ysum = kit.counter("m_ssd_summed", 5, credit=5)
        ssq = kit.counter("m_ssd_ssq", 1, credit=1)
        gated = kit.counter("m_ssd_gated", 2, credit=2)
        yssdn = kit.counter("m_ssd_normed", 1, credit=1)
        block = st.enter_context(nc.Block())

        def turns(eng, body):
            for t, use, s in pairs(eng, 0, NL):
                body(t, use, s, use * 2 + (s + NCT))

        def by(v, n):
            return v.rearrange("p (h e) -> p h e", h=n)

        @block.sync
        def _(sp):
            for s in range(2):
                sp.sem_inc(y_out.sem(s), y_out.credit)

            def load(t, use, s, tile):
                sp.wait_ge(ups.sem, ups.at(t - 2 + 1, 0))
                sp.wait_ge(yssd.sem, yssd.at(t - 2 + 1, 0))
                sp.wait_ge(gated.sem, gated.at(t - 2 + 1, 0))
                sp.wait_ge(yrs.sem, yrs.at(t - 2 + 1, 0))
                issue(t, use, s, tile)

            def issue(t, use, s, tile):
                sp.dma_start(uc[:, s], dram["u"][:, :, bass.ds(tile * P, P)].rearrange("c p t -> p c t")).then_inc(u_in.sem(s), 16)
                sp.dma_start(tok[:, s], tile_of(dram["tok"], tile, 0, 5 * 512)).then_inc(tok_in.sem(s), 16)
                sp.dma_start(sb[:, s].rearrange("p a b -> p (a b)"), tile_of(dram["sb"], tile)).then_inc(sb_in.sem(s), 16)

            for s in range(2):
                issue(s, 0, s, NCT + s)
            with sp.Fori(0, NL // 2 - 1) as i:
                for s in range(2):
                    t = i * 2 + (2 + s)
                    load(t, i + 1, s, t + NCT)

        @block.gpsimd
        def _(pool):
            for x in (davs, kds, dec, skip, gated):
                pool.sem_inc(x.sem, x.credit)

            def body(t, use, s, tile):
                pool.wait_ge(prod.sem, prod.at(t - 1))
                for d in range(2):
                    nc.gpsimd.tensor_tensor(by(dav[:, d], SH), g["tri"][:, 2 * d].unsqueeze(1).to_broadcast([P, SH, P]),
                                                     heads(tile_row(g["dd"], tile, 2 + d), P), ALU.mult).then_inc(davs.sem, 1)
                pool.wait_ge(tok_in.sem(s), tok_in.at(use))
                pool.wait_ge(ups.sem, ups.at(t - 1))
                nc.gpsimd.tensor_tensor(by(kd[:], RH), by(tok[:, s, 512:1024], RH), heads(g["Dk"][:, 0], P), ALU.mult).then_inc(kds.sem, 1)
                pool.wait_ge(news.sem, news.at(t - 1))
                nc.gpsimd.tensor_tensor(by(sd[:, 0], RH), by(g["sf"][:, s, 0], RH), heads(g["Dtot"][:, 0], P), ALU.mult).then_inc(dec.sem, 1)
                nc.gpsimd.tensor_tensor(by(sd[:, 1], SH), by(g["sf"][:, s, 1], SH), heads(tile_row(g["E"], tile, 2), SP_), ALU.mult).then_inc(dec.sem, 1)
                pool.wait_ge(left.sem, left.at(t, 3))
                pool.wait_ge(ysum.sem, ysum.at(t - 1))
                nc.gpsimd.tensor_tensor(by(xd[:], SH), by(xs[:], SH), heads(g["dskip"][:], SP_), ALU.mult).then_inc(skip.sem, 1)
                pool.wait_ge(stats.sem, stats.at(t))
                rstd_root(nc, g, pool, eps_added, t, 1, rs[:, 0:4], mv[:, :, 1], 1).then_inc(rstd.sem, 1)
                pool.wait_ge(ysum.sem, ysum.at(t, 5))
                pool.wait_ge(yssdn.sem, yssdn.at(t - 1))
                nc.gpsimd.tensor_tensor(t1[:], t3[:], tok[:, s, 4 * 512:5 * 512], ALU.mult).then_inc(gated.sem, 1)
                pool.wait_ge(yrs.sem, yrs.at(t, 2))
                pool.wait_ge(y_out.sem(s), y_out.at(use - 1))
                nc.gpsimd.tensor_tensor(yc[:, s, 0:512], yr[:], tok[:, s, 3 * 512:4 * 512], ALU.mult).then_inc(gated.sem, 1)
                pool.wait_ge(ssq.sem, ssq.at(t))
                rstd_root(nc, g, pool, eps_added, t, 2, rs[:, 5:6], rs[:, 4:5], 512).then_inc(rstd.sem, 1)
            turns(pool, body)

        @block.tensor
        def _(pe):
            for x in (turned, prod, yret, yssd, ups):
                pe.sem_inc(x.sem, x.credit)

            def body(t, use, s, tile):
                ident = g["ident"][:, :]
                pe.wait_ge(tok_in.sem(s), tok_in.at(use))
                pe.wait_ge(yrs.sem, yrs.at(t - 1))
                for n in range(2):
                    if n:
                        pe.wait_ge(ysum.sem, ysum.at(t - 1))
                    for h in range(RH):
                        m = nc.tensor.transpose(bank[:, n, h * P:(h + 1) * P], tok[:, s, n * 512 + h * P:n * 512 + (h + 1) * P], ident)
                    m.then_inc(turned.sem, 1)
                pe.wait_ge(u_in.sem(s), u_in.at(use))
                for c in range(4):
                    m = nc.tensor.transpose(bank[:, 2, c * P:(c + 1) * P], uc[:, s, c], ident)
                m.then_inc(turned.sem, 1)
                pe.wait_ge(news.sem, news.at(t - 1))
                for c in range(SG):
                    m = nc.tensor.transpose(bank[:, 3, c * P:(c + 1) * P], uc[:, s, 4 + c], ident)
                m.then_inc(turned.sem, 1)
                pe.wait_ge(davs.sem, davs.at(t))
                pe.wait_ge(exps.sem, exps.at(t - 1))
                for half in range(2):
                    for d in range(2):
                        m = nc.tensor.matmul(bank[:, 5 + half], g["tri"][:, 1 + 2 * d], dav[:, d, half * 512:(half + 1) * 512], start=(d == 0), stop=(d == 1))
                m.then_inc(prod.sem, 1)
                pe.wait_ge(left.sem, left.at(t, 2))
                for h in range(RH):
                    m = nc.tensor.matmul(bank[:, 4, h * P:(h + 1) * P], qk[:, 1, h * P:(h + 1) * P], qk[:, 0, h * P:(h + 1) * P], start=True, stop=True)
                m.then_inc(prod.sem, 1)
                for c in range(SG):
                    m = nc.tensor.matmul(bank[:, 7, c * P:(c + 1) * P], uc[:, s, 4 + c], uc[:, s, 6 + c], start=True, stop=True)
                m.then_inc(prod.sem, 1)
                pe.wait_ge(sTs.sem, sTs.at(t))
                pe.wait_ge(qdec.sem, qdec.at(t))
                pe.wait_ge(sb_in.sem(s), sb_in.at(use))
                for h in range(RH):
                    e = slice(h * P, (h + 1) * P)
                    nc.tensor.matmul(bank[:, 0, e], sT[:, e], tok[:, s, 1024 + h * P:1024 + (h + 1) * P], start=True, stop=False)
                    nc.tensor.matmul(bank[:, 0, e], qd[:, 0, e], g["sf"][:, s, 0, e], start=False, stop=False)
                    m = nc.tensor.matmul(bank[:, 0, e], qd[:, 1, e], sb[:, s, 0, e], start=False, stop=True)
                m.then_inc(yret.sem, 1)
                pe.wait_ge(kds.sem, kds.at(t))
                for h in range(RH):
                    e = slice(h * P, (h + 1) * P)
                    nc.tensor.matmul(bank[:, 4, e], kd[:, e], tok[:, s, 1024 + h * P:1024 + (h + 1) * P], start=True, stop=True)
                pe.wait_ge(left.sem, left.at(t, 4))
                pe.wait_ge(xws.sem, xws.at(t))
                for c in range(SG):
                    m = nc.tensor.matmul(bank[:, 3, c * 256:(c + 1) * 256], bt[:, c * P:(c + 1) * P], xw[:, c * 256:(c + 1) * 256], start=True, stop=True)
                m.then_inc(ups.sem, 1)
                pe.wait_ge(gate.sem, gate.at(t))
                for n, state in ((2, g["sf"][:, s, 1]), (7, sb[:, s, 1])):
                    for c in range(SG):
                        m = nc.tensor.matmul(bank[:, n, c * 256:(c + 1) * 256], uc[:, s, 6 + c], state[:, c * 256:(c + 1) * 256], start=True, stop=True)
                m.then_inc(yssd.sem, 1)
                for h in range(SH):
                    m = nc.tensor.matmul(bank[:, 1, h * SP_:(h + 1) * SP_], L[:, h], xs[:, h * SP_:(h + 1) * SP_], start=True, stop=True)
                m.then_inc(yssd.sem, 1)
            turns(pe, body)

        @block.scalar
        def _(act):
            for x in (left, exps, ssq):
                act.sem_inc(x.sem, x.credit)

            def body(t, use, s, tile):
                act.wait_ge(turned.sem, turned.at(t, 1))
                act.wait_ge(prod.sem, prod.at(t - 1))
                act.wait_ge(qdec.sem, qdec.at(t - 1))
                nc.scalar.activation(qk[:, 0], bank[:, 0], ACT.Copy).then_inc(left.sem, 1)
                act.wait_ge(turned.sem, turned.at(t, 2))
                nc.scalar.activation(qk[:, 1], bank[:, 1], ACT.Copy).then_inc(left.sem, 1)
                act.wait_ge(turned.sem, turned.at(t, 3))
                act.wait_ge(yssd.sem, yssd.at(t - 1))
                act.wait_ge(skip.sem, skip.at(t - 1))
                nc.scalar.activation(xs[:], bank[:, 2], ACT.Copy).then_inc(left.sem, 1)
                act.wait_ge(turned.sem, turned.at(t, 4))
                act.wait_ge(ups.sem, ups.at(t - 1))
                nc.scalar.activation(bt[:], bank[:, 3, 0:SG * P], ACT.Copy).then_inc(left.sem, 1)
                act.wait_ge(prod.sem, prod.at(t, 1))
                nc.scalar.activation(L[:].rearrange("p h n -> p (h n)"), bank[:, 5:7].rearrange("p a b -> p (a b)"), ACT.Exp).then_inc(exps.sem, 1)
                act.wait_ge(gated.sem, gated.at(t, 1))
                nc.scalar.activation(sq[:], t1[:], ACT.Square, accum_out=rs[:, 4:5]).then_inc(ssq.sem, 1)
                act.wait_ge(gated.sem, gated.at(t, 2))
                act.wait_ge(yssdn.sem, yssdn.at(t))
                act.dma_start(tile_of(dram["y"], tile), yc[:, s]).then_inc(y_out.sem(s), 16)
            turns(act, body)
            for s in range(2):
                act.wait_ge(y_out.sem(s), y_out.at(NL // 2 - 1))

        @block.vector
        def _(dve):
            for x in (qdec, xws, sTs, gate, news, yrs, ysum, yssdn):
                dve.sem_inc(x.sem, x.credit)

            def body(t, use, s, tile):
                dve.wait_ge(left.sem, left.at(t, 1))
                dve.wait_ge(yret.sem, yret.at(t - 1))
                for d in range(2):
                    nc.vector.tensor_tensor(qd[:, d], qk[:, 0], g["Dq"][:, d].rearrange("p h n -> p (h n)"), ALU.mult).then_inc(qdec.sem, 1)
                dve.wait_ge(left.sem, left.at(t, 3))
                dve.wait_ge(ups.sem, ups.at(t - 1))
                nc.vector.tensor_tensor(by(xw[:], SH), by(xs[:], SH), heads(tile_row(g["E"], tile, 1), SP_), ALU.mult).then_inc(xws.sem, 1)
                for h in range(SH):
                    m = nc.vector.tensor_scalar(G[:, h], g["tri"][:, 0], g["dd"][:, bass.ds(tile, 1), 0, h:h + 1].rearrange("p a b -> p (a b)"),
                                                g["dd"][:, bass.ds(tile, 1), 1, h:h + 1].rearrange("p a b -> p (a b)"), ALU.mult, ALU.add)
                m.then_inc(gate.sem, 1)
                dve.wait_ge(prod.sem, prod.at(t, 2))
                nc.vector.tensor_tensor(sT[:], bank[:, 4], g["DT"][:].rearrange("p h n -> p (h n)"), ALU.mult).then_inc(sTs.sem, 1)
                dve.wait_ge(gate.sem, gate.at(t, 1))
                dve.wait_ge(exps.sem, exps.at(t))
                nc.vector.tensor_tensor(L[:], L[:], G[:], ALU.mult).then_inc(gate.sem, 1)
                dve.wait_ge(gate.sem, gate.at(t, 2))
                dve.wait_ge(prod.sem, prod.at(t, 3))
                nc.vector.tensor_tensor(L[:].rearrange("p (c r) n -> p c r n", c=SG), L[:].rearrange("p (c r) n -> p c r n", c=SG),
                                                 bank[:, 7, 0:SG * P].rearrange("p (c n) -> p c n", c=SG).unsqueeze(2).to_broadcast([P, SG, SH // SG, P]), ALU.mult).then_inc(gate.sem, 1)
                dve.wait_ge(yret.sem, yret.at(t))
                for h in range(RH):
                    m = nc.vector.bn_stats(bn[:, h], bank[:, 0, h * P:(h + 1) * P])
                m.then_inc(stats.sem, 1)
                dve.wait_ge(stats.sem, stats.at(t, 1))
                dve.wait_ge(ups.sem, ups.at(t))
                dve.wait_ge(dec.sem, dec.at(t))
                for n, b in ((0, 4), (1, 3)):
                    nc.vector.tensor_tensor(g["sf"][:, 1 - s, n], sd[:, n], bank[:, b], ALU.add).then_inc(news.sem, 1)
                for h in range(RH):
                    m = nc.vector.bn_aggr(mv[:, h], bn[:, h])
                m.then_inc(stats.sem, 1)
                dve.wait_ge(rstd.sem, rstd.at(t, 1))
                dve.wait_ge(gated.sem, gated.at(t - 1))
                for h in range(RH):
                    m = nc.vector.tensor_scalar(yr[:, h * P:(h + 1) * P], bank[:, 0, h * P:(h + 1) * P], mv[:, h, 0:1], rs[:, h:h + 1], ALU.subtract, ALU.mult)
                    if h % 2:
                        m.then_inc(yrs.sem, 1)
                dve.wait_ge(yssd.sem, yssd.at(t, 2))
                dve.wait_ge(gated.sem, gated.at(t - 1))
                nc.vector.tensor_tensor(by(t3[:], SH), by(bank[:, 2], SH), heads(tile_row(g["E"], tile, 0), SP_), ALU.mult).then_inc(ysum.sem, 1)
                nc.vector.tensor_tensor(by(t2[:], SH), by(bank[:, 7], SH), heads(tile_row(g["E"], tile, 3), SP_), ALU.mult).then_inc(ysum.sem, 1)
                dve.wait_ge(ysum.sem, ysum.at(t, 1))
                nc.vector.tensor_tensor(t3[:], t3[:], bank[:, 1], ALU.add).then_inc(ysum.sem, 1)
                dve.wait_ge(ysum.sem, ysum.at(t, 3))
                dve.wait_ge(skip.sem, skip.at(t))
                nc.vector.tensor_tensor(t2[:], t2[:], xd[:], ALU.add).then_inc(ysum.sem, 1)
                dve.wait_ge(ysum.sem, ysum.at(t, 4))
                nc.vector.tensor_tensor(t3[:], t3[:], t2[:], ALU.add).then_inc(ysum.sem, 1)
                dve.wait_ge(rstd.sem, rstd.at(t, 2))
                dve.wait_ge(y_out.sem(s), y_out.at(use - 1))
                nc.vector.tensor_scalar(yc[:, s, 512:D], t1[:], rs[:, 5:6], 512.0 ** 0.5, ALU.mult, ALU.mult).then_inc(yssdn.sem, 1)
            turns(dve, body)


def residual(nc, kit, io, g, dram):
    with ExitStack() as st:
        w = kit.sb("r_w", [P, KD, D], stack=st)
        wr = kit.sb("r_wr", [P, KD, NG + NE], stack=st)
        br = kit.sb("r_br", [P, NG + NE], stack=st)
        y = kit.sb("r_y", [P, 2, D], stack=st)
        x = kit.sb("r_x", [P, 2, D], stack=st)
        yT = kit.sb("r_yT", [P, KD, P], stack=st)
        hT = kit.sb("r_hT", [P, KD, P], stack=st)
        sq = kit.sb("r_sq", [P, D], stack=st)
        ss = kit.sb("r_ss", [P, 4], stack=st)
        yn = kit.sb("r_yn", [P, D], stack=st)
        x1 = kit.sb("r_x1", [P, 2, D], stack=st)
        h2 = kit.sb("r_h2", [P, 2, D], stack=st)
        pT = kit.ps("r_pT", [P, KD, P], st)
        py = kit.ps("r_py", [P, 2, 512], st)
        pH = kit.ps("r_pH", [P, KD, P], st)
        pl = kit.ps("r_pl", [P, 512], st)
        w_l = kit.landing("r_w_in", dmas=KD + NG + 3)
        y_in = kit.landing("r_y_in", 2)
        x_in = kit.landing("r_x_in", 2)
        x1_out = kit.landing("r_x1_out", 2, credit=16)
        h2_out = kit.landing("r_h2_out", 2, credit=16)
        wsc = kit.counter("r_w_scaled")
        yTt = kit.counter("r_y_transposed", 1, credit=2)
        yTs = kit.counter("r_yT_ready", 1, credit=2)
        prod = kit.counter("r_product", 1, credit=2)
        ssq = kit.counter("r_ssq", 2, credit=2)
        eps_added = kit.counter("r_eps_added", 2)
        rstd = kit.counter("r_rstd", 2)
        yns = kit.counter("r_y_normed", 1, credit=1)
        x1s = kit.counter("r_x1_ready", 1, credit=2)
        h2s = kit.counter("r_h2_ready", 2, credit=4)
        hTt = kit.counter("r_h_transposed", 1, credit=2)
        hTs = kit.counter("r_hT_ready", 1, credit=2)
        lgp = kit.counter("r_logits_product", 1, credit=2)
        lgs = kit.counter("r_logits_ready", 1, credit=2)
        block = st.enter_context(nc.Block())

        @block.sync
        def _(sp):
            for s in range(2):
                sp.sem_inc(x1_out.sem(s), 16)
                sp.sem_inc(h2_out.sem(s), 16)
            one = w_l.sem(0)
            for k in range(KD):
                sp.dma_start(w[:, k], io["w_out"][0, k * P:(k + 1) * P, :]).then_inc(one, 16)
            sp.dma_start(wr[:, :, 0:NG], io["moe_w_rg"].rearrange("o (k p) n -> p (o k) n", p=P)).then_inc(one, 16)
            for n in range(NG):
                sp.dma_start(wr[:, :, NG + n * EPG:NG + (n + 1) * EPG], io["moe_w_re"][0, n].rearrange("(k p) e -> p k e", p=P)).then_inc(one, 16)
            sp.dma_start(br[:, 0:NG], io["moe_b_rg"].to_broadcast([P, NG])).then_inc(one, 16)
            sp.dma_start(br[:, NG:NG + NE], io["moe_b_re"].rearrange("o g e -> o (g e)").to_broadcast([P, NE])).then_inc(one, 16)
            for t, use, s in pairs(sp, 0, NL):
                sp.wait_ge(yTt.sem, yTt.at(t - 2))
                sp.dma_start(y[:, s], tile_of(dram["y"], t + NCT)).then_inc(y_in.sem(s), 16)
                sp.wait_ge(x1s.sem, x1s.at(t - 2))
                sp.dma_start(x[:, s], tile_of(io["x"].rearrange("o (t p) d -> (o t) p d", p=P), t)).then_inc(x_in.sem(s), 16)

        @block.gpsimd
        def _(pool):
            for t, use, s in pairs(pool, 0, NL):
                for n in range(2):
                    pool.wait_ge(ssq.sem, ssq.at(t, n + 1))
                    rstd_root(nc, g, pool, eps_added, t, n + 1, ss[:, 2 + n:3 + n], ss[:, n:n + 1], D).then_inc(rstd.sem, 1)

        @block.tensor
        def _(pe):
            for x_ in (yTt, prod, hTt, lgp):
                pe.sem_inc(x_.sem, x_.credit)
            ident = g["ident"][:, :]
            pe.wait_ge(wsc.sem, wsc.at(0))

            def project(t, use, s):
                pe.wait_ge(y_in.sem(s), y_in.at(use))
                pe.wait_ge(yTs.sem, yTs.at(t - 1))
                for k in range(KD):
                    m = nc.tensor.transpose(pT[:, k], y[:, s, k * P:(k + 1) * P], ident)
                m.then_inc(yTt.sem, 1)
                pe.wait_ge(yTs.sem, yTs.at(t))
                pe.wait_ge(yns.sem, yns.at(t - 1))
                for n in range(2):
                    for k in range(KD):
                        m = nc.tensor.matmul(py[:, n], yT[:, k], w[:, k, n * 512:(n + 1) * 512], start=(k == 0), stop=(k == KD - 1))
                m.then_inc(prod.sem, 1)

            def route(t, s):
                pe.wait_ge(h2s.sem, h2s.at(t))
                pe.wait_ge(hTs.sem, hTs.at(t - 1))
                for k in range(KD):
                    m = nc.tensor.transpose(pH[:, k], h2[:, s, k * P:(k + 1) * P], ident)
                m.then_inc(hTt.sem, 1)
                pe.wait_ge(hTs.sem, hTs.at(t))
                pe.wait_ge(lgs.sem, lgs.at(t - 1))
                for k in range(KD):
                    m = nc.tensor.matmul(pl[:, 0:NG + NE], hT[:, k], wr[:, k], start=(k == 0), stop=(k == KD - 1))
                m.then_inc(lgp.sem, 1)

            project(0, 0, 0)
            with pe.Fori(0, NL // 2 - 1) as i:
                project(i * 2 + 1, i, 1)
                route(i * 2, 0)
                project(i * 2 + 2, i + 1, 0)
                route(i * 2 + 1, 1)
            project(NL - 1, NL // 2 - 1, 1)
            route(NL - 2, 0)
            route(NL - 1, 1)

        @block.scalar
        def _(act):
            for x_ in (yTs, ssq, hTs):
                act.sem_inc(x_.sem, x_.credit)

            def first(t, use, s):
                act.wait_ge(yTt.sem, yTt.at(t))
                act.wait_ge(prod.sem, prod.at(t - 1))
                nc.scalar.activation(yT[:], pT[:], ACT.Copy).then_inc(yTs.sem, 1)
                act.wait_ge(prod.sem, prod.at(t))
                act.wait_ge(rstd.sem, rstd.at(t - 1, 2)) if not isinstance(t, int) or t else None
                nc.scalar.activation(sq[:], py[:].rearrange("p a b -> p (a b)"), ACT.Square, accum_out=ss[:, 0:1]).then_inc(ssq.sem, 1)
                act.wait_ge(x1s.sem, x1s.at(t))
                nc.scalar.activation(sq[:], x1[:, s], ACT.Square, accum_out=ss[:, 1:2]).then_inc(ssq.sem, 1)
                act.dma_start(tile_of(dram["x1"], t), x1[:, s]).then_inc(x1_out.sem(s), 16)

            def second(t, use, s):
                act.wait_ge(h2s.sem, h2s.at(t))
                act.dma_start(tile_of(dram["h2"], t), h2[:, s]).then_inc(h2_out.sem(s), 16)
                act.wait_ge(hTt.sem, hTt.at(t))
                act.wait_ge(lgp.sem, lgp.at(t - 1))
                nc.scalar.activation(hT[:], pH[:], ACT.Copy).then_inc(hTs.sem, 1)

            first(0, 0, 0)
            with act.Fori(0, NL // 2 - 1) as i:
                first(i * 2 + 1, i, 1)
                second(i * 2, i, 0)
                first(i * 2 + 2, i + 1, 0)
                second(i * 2 + 1, i, 1)
            first(NL - 1, NL // 2 - 1, 1)
            second(NL - 2, NL // 2 - 1, 0)
            second(NL - 1, NL // 2 - 1, 1)
            for s in range(2):
                act.wait_ge(x1_out.sem(s), x1_out.at(NL // 2 - 1))
                act.wait_ge(h2_out.sem(s), h2_out.at(NL // 2 - 1))

        @block.vector
        def _(dve):
            for x_ in (yns, x1s, h2s, lgs):
                dve.sem_inc(x_.sem, x_.credit)
            dve.wait_ge(w_l.sem(0), w_l.at(0))
            for k in range(KD):
                m = nc.vector.tensor_scalar(w[:, k], w[:, k], g["wn"][:, k:k + 1], None, ALU.mult)
            m.then_inc(wsc.sem, 1)

            def first(t, use, s):
                dve.wait_ge(rstd.sem, rstd.at(t, 1))
                dve.wait_ge(x1s.sem, x1s.at(t - 1))
                nc.vector.scalar_tensor_tensor(out=yn[:], in0=py[:].rearrange("p a b -> p (a b)"), scalar=ss[:, 2:3], in1=g["mod"][:, 2 * D:3 * D], op0=ALU.mult, op1=ALU.mult).then_inc(yns.sem, 1)
                dve.wait_ge(yns.sem, yns.at(t))
                dve.wait_ge(x_in.sem(s), x_in.at(use))
                dve.wait_ge(x1_out.sem(s), x1_out.at(use - 1))
                nc.vector.tensor_tensor(x1[:, s], yn[:], x[:, s], ALU.add).then_inc(x1s.sem, 1)
                dve.wait_ge(rstd.sem, rstd.at(t, 2))
                dve.wait_ge(h2_out.sem(s), h2_out.at(use - 1))
                dve.wait_ge(hTt.sem, hTt.at(t - 2))
                nc.vector.scalar_tensor_tensor(out=h2[:, s], in0=x1[:, s], scalar=ss[:, 3:4], in1=g["mod"][:, 4 * D:5 * D], op0=ALU.mult, op1=ALU.mult).then_inc(h2s.sem, 1)
                dve.wait_ge(h2s.sem, h2s.at(t, 1))
                nc.vector.tensor_tensor(h2[:, s], h2[:, s], g["mod"][:, 3 * D:4 * D], ALU.add).then_inc(h2s.sem, 1)

            def second(t):
                dve.wait_ge(lgp.sem, lgp.at(t))
                nc.vector.tensor_tensor(g["logits"][:, bass.ds(t, 1)].rearrange("p o n -> p (o n)"), pl[:, 0:NG + NE], br[:], ALU.add).then_inc(lgs.sem, 1)

            first(0, 0, 0)
            with dve.Fori(0, NL // 2 - 1) as i:
                first(i * 2 + 1, i, 1)
                second(i * 2)
                first(i * 2 + 2, i + 1, 0)
                second(i * 2 + 1)
            first(NL - 1, NL // 2 - 1, 1)
            second(NL - 2)
            second(NL - 1)


def routing(nc, kit, io, g, dram):
    T4, T8, T32 = [P, NL, NG], [P, NL, EPG], [P, NL, NE]
    BIG = 1e30
    with ExitStack() as st:
        iota = kit.sb("o_iota", [P, EPG], stack=st)
        mult = kit.sb("o_mult", [P, NL - 1], stack=st)
        mg = kit.sb("o_mg", [P, NL], stack=st)
        e4 = kit.sb("o_e4", T4, stack=st)
        og = kit.sb("o_og", T4, stack=st)
        den = kit.sb("o_den", [P, NL], stack=st)
        w32 = kit.sb("o_w32", [P, NL, NG, EPG], stack=st)
        le = kit.sb("o_le", T8, stack=st)
        c8 = kit.sb("o_c8", T8, stack=st)
        m12 = kit.sb("o_m12", [P, 2, NL], stack=st)
        fi = kit.sb("o_fi", [P, NL], stack=st)
        o8 = kit.sb("o_o8", [P, 2, NL, EPG], stack=st)
        oh = kit.sb("o_oh", [P, 2, NL, NG, EPG], stack=st)
        both = kit.sb("o_both", T32, stack=st)
        rank = kit.sb("o_rank", T32, stack=st)
        tot = kit.sb("o_tot", [P, NL + 1, NE], stack=st)
        cnt = kit.sb("o_cnt", [P, NE], stack=st)
        zero = kit.sb("o_zero", [P, NE], stack=st)
        start = kit.sb("o_start", [P, NE], stack=st)
        cmp = kit.sb("o_cmp", [P, NE, NL - 1], stack=st)
        nb = kit.sb("o_nb", [P, NE], stack=st)
        sl = kit.sb("o_sl", [P, 2, NL], stack=st)
        ex = kit.sb("o_ex", [P, NL], stack=st)
        h2 = kit.sb("o_h2", [P, 4, D], stack=st)
        z = kit.sb("o_z", [P, D], stack=st)
        pr = kit.ps("o_pr", [P, 2, 512], st)
        c_in = kit.landing("o_const_in", dmas=2)
        h_in = kit.landing("o_h_in", 4)
        h_out = kit.landing("o_h_out", 4, dmas=2)
        z_out = kit.landing("o_z_out")
        step = kit.counter("o_step", 1)
        asked = kit.counter("o_exp_done", 2)
        counts = kit.counter("o_counts")
        zeroed = kit.counter("o_zeroed")
        marks = {}
        block = st.enter_context(nc.Block())

        @block.vector
        def _(dve):
            n = [0]
            V = nc.vector

            def link(ins):
                n[0] += 1
                ins.then_inc(step.sem, 1)
                dve.wait_ge(step.sem, n[0])

            def first_of(values, largest, out, width):
                link(V.tensor_tensor(out, values, largest.unsqueeze(2).to_broadcast([P, NL, width]), ALU.is_lt))
                link(V.scalar_tensor_tensor(out=out, in0=out, scalar=99.0, in1=iota[:, 0:width].unsqueeze(1).to_broadcast([P, NL, width]), op0=ALU.mult, op1=ALU.add))
                link(V.tensor_reduce(fi[:], out, AX, ALU.min))
                link(V.tensor_tensor(out, out, fi[:].unsqueeze(2).to_broadcast([P, NL, width]), ALU.is_equal))

            dve.wait_ge(c_in.sem(0), c_in.at(0))
            link(V.memset(zero[:], 0.0))
            lg4 = g["logits"][:, :, 0:NG]
            le32 = g["logits"][:, :, NG:].rearrange("p t (g e) -> p t g e", g=NG)
            link(V.tensor_reduce(mg[:], lg4, AX, ALU.max))
            link(V.tensor_tensor(e4[:], lg4, mg[:].unsqueeze(2).to_broadcast(T4), ALU.subtract))
            marks["shifted"] = n[0]
            first_of(lg4, mg[:], og[:], NG)
            link(V.tensor_tensor(w32[:], le32, og[:].unsqueeze(3).to_broadcast([P, NL, NG, EPG]), ALU.mult))
            link(V.tensor_reduce(le[:], w32[:].rearrange("p t g e -> p t e g"), AX, ALU.add))
            link(V.tensor_reduce(m12[:, 0], le[:], AX, ALU.max))
            first_of(le[:], m12[:, 0], o8[:, 0], EPG)
            link(V.scalar_tensor_tensor(out=c8[:], in0=o8[:, 0], scalar=-BIG, in1=le[:], op0=ALU.mult, op1=ALU.add))
            link(V.tensor_reduce(m12[:, 1], c8[:], AX, ALU.max))
            first_of(c8[:], m12[:, 1], o8[:, 1], EPG)
            link(V.tensor_tensor(ex[:], m12[:, 1], m12[:, 0], ALU.subtract))
            marks["difference"] = n[0]
            for k in range(2):
                link(V.tensor_tensor(oh[:, k], og[:].unsqueeze(3).to_broadcast([P, NL, NG, EPG]), o8[:, k].unsqueeze(2).to_broadcast([P, NL, NG, EPG]), ALU.mult))
            link(V.tensor_tensor(both[:], oh[:, 0].rearrange("p t g e -> p t (g e)"), oh[:, 1].rearrange("p t g e -> p t (g e)"), ALU.add))
            marks["chosen"] = n[0]
            dve.wait_ge(asked.sem, 2)
            link(V.tensor_reduce(den[:], e4[:], AX, ALU.add))
            link(V.scalar_tensor_tensor(out=den[:], in0=ex[:], scalar=1.0, in1=den[:], op0=ALU.add, op1=ALU.mult))
            link(V.reciprocal(g["wtop"][:, 0], den[:]))
            link(V.tensor_tensor(g["wtop"][:, 1], g["wtop"][:, 0], ex[:], ALU.mult))
            dve.wait_ge(counts.sem, counts.at(0))
            link(V.memset(tot[:, 0], 0.0))
            link(V.tensor_copy(rank[:], pr[:, 0].rearrange("p (t e) -> p t e", e=NE)))
            for t in range(NL):
                link(V.tensor_tensor(tot[:, t + 1], tot[:, t], pr[:, 1, t * NE:(t + 1) * NE], ALU.add))
            link(V.tensor_tensor_scan(start[:], tot[:, NL], zero[:], 0.0, ALU.add, ALU.add))
            link(V.tensor_tensor(start[:], start[:], tot[:, NL], ALU.subtract))
            link(V.tensor_tensor(rank[:], rank[:], tot[:, 0:NL], ALU.add))
            link(V.tensor_tensor(rank[:], rank[:], start[:].unsqueeze(1).to_broadcast(T32), ALU.add))
            for k in range(2):
                link(V.tensor_tensor(w32[:].rearrange("p t g e -> p t (g e)"), oh[:, k].rearrange("p t g e -> p t (g e)"), rank[:], ALU.mult))
                link(V.tensor_reduce(sl[:, k], w32[:].rearrange("p t g e -> p t (g e)"), AX, ALU.add))
            link(V.tensor_copy(g["slots"][:], sl[:]))
            marks["slots"] = n[0]
            link(V.tensor_tensor(cmp[:], tot[:, NL].unsqueeze(2).to_broadcast([P, NE, NL - 1]), mult[:].unsqueeze(1).to_broadcast([P, NE, NL - 1]), ALU.is_gt))
            link(V.tensor_reduce(nb[:], cmp[:], AX, ALU.add))
            link(V.tensor_scalar(nb[:], nb[:], 1.0, None, ALU.add))
            link(V.tensor_copy(g["spans"][:, 0], start[0:1]))
            link(V.tensor_copy(g["spans"][:, 1], nb[0:1]))

        @block.scalar
        def _(act):
            act.wait_ge(step.sem, marks["shifted"])
            nc.scalar.activation(e4[:], e4[:], ACT.Exp).then_inc(asked.sem, 1)
            act.wait_ge(step.sem, marks["difference"])
            nc.scalar.activation(ex[:], ex[:], ACT.Exp).then_inc(asked.sem, 1)

        @block.tensor
        def _(pe):
            pe.wait_ge(step.sem, marks["chosen"])
            flat = both[:].rearrange("p t e -> p (t e)")
            nc.tensor.matmul(pr[:, 0], g["tri"][:, 3], flat, start=True, stop=True)
            nc.tensor.matmul(pr[:, 1], g["tri"][:, 4], flat, start=True, stop=True).then_inc(counts.sem, 1)

        @block.sync
        def _(sp):
            sp.dma_start(iota[:], io["iota8"]).then_inc(c_in.sem(0), 16)
            sp.dma_start(mult[:], io["multiples"]).then_inc(c_in.sem(0), 16)
            for t in range(NL):
                if t >= 4:
                    sp.wait_ge(h_out.sem(t % 4), 32 * (t // 4))
                sp.dma_start(h2[:, t % 4], dram["h2"][t]).then_inc(h_in.sem(t % 4), 16)

        @block.gpsimd
        def _(pool):
            nc.gpsimd.memset(z[:], 0.0).then_inc(zeroed.sem, 1)
            pool.wait_ge(zeroed.sem, 1)
            for rows in ("hs", "ys"):
                pool.dma_start(dram[rows][2 * SEQ:ROWS, :], z[:]).then_inc(z_out.sem(0), 16)
            pool.wait_ge(step.sem, marks["slots"])
            for t in range(NL):
                pool.wait_ge(h_in.sem(t % 4), 16 * (t // 4 + 1))
                for k in range(2):
                    pool.indirect_dma_start(dram["hs"], bass.IndirectOffsetOnAxis(ap=g["slots"][:, k, t:t + 1], axis=0), h2[:, t % 4], None).then_inc(h_out.sem(t % 4), 16)
            for s in range(4):
                pool.wait_ge(h_out.sem(s), 32 * NL // 4)
            pool.wait_ge(z_out.sem(0), 32)


def experts(nc, kit, io, g, dram):
    MAXB = NL
    F32R = mybir.dt.float32r
    THIRD = 2 * KD * DE // 2
    HALF = THIRD // 2
    with ExitStack() as st:
        raw = kit.sb("e_w_raw", [P, 3, THIRD], stack=st)
        wh = kit.sb("e_w_high", [P, 3, THIRD], F32R, stack=st)
        wl = kit.sb("e_w_low", [P, 3, THIRD], F32R, stack=st)
        xb = kit.sb("e_x", [P, D], stack=st)
        xT = kit.sb("e_xT", [P, 2, KD, P], F32R, stack=st)
        sg = kit.sb("e_sg", [P, 2, 256], stack=st)
        hid = kit.sb("e_hid", [P, DE], stack=st)
        hT = kit.sb("e_hT", [P, 2, DE // P, P], F32R, stack=st)
        y = kit.sb("e_y", [P, D], stack=st)
        pX = kit.ps("e_pX", [P, KD, P], st)
        pG = kit.ps("e_pG", [P, 2, 2, 256], st)
        pH = kit.ps("e_pH", [P, 2, 4, P], st)
        pY = kit.ps("e_pY", [P, 2, 512], st)
        w_in = kit.landing("e_w_in", 3, dmas=2)
        x_in = kit.landing("e_x_in")
        y_out = kit.landing("e_y_out", credit=16)
        whs = kit.counter("e_w_high_ready", 6)
        wls = kit.counter("e_w_low_ready", 6, credit=6)
        xTt = kit.counter("e_x_transposed", 1, credit=1)
        xTs = kit.counter("e_xT_high_ready", 1, credit=1)
        xTl = kit.counter("e_xT_low_ready", 1, credit=1)
        prodG = kit.counter("e_gate_up", 2, credit=2)
        sgs = kit.counter("e_silu", 2, credit=2)
        hids = kit.counter("e_hidden", 2, credit=2)
        hTt = kit.counter("e_hidden_transposed", 2, credit=2)
        hTs = kit.counter("e_hT_high_ready", 2, credit=2)
        hTl = kit.counter("e_hT_low_ready", 2, credit=2)
        prodY = kit.counter("e_down", 1, credit=1)
        ya = kit.counter("e_y_act", 1, credit=1)
        yd = kit.counter("e_y_dve", 1, credit=1)
        junk = kit.counter("e_paused")
        block = st.enter_context(nc.Block())

        def over_blocks(eng, body, enter=None):
            count = eng.alloc_register("e_block")
            eng.reg_mov(count, 0)
            at = eng.alloc_register("e_row")
            left = eng.alloc_register("e_blocks_left")

            def one(following):
                body(eng.snap(count, min_val=0, max_val=2 * NE), eng.snap(at, min_val=0, max_val=2 * SEQ), following)
                eng.reg_add(count, count, 1)
                eng.reg_add(at, at, P)

            def expert(e, following):
                blocks = eng.value_load(g["spans"][0:1, 1, bass.ds(e, 1)], min_val=1, max_val=MAXB)
                row0 = eng.value_load(g["spans"][0:1, 0, bass.ds(e, 1)], min_val=0, max_val=2 * SEQ)
                eng.reg_mov(at, row0)
                if enter:
                    enter(e)
                if following is None:
                    with eng.Fori(0, blocks) as j:
                        one(None)
                else:
                    eng.reg_mov(left, blocks)
                    with eng.If_ne(left, 1):
                        with eng.Fori(1, blocks) as j:
                            one(None)
                    one(following)

            with eng.Fori(0, NE - 1) as e:
                expert(e, e + 1)
            expert(NE - 1, None)
            return count

        @block.sync
        def _(sp):
            with sp.Fori(0, NE) as e:
                for third in range(3):
                    sp.wait_ge(wls.sem, wls.at(e - 1, 2 * third + 2))
                    for n, src in enumerate(("moe_w_gate", "moe_w_up")):
                        if third < 2:
                            to = raw[:, third].rearrange("p (k n f) -> p k n f", k=KD, n=2)[:, :, n]
                            sp.dma_start(to, io[src][0, bass.ds(e, 1), :, third * 256:(third + 1) * 256].rearrange("o (k p) f -> p (o k) f", p=P)).then_inc(w_in.sem(third), 16)
                        else:
                            to = raw[:, third, n * HALF:(n + 1) * HALF].rearrange("p (k f) -> p k f", k=2)
                            sp.dma_start(to, io["moe_w_down"][0, bass.ds(e, 1), n * 256:(n + 1) * 256].rearrange("o (k p) f -> p (o k) f", p=P)).then_inc(w_in.sem(third), 16)

        @block.gpsimd
        def _(pool):
            def load(b, row, following):
                pool.wait_ge(xTt.sem, xTt.at(b - 1))
                pool.sem_inc(junk.sem, 1)
                pool.dma_start(xb[:], dram["hs"][bass.ds(row, P), :]).then_inc(x_in.sem(0), 16)
            count = over_blocks(pool, load)
            b = pool.snap(count, min_val=0, max_val=2 * NE)
            pool.wait_ge(xTt.sem, xTt.at(b - 1))
            pool.sem_inc(junk.sem, 1)
            pool.dma_start(xb[:], dram["hs"][0:P, :]).then_inc(x_in.sem(0), 16)

        @block.tensor
        def _(pe):
            for x_ in (xTt, prodG, hTt, prodY):
                pe.sem_inc(x_.sem, x_.credit)
            ident = g["ident"][:, :]

            def turn_x(b):
                pe.wait_ge(x_in.sem(0), x_in.at(b))
                pe.wait_ge(xTl.sem, xTl.at(b - 1))
                for k in range(KD):
                    m = nc.tensor.transpose(pX[:, k], xb[:, k * P:(k + 1) * P], ident)
                m.then_inc(xTt.sem, 1)

            def turn_h(b, half):
                pe.wait_ge(hids.sem, hids.at(b, half + 1))
                pe.wait_ge(hTl.sem, hTl.at(b - 1, half + 1))
                for c in range(2):
                    m = nc.tensor.transpose(pH[:, half, c], hid[:, (2 * half + c) * P:(2 * half + c + 1) * P], ident)
                m.then_inc(hTt.sem, 1)

            def body(b, row, following, e=None):
                for half in range(2):
                    pe.wait_ge(hids.sem, hids.at(b - 1, half + 1))
                    pe.wait_ge(xTs.sem, xTs.at(b))
                    pe.wait_ge(wls.sem, wls.at(expert_of[0], 2 * half + 2))
                    for k in range(KD):
                        w = slice(k * 512, (k + 1) * 512)
                        nc.tensor.matmul(pG[:, half], xT[:, 0, k], wh[:, half, w], start=(k == 0), stop=False)
                        nc.tensor.matmul(pG[:, half], xT[:, 0, k], wl[:, half, w], start=False, stop=False)
                    pe.wait_ge(xTl.sem, xTl.at(b))
                    for k in range(KD):
                        m = nc.tensor.matmul(pG[:, half], xT[:, 1, k], wh[:, half, k * 512:(k + 1) * 512], start=False, stop=(k == KD - 1))
                    m.then_inc(prodG.sem, 1)
                turn_h(b, 0)
                turn_x(b + 1)
                turn_h(b, 1)
                pe.wait_ge(ya.sem, ya.at(b - 1))
                pe.wait_ge(yd.sem, yd.at(b - 1))
                pe.wait_ge(wls.sem, wls.at(expert_of[0], 6))
                for k in range(DE // P):
                    for part, with_ in ((0, wh), (0, wl), (1, wh)):
                        if k % 2 == 0:
                            part_ready = hTl if part else hTs
                            pe.wait_ge(part_ready.sem, part_ready.at(b, k // 2 + 1))
                        for n in range(2):
                            c0 = k * D + n * 512
                            m = nc.tensor.matmul(pY[:, n], hT[:, part, k], with_[:, 2, c0:c0 + 512], start=(k == 0 and part == 0 and with_ is wh),
                                                 stop=(k == DE // P - 1 and part == 1))
                m.then_inc(prodY.sem, 1)

            expert_of = [None]

            def enter(e):
                expert_of[0] = e
            turn_x(0)
            over_blocks(pe, body, enter)

        @block.scalar
        def _(act):
            for x_ in (xTs, sgs, hTs, ya):
                act.sem_inc(x_.sem, x_.credit)
            act.sem_inc(y_out.sem(0), 16)

            def xT_copy(b):
                act.wait_ge(xTt.sem, xTt.at(b))
                act.wait_ge(prodG.sem, prodG.at(b - 1))
                nc.scalar.activation(xT[:, 0], pX[:], ACT.Copy).then_inc(xTs.sem, 1)

            def high(e, third):
                act.wait_ge(w_in.sem(third), w_in.at(e))
                for n in range(2):
                    part = slice(n * HALF, (n + 1) * HALF)
                    nc.scalar.activation(wh[:, third, part], raw[:, third, part], ACT.Copy).then_inc(whs.sem, 1)

            def body(b, row, following):
                for half in range(2):
                    act.wait_ge(prodG.sem, prodG.at(b, half + 1))
                    nc.scalar.activation(sg[:, half], pG[:, half, 0], ACT.Silu).then_inc(sgs.sem, 1)
                    if following is not None and half == 0:
                        high(following, 0)
                for half in range(2):
                    act.wait_ge(hTt.sem, hTt.at(b, half + 1))
                    act.wait_ge(prodY.sem, prodY.at(b - 1))
                    nc.scalar.activation(hT[:, 0, 2 * half:2 * half + 2], pH[:, half, 0:2], ACT.Copy).then_inc(hTs.sem, 1)
                    if half == 0:
                        xT_copy(b + 1)
                if following is not None:
                    high(following, 1)
                act.wait_ge(prodY.sem, prodY.at(b))
                act.wait_ge(y_out.sem(0), b * 16 + 16)
                nc.scalar.activation(y[:, 0:512], pY[:, 0], ACT.Copy).then_inc(ya.sem, 1)
                act.wait_ge(ya.sem, ya.at(b))
                act.wait_ge(yd.sem, yd.at(b))
                act.dma_start(dram["ys"][bass.ds(row, P), :], y[:]).then_inc(y_out.sem(0), 16)
                if following is not None:
                    high(following, 2)
            for third in range(3):
                high(0, third)
            xT_copy(0)
            count = over_blocks(act, body)
            b = act.snap(count, min_val=0, max_val=2 * NE)
            act.wait_ge(y_out.sem(0), b * 16 + 16)
            act.sem_inc(junk.sem, 1)

        @block.vector
        def _(dve):
            for x_ in (xTl, hids, hTl, yd, wls):
                dve.sem_inc(x_.sem, x_.credit)

            def xT_low(b):
                dve.wait_ge(xTs.sem, xTs.at(b))
                nc.vector.tensor_tensor(xT[:, 1], pX[:], xT[:, 0].bitcast(F32), ALU.subtract).then_inc(xTl.sem, 1)

            def low(e, third):
                for n in range(2):
                    part = slice(n * HALF, (n + 1) * HALF)
                    dve.wait_ge(whs.sem, whs.at(e, 2 * third + n + 1))
                    nc.vector.tensor_tensor(wl[:, third, part], raw[:, third, part], wh[:, third, part].bitcast(F32), ALU.subtract).then_inc(wls.sem, 1)

            def body(b, row, following):
                for half in range(2):
                    dve.wait_ge(sgs.sem, sgs.at(b, half + 1))
                    dve.wait_ge(hTt.sem, hTt.at(b - 1, half + 1))
                    nc.vector.tensor_tensor(hid[:, half * 256:(half + 1) * 256], sg[:, half], pG[:, half, 1], ALU.mult).then_inc(hids.sem, 1)
                    if following is not None and half == 0:
                        low(following, 0)
                for half in range(2):
                    dve.wait_ge(hTs.sem, hTs.at(b, half + 1))
                    nc.vector.tensor_tensor(hT[:, 1, 2 * half:2 * half + 2], pH[:, half, 0:2], hT[:, 0, 2 * half:2 * half + 2].bitcast(F32), ALU.subtract).then_inc(hTl.sem, 1)
                    if half == 0:
                        xT_low(b + 1)
                if following is not None:
                    low(following, 1)
                dve.wait_ge(prodY.sem, prodY.at(b))
                dve.wait_ge(y_out.sem(0), b * 16 + 16)
                nc.vector.tensor_copy(y[:, 512:D], pY[:, 1]).then_inc(yd.sem, 1)
                if following is not None:
                    low(following, 2)
            for third in range(3):
                low(0, third)
            xT_low(0)
            over_blocks(dve, body)


def combine(nc, kit, io, g, dram):
    B = 3
    with ExitStack() as st:
        yy = kit.sb("c_yy", [P, B, 2, D], stack=st)
        x1 = kit.sb("c_x1", [P, B, D], stack=st)
        v = kit.sb("c_v", [P, B, D], stack=st)
        sq = kit.sb("c_sq", [P, B, D], stack=st)
        ss = kit.sb("c_ss", [P, B, 2], stack=st)
        y_in = kit.landing("c_y_in", B, dmas=2)
        x_in = kit.landing("c_x_in", B)
        o_out = kit.landing("c_out", B)
        summed = kit.counter("c_summed", 2)
        ssq = kit.counter("c_ssq")
        eps_added = kit.counter("c_eps_added")
        rstd = kit.counter("c_rstd")
        outs = kit.counter("c_out_ready", 2)
        block = st.enter_context(nc.Block())

        @block.gpsimd
        def _(pool):
            def gather(t):
                if t >= B:
                    pool.wait_ge(summed.sem, summed.at(t - B))
                for k in range(2):
                    pool.indirect_dma_start(yy[:, t % B, k], None, dram["ys"], bass.IndirectOffsetOnAxis(ap=g["slots"][:, k, t:t + 1], axis=0)).then_inc(y_in.sem(t % B), 16)

            def root(t):
                pool.wait_ge(ssq.sem, ssq.at(t))
                rstd_root(nc, g, pool, eps_added, t, 1, ss[:, t % B, 1:2], ss[:, t % B, 0:1], D).then_inc(rstd.sem, 1)
            for t in range(NL + 2):
                if t < NL:
                    gather(t)
                if t >= 2:
                    root(t - 2)

        @block.sync
        def _(sp):
            def load(t):
                if t >= B:
                    sp.wait_ge(outs.sem, outs.at(t - B))
                sp.dma_start(x1[:, t % B], dram["x1"][t]).then_inc(x_in.sem(t % B), 16)

            def store(t):
                sp.wait_ge(outs.sem, outs.at(t))
                sp.dma_start(io["out0"][0, t * P:(t + 1) * P, :], v[:, t % B]).then_inc(o_out.sem(t % B), 16)
            for t in range(NL + B - 1):
                if t >= B - 1:
                    store(t - B + 1)
                if t < NL:
                    load(t)
            for s in range(B):
                sp.wait_ge(o_out.sem(s), 16 * len(range(s, NL, B)))

        @block.scalar
        def _(act):
            for t in range(NL):
                act.wait_ge(summed.sem, summed.at(t))
                if t >= B:
                    act.wait_ge(outs.sem, outs.at(t - B))
                nc.scalar.activation(sq[:, t % B], v[:, t % B], ACT.Square, accum_out=ss[:, t % B, 0:1]).then_inc(ssq.sem, 1)

        @block.vector
        def _(dve):
            def add(t):
                s = t % B
                dve.wait_ge(y_in.sem(s), y_in.at(t // B))
                if t >= B:
                    dve.wait_ge(o_out.sem(s), 16 * (t // B))
                nc.vector.tensor_scalar(v[:, s], yy[:, s, 0], g["wtop"][:, 0, t:t + 1], None, ALU.mult).then_inc(summed.sem, 1)
                dve.wait_ge(summed.sem, summed.at(t, 1))
                nc.vector.scalar_tensor_tensor(out=v[:, s], in0=yy[:, s, 1], scalar=g["wtop"][:, 1, t:t + 1], in1=v[:, s], op0=ALU.mult, op1=ALU.add).then_inc(summed.sem, 1)

            def finish(t):
                s = t % B
                dve.wait_ge(rstd.sem, rstd.at(t))
                nc.vector.scalar_tensor_tensor(out=v[:, s], in0=v[:, s], scalar=ss[:, s, 1:2], in1=g["mod"][:, 5 * D:6 * D], op0=ALU.mult, op1=ALU.mult).then_inc(outs.sem, 1)
                dve.wait_ge(outs.sem, outs.at(t, 1))
                dve.wait_ge(x_in.sem(s), x_in.at(t // B))
                nc.vector.tensor_tensor(v[:, s], v[:, s], x1[:, s], ALU.add).then_inc(outs.sem, 1)
            for t in range(NL + 1):
                if t < NL:
                    add(t)
                if t >= 1:
                    finish(t - 1)


def program(nc, io):
    kit = Kit(nc)
    g = globals_of(kit)

    def scratch(name, shape):
        return nc.dram_tensor(name, shape, F32).ap()
    dram = {
        "tok": scratch("by_token", (NT, P, NTOK)),
        "ch": scratch("by_channel", (NCH, P, NT * P)),
        "u": scratch("convolved", (NCH, P, NT * P)),
        "sb": scratch("backward_states", (NT, P, D)),
        "y": scratch("mixed", (NT, P, D)),
        "x1": scratch("after_mixing", (NL, P, D)),
        "h2": scratch("second_norm", (NL, P, D)),
        "hs": scratch("rows_sorted", (ROWS, D)),
        "ys": scratch("rows_done", (ROWS, D)),
    }
    for stage in (modulation, projection, convolution, states, mixing, residual, routing, experts, combine):
        if stage is convolution:
            g.update(routing_globals_of(kit))
            mixing_only = ExitStack()
            g.update(mixing_globals_of(kit, mixing_only))
        if stage is routing:
            mixing_only.close()
            kit.retire()
        stage(nc, kit, io, g, dram)
    kit.keep.close()


_INS = ['x', 'c', 'ctx', 'c_ctx', 'w_mod', 'b_mod', 'norm_pre_mix', 'norm_post_mix', 'norm_pre_ffn',
        'norm_post_ffn', 'w_in', 'w_out', 'ret_decay_f', 'ret_decay_b', 'ret_gn_w', 'ssd_conv_w',
        'ssd_conv_b', 'ssd_dt_bias_f', 'ssd_dt_bias_b', 'ssd_a_log_f', 'ssd_a_log_b', 'ssd_d',
        'ssd_norm_w', 'moe_w_rg', 'moe_b_rg', 'moe_w_re', 'moe_b_re', 'moe_w_gate', 'moe_w_up', 'moe_w_down']
_OUTS = [((1, SEQ, D), 'float32')]


def constants():
    f = np.float32
    quarter = P // 4
    freq = 10000.0 ** (-np.arange(quarter) / quarter)
    t = np.arange(SEQ)
    ang = np.stack([(t // 64)[:, None] * freq, (t % 64)[:, None] * freq], 1)
    cos = np.repeat(np.cos(ang)[:, :, None], 2, 2).reshape(SEQ, P)
    sin = np.stack([-np.sin(ang), np.sin(ang)], 2).reshape(SEQ, P)
    cos = np.concatenate([np.ones((CTX, P)), cos])
    sin = np.concatenate([np.zeros((CTX, P)), sin])
    s = float(P) ** -0.5
    rope = np.stack([cos, sin, cos * s, sin * s], 1).reshape(NT, P, 4 * P).astype(f)
    i = np.arange(P)
    rel = i[None, :] - i[:, None]
    return {
        "rope": rope,
        "ident": np.eye(P, dtype=f),
        "tri": np.stack([rel >= 0, rel < 0, rel <= 0, rel > 0, rel < 9999], 1).astype(f),
        "rel": np.stack([np.maximum(rel, 0), np.maximum(-rel, 0), np.tile(i + 1, (P, 1)), np.tile(P - i, (P, 1))], 1).astype(f),
        "relk": np.stack([P - 1 - i, i], 1).astype(f),
        "iota8": np.tile(np.arange(EPG).astype(f), (P, 1)),
        "multiples": np.tile(np.arange(1, NL).astype(f) * P, (P, 1)),
    }


def kernel(**inputs):
    import concourse.bacc as _bacc
    from concourse import mybir as _mybir
    from concourse.bass_utils import run_bass_kernel_spmd as _run

    nc = _bacc.Bacc("TRN2", target_bir_lowering=False, num_devices=1)
    arrays, io = {}, {}
    given = {name: np.ascontiguousarray(inputs[name]) for name in _INS}
    for name, a in {**given, **constants()}.items():
        arrays[f"in_{name}_dram"] = a
        io[name] = nc.dram_tensor(f"in_{name}_dram", a.shape, _mybir.dt.from_np(a.dtype), kind="ExternalInput").ap()
    for i, (shape, dtype) in enumerate(_OUTS):
        dt = _mybir.dt.from_np(np.dtype(dtype))
        io[f"out{i}"] = nc.dram_tensor(f"out_{i}_dram", shape, dt, kind="ExternalOutput").ap()
    program(nc, io)
    r = _run(nc, [arrays], core_ids=[0])
    got = tuple(r.results[0][f"out_{i}_dram"] for i in range(len(_OUTS)))
    return got[0]
```

```python
from contextlib import ExitStack

import numpy as np
import concourse.bass as bass
from concourse import mybir

F32 = mybir.dt.float32
I32 = mybir.dt.int32
F32R = mybir.dt.float32r
ALU = mybir.AluOpType
ACT = mybir.ActivationFunctionType
AX = mybir.AxisListType.X

P = 128
D = 1024
KD = D // P
SEQ = 2048
CTX = 256
NT = (SEQ + CTX) // P
NCT = CTX // P
NL = SEQ // P
RH = 4
RW = 512
SH = 8
SP_ = 64
SG = 2
DPROJ = 3600
NTOK = 5 * 512 + 16
NCH = 8
CONV = 5
NG = 4
EPG = 8
NE = 32
DE = 512
ROWS = 2 * SEQ + P
EPS = 1e-6
EPS_OF = {1: 0, 512: 4, D: 8}


class Counter:

    def __init__(self, sem, per=1, credit=0):
        self.sem, self.per, self.credit = sem, per, credit

    def at(self, turn, n=None):
        return turn * self.per + (self.credit + (self.per if n is None else n))


class Landing:

    def __init__(self, sems, dmas=1, credit=0):
        self.sems, self.dmas, self.credit = sems, dmas, credit

    def sem(self, slot):
        return self.sems[slot]

    def at(self, use):
        return use * (16 * self.dmas) + (16 * self.dmas + self.credit)


class Kit:

    def __init__(self, nc):
        self.nc = nc
        self.keep = ExitStack()
        self.sems = []

    def semaphore(self, name):
        self.sems.append(self.nc.alloc_semaphore(name))
        return self.sems[-1]

    def counter(self, name, per=1, credit=0):
        return Counter(self.semaphore(name), per, credit)

    def landing(self, name, slots=1, dmas=1, credit=0):
        return Landing([self.semaphore(f"{name}{s}") for s in range(slots)], dmas, credit)

    def retire(self):
        self.nc.clear_and_free_semaphores(self.sems)
        self.nc.all_engine_barrier()
        self.sems = []

    def sb(self, name, shape, dt=F32, stack=None):
        return (stack or self.keep).enter_context(self.nc.sbuf_tensor(name, shape, dt))

    def ps(self, name, shape, stack):
        return stack.enter_context(self.nc.psum_tensor(name, shape, F32))


def pairs(eng, first, last):
    with eng.Fori(0, (last - first) // 2) as i:
        for s in range(2):
            yield i * 2 + (first + s), i, s


def globals_of(kit):
    return {
        "ident": kit.sb("ident", [P, P]),
        "csil": kit.sb("csil", [P, 2, KD]),
        "cols": kit.sb("cols", [P, 2, KD, 2]),
        "neghalf": kit.sb("neghalf", [P, 16]),
        "eps": kit.sb("eps", [P, 12]),
    }


def mixing_globals_of(kit, st):
    return {
        "E": kit.sb("E", [P, NT, 6, SH], stack=st),
        "dd": kit.sb("dd", [P, NT, 4, SH], stack=st),
        "dskip": kit.sb("dskip", [P, SH], stack=st),
        "wn": kit.sb("wn", [P, KD], stack=st),
        "DT": kit.sb("DT", [P, RH, P], stack=st),
        "Dq": kit.sb("Dq", [P, 2, RH, P], stack=st),
        "Dk": kit.sb("Dk", [P, 2, RH], stack=st),
        "Dtot": kit.sb("Dtot", [P, 2, RH], stack=st),
        "sf": kit.sb("sf", [P, 2, 2, 512], stack=st),
    }


def routing_globals_of(kit):
    return {
        "tri": kit.sb("tri", [P, 5, P]),
        "mod": kit.sb("mod", [P, 4, D]),
        "logits": kit.sb("logits", [P, NL, NG + NE]),
        "slots": kit.sb("slots", [P, 2, NL], I32),
        "wtop": kit.sb("wtop", [P, 2, NL]),
        "spans": kit.sb("spans", [1, 2, NE], I32),
    }


def tile_of(dram, t, lo=None, hi=None):
    v = dram[bass.ds(t, 1), :, :] if lo is None else dram[bass.ds(t, 1), :, lo:hi]
    return v.rearrange("o p f -> p (o f)")


def modulation(nc, kit, io, g, dram):
    NMOD = 4
    with ExitStack() as st:
        ccol = kit.sb("ccol", [P, 2, KD], stack=st)
        csil = g["csil"]
        shift_scale = kit.sb("shift_scale", [P, 2 * D], stack=st)
        both = kit.sb("both", [P, KD, P], stack=st)
        wm = kit.sb("wm", [P, 2, KD, 512], stack=st)
        bm = kit.sb("bm", [P, 2, 512], stack=st)
        ncol = kit.sb("ncol", [P, KD], stack=st)
        acc = kit.ps("mod_acc", [P, 2, 512], st)
        colT = kit.ps("mod_colT", [P, 4, 4, P], st)
        c_in = kit.landing("c_in", dmas=2)
        w_in = kit.landing("wmod_in", 2, dmas=2)
        n_in = kit.landing("norm_cols_in", dmas=2)
        silu = kit.counter("c_silu")
        spread = kit.counter("c_spread", 2)
        row_acc = kit.counter("mod_row_acc", 1, credit=2)
        row = kit.counter("mod_row", 1, credit=2)
        cols_t = kit.counter("mod_cols_t")
        fin = kit.counter("mod_final")
        block = st.enter_context(nc.Block())

        @block.sync
        def _(sp):
            for n, src in enumerate((io["c"].rearrange("a d -> (a d)"), io["c_ctx"])):
                sp.dma_start(ccol[:, n, :], src.rearrange("(k p) -> p k", p=P), allow_slow_non_contiguous=True).then_inc(c_in.sem(0), 16)
            sp.dma_start(ncol[:, :], io["norm_pre_mix"].rearrange("o (k p) -> p (o k)", p=P), allow_slow_non_contiguous=True).then_inc(n_in.sem(0), 16)
            sp.dma_start(g["ident"][:, :], io["ident"]).then_inc(n_in.sem(0), 16)
            wsrc = io["w_mod"].rearrange("o (k p) (n f) -> n p (o k) f", p=P, f=512)
            bsrc = io["b_mod"].rearrange("o (n f) -> n o f", f=512)
            for t, use, s in pairs(sp, 0, NMOD):
                sp.wait_ge(row_acc.sem, row_acc.at(t - 2))
                sp.wait_ge(row.sem, row.at(t - 2))
                sp.dma_start(wm[:, s], wsrc[bass.ds(t, 1)].rearrange("o p k f -> p (o k) f")).then_inc(w_in.sem(s), 16)
                sp.dma_start(bm[:, s], bsrc[bass.ds(t, 1)].rearrange("a o f -> (a o) f").to_broadcast([P, 512])).then_inc(w_in.sem(s), 16)

        @block.gpsimd
        def _(pool):
            nc.gpsimd.memset(g["neghalf"][:], -0.5)
            for count, at in EPS_OF.items():
                nc.gpsimd.memset(g["eps"][:, at:at + 4], count * EPS)

        @block.scalar
        def _(act):
            act.wait_ge(c_in.sem(0), c_in.at(0))
            nc.scalar.activation(csil[:], ccol[:], ACT.Silu).then_inc(silu.sem, 1)

        @block.tensor
        def _(pe):
            pe.sem_inc(row_acc.sem, row_acc.credit)
            pe.wait_ge(spread.sem, spread.at(0))

            for t, use, s in pairs(pe, 0, NMOD):
                pe.wait_ge(w_in.sem(s), w_in.at(use))
                pe.wait_ge(row.sem, row.at(t - 2))
                for k in range(KD):
                    m = nc.tensor.matmul(acc[:, s], both[:, k], wm[:, s, k], start=(k == 0), stop=(k == KD - 1))
                m.then_inc(row_acc.sem, 1)
            pe.wait_ge(row.sem, row.at(NMOD - 1))
            pe.wait_ge(n_in.sem(0), n_in.at(0))
            for b in range(16):
                m = nc.tensor.transpose(colT[:, b // 4, b % 4], shift_scale[:, b * P:(b + 1) * P], g["ident"][:, :])
            m.then_inc(cols_t.sem, 1)

        @block.vector
        def _(dve):
            dve.sem_inc(row.sem, row.credit)
            dve.wait_ge(silu.sem, silu.at(0))
            nc.vector.tensor_copy(both[:, :, 0:64], csil[:, 0, :, None].to_broadcast([P, KD, 64])).then_inc(spread.sem, 1)
            nc.vector.tensor_copy(both[:, :, 64:P], csil[:, 1, :, None].to_broadcast([P, KD, 64])).then_inc(spread.sem, 1)
            for t, use, s in pairs(dve, 0, NMOD):
                dve.wait_ge(row_acc.sem, row_acc.at(t))
                dve.wait_ge(w_in.sem(s), w_in.at(use))
                nc.vector.tensor_tensor(shift_scale[:, bass.ds(t * 512, 512)], acc[:, s], bm[:, s], ALU.add).then_inc(row.sem, 1)
            dve.wait_ge(n_in.sem(0), n_in.at(0))
            dve.wait_ge(row.sem, row.at(NMOD - 1))
            dve.wait_ge(cols_t.sem, cols_t.at(0))
            nc.vector.tensor_copy(g["cols"][:, 0], colT[:, 0:2, :, 0:65:64].rearrange("p a b c -> p (a b) c"))
            nc.vector.tensor_copy(g["cols"][:, 1], colT[:, 2:4, :, 0:65:64].rearrange("p a b c -> p (a b) c")).then_inc(fin.sem, 1)
            dve.wait_ge(fin.sem, fin.at(0))
            nc.vector.scalar_tensor_tensor(out=g["cols"][:, 1], in0=g["cols"][:, 1], scalar=1.0,
                                           in1=ncol[:, :, None].to_broadcast([P, KD, 2]), op0=ALU.add, op1=ALU.mult)


def rstd_root(nc, g, pool, eps_added, turn, n, out, ssq, count):
    w = out.shape[-1]
    nc.gpsimd.tensor_tensor(out, ssq, g["eps"][:, EPS_OF[count]:EPS_OF[count] + w], ALU.add).then_inc(eps_added.sem, 1)
    pool.wait_ge(eps_added.sem, eps_added.at(turn, n))
    return nc.gpsimd.tensor_tensor(out, out, g["neghalf"][:, 0:w], ALU.pow)


def projection(nc, kit, io, g, dram):
    NGR = NT // 2
    HALF = KD * 512 // 2
    NB = 6
    SPLIT = ("k", "v", "q", "g", "dt", "z", "ch0", "ch1")
    COLUMN = {"q": 0, "k": 1, "v": 2, "g": 3, "z": 4, "ch0": 5, "ch1": 6, "dt": 7}
    PLACE = {"q": 0, "k": 1, "v": 2, "g": 3, "z": 0, "ch0": 1, "ch1": 2}
    LEAVES = {"z": 2, "ch0": 4, "ch1": 6}
    PIECES = [(c, ks) for c in SPLIT for ks in ([slice(0, KD)] if c == "dt" else [slice(k, k + 2) for k in range(0, KD, 2)])]
    LAST = {c: n for n, (c, _) in enumerate(PIECES)}
    OUTS = ([(c, j) for c in ("q", "k", "v") for j in range(2)],
            [(c, j) for c in ("g", "z", "ch0", "ch1") for j in range(2)] + [("dt", 0)])
    DVE_TAKES = ([c in "qk" for c, _ in OUTS[0]], [c[:2] == "ch" and j == 0 for c, j in OUTS[1]])
    TURN_X = ({2: 0, 4: 1}, {4: 0, 6: 1})
    SKIPPED = (2, 4)

    def ordinal(p, o):
        return sum(1 for q in range(o + 1) if DVE_TAKES[p][q] == DVE_TAKES[p][o])

    with ExitStack() as st:
        wh = kit.sb("w_high", [P, 4, KD, 512], F32R, stack=st)
        wl = kit.sb("w_low", [P, 4, KD, 512], F32R, stack=st)
        dh = kit.sb("w_dt_high", [P, KD, 16], F32R, stack=st)
        dl = kit.sb("w_dt_low", [P, KD, 16], F32R, stack=st)
        xt = kit.sb("xt", [P, 2, D], stack=st)
        xn = kit.sb("xn", [P, 2, D], stack=st)
        hh = kit.sb("hT_high", [P, 2, KD, 2 * P], F32R, stack=st)
        hl = kit.sb("hT_low", [P, 2, KD, 2 * P], F32R, stack=st)
        hraw = kit.sb("hT_whole", [P, KD, P], stack=st)
        rope = kit.sb("rope", [P, 2, 4, P], stack=st)
        tok = kit.sb("tok", [P, 2, 3 * 512], stack=st)
        ch = kit.sb("ch", [P, NCH, 2 * P], stack=st)
        raw = ch[:].rearrange("p c t -> p (c t)").rearrange("p (s f) -> p s f", s=2)
        ra = kit.sb("rope_sine_part", [P, 512], stack=st)
        stat = kit.sb("stat", [P, 2, 2], stack=st)
        xT = kit.ps("xT", [P, KD, P], st)
        acc = kit.ps("proj_acc", [P, NB, 512], st)
        w_in = kit.landing("w_in_in", 2)
        x_in = kit.landing("x_in", 2)
        rope_in = kit.landing("rope_in", 2)
        tok_out = kit.landing("tok_out", 2, credit=16)
        ch_out = kit.landing("ch_out", 1, credit=16)
        whs = kit.counter("w_high_ready")
        wls = kit.counter("w_low_ready")
        ssq = kit.counter("x_ssq", 2)
        rstd = kit.counter("x_rstd", 2)
        eps_added = kit.counter("x_eps_added", 2)
        xnorm = kit.counter("x_normed", 2, credit=2)
        xTd = kit.counter("x_transposed", 2, credit=2)
        hTm = kit.counter("hT_modulated", 2, credit=2)
        hTh = kit.counter("hT_high_ready", 2)
        hTl = kit.counter("hT_low_ready", 2, credit=2)
        accd = [kit.counter(f"proj_acc_ready{p}", len(OUTS[p]), credit=len(OUTS[p])) for p in range(2)]
        rtmp = kit.counter("rope_products", 4, credit=2)
        edve = [kit.counter(f"proj_out_dve{p}", sum(DVE_TAKES[p]), credit=sum(DVE_TAKES[p])) for p in range(2)]
        eact = [kit.counter(f"proj_out_act{p}", len(OUTS[p]) - sum(DVE_TAKES[p]), credit=len(OUTS[p]) - sum(DVE_TAKES[p])) for p in range(2)]
        block = st.enter_context(nc.Block())

        def turns(eng, body, between=None):
            body(0, 0, 0, 0, True, False)
            with eng.Fori(0, NGR // 2) as i:
                for s in range(2):
                    t = i * 2 + (1 + s)
                    body(t, 0, t, 1 - s, False, False)
            if between:
                between()
            with eng.Fori(0, NGR // 2 - 1) as i:
                for s in range(2):
                    body(i * 2 + (NGR + s), 1, i * 2 + s, 1 - s, False, False)
            body(2 * NGR - 3, 1, NGR - 3, 1, False, False)
            body(2 * NGR - 2, 1, NGR - 2, 0, False, True)
            body(2 * NGR - 1, 1, NGR - 1, 1, True, None)

        def piece(n):
            c, ks = PIECES[n]
            if c == "dt":
                return raw[:, n % 2, 0:KD * 16].rearrange("p (k f) -> p k f", k=KD), dh[:], dl[:]
            return raw[:, n % 2].rearrange("p (k f) -> p k f", k=2), wh[:, PLACE[c], ks], wl[:, PLACE[c], ks]

        def number(p, o, ctx):
            return o + 1 - (SKIPPED[p] if ctx and p else 0)

        def taken(p, o, ctx):
            skipped = sum(1 for q in range(SKIPPED[p]) if DVE_TAKES[p][q] == DVE_TAKES[p][o]) if ctx and p else 0
            return ordinal(p, o) - skipped

        @block.sync
        def _(sp):
            xsrc = io["x"].rearrange("o (t p) d -> (o t) p d", p=P)
            wsrc = io["w_in"].rearrange("o (k p) f -> p (o k) f", p=P)

            def load_x(t, pair):
                for j in range(2):
                    sp.wait_ge(xnorm.sem, xnorm.at(t - 1, j + 1))
                    src = io["ctx"][0, j * P:(j + 1) * P, :] if pair is None else tile_of(xsrc, pair * 2 + j)
                    sp.dma_start(xt[:, j], src).then_inc(x_in.sem(j), 16)

            def load_w(chunk):
                for n, (c, ks) in enumerate(PIECES):
                    if c != chunk:
                        continue
                    if n >= 2:
                        sp.wait_ge(wls.sem, wls.at(n - 2))
                    if c in LEAVES:
                        sp.wait_ge(accd[0].sem, accd[0].at(NGR - 1, LEAVES[c]))
                    c0 = DPROJ - 16 if c == "dt" else COLUMN[c] * 512
                    sp.dma_start(piece(n)[0], wsrc[:, ks, c0:c0 + (16 if c == "dt" else 512)]).then_inc(w_in.sem(n % 2), 16)

            def load_rope(t):
                for j in range(2):
                    sp.wait_ge(edve[0].sem, edve[0].at(t - 1))
                    sp.dma_start(rope[:, j].rearrange("p a b -> p (a b)"), tile_of(io["rope"], t * 2 + j)).then_inc(rope_in.sem(j), 16)

            def store(p, turn, pair, ctx):
                if ctx and p:
                    sp.wait_ge(edve[p].sem, edve[p].at(turn, taken(p, 6, ctx)))
                    sp.wait_ge(eact[p].sem, eact[p].at(turn, taken(p, 8, ctx)))
                else:
                    sp.wait_ge(edve[p].sem, edve[p].at(turn))
                    sp.wait_ge(eact[p].sem, eact[p].at(turn))
                if p:
                    sp.dma_start(dram["ch"][:, :, bass.ds(pair * (2 * P), 2 * P)].rearrange("c p t -> p c t"), ch[:]).then_inc(ch_out.sem(0), 16)
                first = (0, 3 * 512)[p]
                lo, hi = (SKIPPED[p] * 256 if ctx else 0), (3 * 512, 2 * 512 + 16)[p]
                for j in range(2):
                    sp.dma_start(tile_of(dram["tok"], pair * 2 + j, first + lo, first + hi), tok[:, j, lo:hi]).then_inc(tok_out.sem(j), 16)

            for j in range(2):
                sp.sem_inc(tok_out.sem(j), tok_out.credit)
            sp.sem_inc(ch_out.sem(0), ch_out.credit)
            load_x(0, None)
            load_w("k")
            load_rope(0)
            load_w("v")
            load_x(1, 0)
            for c in ("q", "g", "dt"):
                load_w(c)
            store(0, 0, 0, True)
            with sp.Fori(1, NGR - 1) as t:
                load_rope(t)
                load_x(t + 1, t)
                store(0, t, t, False)
            load_rope(NGR - 1)
            load_x(NGR, 0)
            for c in LEAVES:
                load_w(c)
            store(0, NGR - 1, NGR - 1, False)
            with sp.Fori(0, NGR - 2) as t:
                load_x(t + (NGR + 1), t + 1)
                store(1, t, t + 1, False)
            load_x(2 * NGR - 1, None)
            store(1, NGR - 2, NGR - 1, False)
            store(1, NGR - 1, 0, True)
            for j in range(2):
                sp.wait_ge(tok_out.sem(j), tok_out.at(2 * NGR - 1))
            sp.wait_ge(ch_out.sem(0), ch_out.at(NGR - 1))

        @block.gpsimd
        def _(pool):
            with pool.Fori(0, 2 * NGR) as t:
                for j in range(2):
                    pool.wait_ge(ssq.sem, ssq.at(t, j + 1))
                    rstd_root(nc, g, pool, eps_added, t, j + 1, stat[:, j, 1:2], stat[:, j, 0:1], D).then_inc(rstd.sem, 1)

        @block.scalar
        def _(act):
            for p in range(2):
                act.sem_inc(eact[p].sem, eact[p].credit)
            act.sem_inc(hTm.sem, hTm.credit)

            def square(t, j):
                act.wait_ge(x_in.sem(j), x_in.at(t))
                act.wait_ge(xTd.sem, xTd.at(t - 1, j + 1))
                nc.scalar.activation(xn[:, j], xt[:, j], ACT.Square, accum_out=stat[:, j, 0:1]).then_inc(ssq.sem, 1)

            def modulate(t, s, j, ctx):
                act.wait_ge(xTd.sem, xTd.at(t, j + 1))
                act.wait_ge(hTl.sem, hTl.at(t, j) if j else hTl.at(t - 1))
                c = 1 if ctx else 0
                span = slice(j * P, (j + 1) * P)
                for k in range(KD):
                    m = nc.scalar.activation(hraw[:, k], xT[:, k], ACT.Identity,
                                             bias=g["cols"][:, 0, k, c:c + 1], scale=g["cols"][:, 1, k, c:c + 1])
                m.then_inc(hTm.sem, 1)
                act.wait_ge(hTm.sem, hTm.at(t, j + 1))
                nc.scalar.activation(hh[:, s, :, span], hraw[:], ACT.Copy).then_inc(hTh.sem, 1)

            def high(chunk):
                for n, (c, ks) in enumerate(PIECES):
                    if c == chunk:
                        act.wait_ge(w_in.sem(n % 2), w_in.at(n // 2))
                        nc.scalar.activation(piece(n)[1], piece(n)[0], ACT.Copy).then_inc(whs.sem, 1)

            def body(t, p, turn, s, ctx, following):
                if following is not None:
                    for j in range(2):
                        square(t + 1, j)
                for o, (c, j) in enumerate(OUTS[p]):
                    if not (DVE_TAKES[p][o] or ctx and o < SKIPPED[p]):
                        act.wait_ge(accd[p].sem, accd[p].at(turn, number(p, o, ctx)))
                        if c[:2] == "ch":
                            act.wait_ge(ch_out.sem(0), ch_out.at(turn - 1))
                            b = 4 * int(c[2]) + 2 * j
                            m = nc.scalar.activation(ch[:, b:b + 2], acc[:, o % NB].rearrange("p (a b) -> p a b", a=2), ACT.Copy)
                        elif c == "dt":
                            for jj in range(2):
                                act.wait_ge(tok_out.sem(jj), tok_out.at(t - 1))
                            m = nc.scalar.activation(tok[:, :, 1024:1040], acc[:, o % NB, 0:32].rearrange("p (a b) -> p a b", a=2), ACT.Copy)
                        else:
                            act.wait_ge(tok_out.sem(j), tok_out.at(t - 1))
                            at = {"v": 1024, "g": 0, "z": 512}[c]
                            m = nc.scalar.activation(tok[:, j, at:at + 512], acc[:, o % NB], ACT.Copy if c == "v" else ACT.Silu)
                        m.then_inc(eact[p].sem, 1)
                    if following is not None and o in TURN_X[p]:
                        modulate(t + 1, 1 - s, TURN_X[p][o], following)
                if ctx and p == 0:
                    for c in ("q", "g", "dt"):
                        high(c)

            for j in range(2):
                square(0, j)
            for j in range(2):
                modulate(0, 0, j, True)
            high("k")
            high("v")
            turns(act, body, lambda: [high(c) for c in LEAVES])

        @block.tensor
        def _(pe):
            pe.sem_inc(xTd.sem, xTd.credit)
            for p in range(2):
                pe.sem_inc(accd[p].sem, accd[p].credit + (0 if p else SKIPPED[0]))

            def turn_x(t, j):
                pe.wait_ge(xnorm.sem, xnorm.at(t, j + 1))
                pe.wait_ge(hTm.sem, hTm.at(t, j) if j else hTm.at(t - 1, 2))
                for k in range(KD):
                    m = nc.tensor.transpose(xT[:, k], xn[:, j, k * P:(k + 1) * P], g["ident"][:, :])
                m.then_inc(xTd.sem, 1)

            def free(p, turn, o, ctx):
                same = o >= NB and not (ctx and p)
                q = o - NB if same else (o + NB if p and not ctx and o + NB < len(OUTS[p]) else o)
                e = edve[p] if DVE_TAKES[p][q] else eact[p]
                pe.wait_ge(e.sem, e.at(turn, ordinal(p, q)) if same else e.at(turn - 1, ordinal(p, q)))

            def products(t, p, turn, s, ctx, o):
                c, j = OUTS[p][o]
                bank = acc[:, o % NB]
                pe.wait_ge(wls.sem, wls.at(LAST[c]))
                if c[:2] == "ch":
                    for b in range(2):
                        w = slice((2 * j + b) * P, (2 * j + b + 1) * P)
                        for k in range(KD):
                            for n, (a, h) in enumerate(((wh, hh), (wh, hl), (wl, hh))):
                                m = nc.tensor.matmul(bank[:, b * 2 * P:(b + 1) * 2 * P], a[:, PLACE[c], k, w], h[:, s, k], start=(k == 0 and n == 0), stop=(k == KD - 1 and n == 2))
                    return m
                for jj in (range(2) if c == "dt" else (j,)):
                    span = slice(jj * P, (jj + 1) * P)
                    for k in range(KD):
                        for n, (h, high_) in enumerate(((hh, True), (hh, False), (hl, True))):
                            if c == "dt":
                                m = nc.tensor.matmul(bank[:, jj * 16:(jj + 1) * 16], h[:, s, k, span], (dh if high_ else dl)[:, k], start=(k == 0 and n == 0), stop=(k == KD - 1 and n == 2))
                            else:
                                m = nc.tensor.matmul(bank, h[:, s, k, span], (wh if high_ else wl)[:, PLACE[c], k], start=(k == 0 and n == 0), stop=(k == KD - 1 and n == 2))
                return m

            def body(t, p, turn, s, ctx, following):
                pe.wait_ge(hTl.sem, hTl.at(t))
                for o in range(len(OUTS[p])):
                    if not (ctx and o < SKIPPED[p]):
                        free(p, turn, o, ctx)
                        products(t, p, turn, s, ctx, o).then_inc(accd[p].sem, 1)
                    if following is not None and o in TURN_X[p]:
                        turn_x(t + 1, TURN_X[p][o])

            def between():
                pe.wait_ge(edve[0].sem, edve[0].at(NGR - 1))
                pe.wait_ge(eact[0].sem, eact[0].at(NGR - 1))
            for j in range(2):
                turn_x(0, j)
            turns(pe, body, between)

        @block.vector
        def _(dve):
            dve.sem_inc(xnorm.sem, xnorm.credit)
            for p in range(2):
                dve.sem_inc(edve[p].sem, edve[p].credit + (0 if p else SKIPPED[0]))
            dve.sem_inc(rtmp.sem, rtmp.credit)
            dve.sem_inc(hTl.sem, hTl.credit)

            def norm(t, j):
                dve.wait_ge(rstd.sem, rstd.at(t, j + 1))
                nc.vector.tensor_scalar(xn[:, j], xt[:, j], stat[:, j, 1:2], float(D) ** 0.5, ALU.mult, ALU.mult).then_inc(xnorm.sem, 1)

            def low_h(t, s, j):
                dve.wait_ge(hTh.sem, hTh.at(t, j + 1))
                part, high_ = (h[:, s, :, j * P:(j + 1) * P] for h in (hl, hh))
                nc.vector.tensor_tensor(part, hraw[:], high_.bitcast(F32), ALU.subtract).then_inc(hTl.sem, 1)

            def low(chunk):
                for n, (c, ks) in enumerate(PIECES):
                    if c == chunk:
                        whole, high_, low_ = piece(n)
                        dve.wait_ge(whs.sem, whs.at(n))
                        nc.vector.tensor_tensor(low_, whole, high_.bitcast(F32), ALU.subtract).then_inc(wls.sem, 1)

            def turned(t, turn, j, n, o):
                dve.wait_ge(rope_in.sem(j), rope_in.at(turn))
                dve.wait_ge(edve[0].sem, edve[0].at(turn, o) if o else edve[0].at(turn - 1))
                a = acc[:, o % NB].rearrange("p (h e q i) -> p h e q i", h=RH, e=2, q=2)
                sin = rope[:, j, 2 * n + 1].rearrange("p (e q i) -> p e q i", e=2, q=2)
                dve.wait_ge(tok_out.sem(j), tok_out.at(t - 1))
                to = tok[:, j, n * 512:(n + 1) * 512]
                nc.vector.tensor_tensor(to.rearrange("p (h f) -> p h f", h=RH), acc[:, o % NB].rearrange("p (h f) -> p h f", h=RH),
                                        rope[:, j, 2 * n].unsqueeze(1).to_broadcast([P, RH, P]), ALU.mult)
                b = ra[:].rearrange("p (h e q i) -> p h e q i", h=RH, e=2, q=2)
                for q in range(2):
                    m = nc.vector.tensor_tensor(b[:, :, :, q], a[:, :, :, 1 - q], sin[:, :, q].unsqueeze(1).to_broadcast([P, RH, 2, 32]), ALU.mult)
                m.then_inc(rtmp.sem, 1)
                dve.wait_ge(rtmp.sem, turn * 4 + (o + 1))
                nc.vector.tensor_tensor(to, to, ra[:], ALU.add).then_inc(edve[0].sem, 1)

            def body(t, p, turn, s, ctx, following):
                if following is not None:
                    for j in range(2):
                        norm(t + 1, j)
                for o, (c, j) in enumerate(OUTS[p]):
                    if DVE_TAKES[p][o] and not (ctx and o < SKIPPED[p]):
                        dve.wait_ge(accd[p].sem, accd[p].at(turn, number(p, o, ctx)))
                        if p == 0:
                            turned(t, turn, j, o // 2, o)
                        else:
                            dve.wait_ge(ch_out.sem(0), ch_out.at(turn - 1))
                            b = 4 * int(c[2]) + 2 * j
                            nc.vector.tensor_copy(ch[:, b:b + 2], acc[:, o % NB].rearrange("p (a b) -> p a b", a=2)).then_inc(edve[p].sem, 1)
                    if following is not None and o in TURN_X[p]:
                        low_h(t + 1, 1 - s, TURN_X[p][o])
                if ctx and p == 0:
                    for c in ("q", "g", "dt"):
                        low(c)

            for j in range(2):
                norm(0, j)
            for j in range(2):
                low_h(0, 0, j)
            low("k")
            low("v")

            def between():
                for c in LEAVES:
                    low(c)
                dve.wait_ge(wls.sem, wls.at(len(PIECES) - 1))
            turns(dve, body, between)


def convolution(nc, kit, io, g, dram):
    NMOD = 8
    W = CTX + SEQ + 8
    LAT = CTX + 4
    NS = NT * SH
    with ExitStack() as st:
        u = kit.sb("cu", [P, 2, W], stack=st)
        v = kit.sb("cv", [P, 2, W], stack=st)
        cw = kit.sb("cw", [P, CONV, NCH], stack=st)
        cb = kit.sb("cb", [P, NCH], stack=st)
        raw = kit.sb("dt_raw", [P, NT, 2, SH], stack=st)
        bias = kit.sb("dt_bias", [P, 2, SH], stack=st)
        alog = kit.sb("a_log", [P, 2, SH], stack=st)
        y = kit.sb("dt_y", [P, NT, 2, SH], stack=st)
        z = kit.sb("dt_z", [P, NT, 2, SH], stack=st)
        r = kit.sb("dt_r", [P, NT, 2, SH], stack=st)
        dt = kit.sb("dt_dt", [P, NT, 2, SH], stack=st)
        da = kit.sb("dt_da", [P, 2, NT, SH], stack=st)
        rel = kit.sb("rel", [P, 4, P], stack=st)
        relk = kit.sb("relk", [P, 2], stack=st)
        lg = kit.sb("lg", [P, 2, RH], stack=st)
        dec = kit.sb("ret_decay", [P, 2, RH], stack=st)
        lat = kit.sb("c_lat", [P, KD, P], stack=st)
        wm = kit.sb("wm_rest", [P, 2, KD, 512], stack=st)
        bm = kit.sb("bm_rest", [P, NMOD * 512], stack=st)
        nrow = kit.sb("nrow", [P, 3, D], stack=st)
        acc = kit.ps("dt_sums", [P, 2, 512], st)
        rows = kit.ps("mod_rows", [P, 2, 512], st)
        m_in = kit.landing("mod_small_in", dmas=4)
        wm_in = kit.landing("wmod_rest_in", 2)
        spread = kit.counter("c_lat_spread")
        mrow = kit.counter("mod_rest_acc", 1, credit=2)
        mcopy = kit.counter("mod_rest_left", 1, credit=2)
        gained = kit.counter("mod_rest_gained", 8)
        small_in = kit.landing("conv_small_in", dmas=18)
        raw_in = kit.landing("dt_raw_in")
        u_in = kit.landing("conv_in", 2, dmas=2)
        u_out = kit.landing("conv_out", 2, dmas=2, credit=32)
        padded = kit.counter("conv_padded", 6)
        tap = kit.counter("conv_tap", CONV, credit=CONV)
        silu = kit.counter("conv_silu", 1, credit=1)
        dstep = kit.counter("dt_step", 20)
        dact = kit.counter("dt_act", 4)
        sums = kit.counter("dt_sums_ready")
        tabs = kit.counter("decay_tables", 5)
        block = st.enter_context(nc.Block())

        @block.sync
        def _(sp):
            for s in range(2):
                sp.sem_inc(u_out.sem(s), u_out.credit)
            one = small_in.sem(0)
            for k in range(CONV):
                sp.dma_start(cw[:, k], io["ssd_conv_w"][0, k, :].rearrange("(c p) -> p c", p=P), allow_slow_non_contiguous=True).then_inc(one, 16)
            sp.dma_start(cb[:], io["ssd_conv_b"].rearrange("o (c p) -> p (o c)", p=P), allow_slow_non_contiguous=True).then_inc(one, 16)
            for n, d in enumerate("fb"):
                sp.dma_start(bias[:, n], io[f"ssd_dt_bias_{d}"].to_broadcast([P, SH])).then_inc(one, 16)
                sp.dma_start(alog[:, n], io[f"ssd_a_log_{d}"].to_broadcast([P, SH])).then_inc(one, 16)
                sp.dma_start(dec[:, n], io[f"ret_decay_{d}"].to_broadcast([P, RH])).then_inc(one, 16)
            sp.dma_start(g["tri"][:], io["tri"]).then_inc(one, 16)
            sp.dma_start(rel[:], io["rel"]).then_inc(one, 16)
            sp.dma_start(relk[:], io["relk"]).then_inc(one, 16)
            sp.dma_start(g["dskip"][:], io["ssd_d"].to_broadcast([P, SH])).then_inc(one, 16)
            sp.dma_start(g["wn"][:, 0:4], io["ret_gn_w"].rearrange("o (k p) -> p (o k)", p=P), allow_slow_non_contiguous=True).then_inc(one, 16)
            sp.dma_start(g["wn"][:, 4:8], io["ssd_norm_w"].rearrange("o (k p) -> p (o k)", p=P), allow_slow_non_contiguous=True).then_inc(one, 16)
            sp.dma_start(raw[:].rearrange("p t d h -> p t (d h)"), dram["tok"][:, :, 5 * 512:NTOK].rearrange("t p f -> p t f")).then_inc(raw_in.sem(0), 16)
            sp.wait_ge(padded.sem, padded.at(0))

            def load(t, use, s):
                sp.wait_ge(tap.sem, tap.at(t - 2 + 1, 0))
                src = tile_of(dram["ch"], t)
                sp.dma_start(u[:, s, 2:2 + CTX], src[:, 0:CTX]).then_inc(u_in.sem(s), 16)
                sp.dma_start(u[:, s, LAT + 2:LAT + 2 + SEQ], src[:, CTX:CTX + SEQ]).then_inc(u_in.sem(s), 16)

            def store(t, use, s):
                sp.wait_ge(silu.sem, silu.at(t))
                dst = tile_of(dram["u"], t)
                sp.dma_start(dst[:, 0:CTX], v[:, s, 2:2 + CTX]).then_inc(u_out.sem(s), 16)
                sp.dma_start(dst[:, CTX:CTX + SEQ], v[:, s, LAT + 2:LAT + 2 + SEQ]).then_inc(u_out.sem(s), 16)

            for s in range(2):
                src = tile_of(dram["ch"], s)
                sp.dma_start(u[:, s, 2:2 + CTX], src[:, 0:CTX]).then_inc(u_in.sem(s), 16)
                sp.dma_start(u[:, s, LAT + 2:LAT + 2 + SEQ], src[:, CTX:CTX + SEQ]).then_inc(u_in.sem(s), 16)
            with sp.Fori(0, NCH // 2 - 1) as i:
                for s in range(2):
                    store(i * 2 + s, i, s)
                    load(i * 2 + (s + 2), i, s)
            for s in range(2):
                store(NCH - 2 + s, NCH // 2 - 1, s)
                sp.wait_ge(u_out.sem(s), u_out.at(NCH // 2 - 1))

        @block.gpsimd
        def _(pool):
            for s in range(2):
                for a, b in ((0, 2), (CTX + 2, LAT + 2), (W - 2, W)):
                    nc.gpsimd.memset(u[:, s, a:b], 0.0).then_inc(padded.sem, 1)
            for n, src in enumerate(("norm_post_mix", "norm_pre_ffn", "norm_post_ffn")):
                pool.dma_start(nrow[:, n, :], io[src].to_broadcast([P, D])).then_inc(m_in.sem(0), 16)
            pool.dma_start(bm[:], io["b_mod"][:, 4 * 512:].to_broadcast([P, NMOD * 512])).then_inc(m_in.sem(0), 16)
            wsrc = io["w_mod"].rearrange("o (k p) (n f) -> n p (o k) f", p=P, f=512)
            for t in range(NMOD):
                pool.wait_ge(mrow.sem, mrow.at(t - 2))
                pool.dma_start(wm[:, t % 2], wsrc[t + 4]).then_inc(wm_in.sem(t % 2), 16)
            pool.wait_ge(m_in.sem(0), m_in.at(0))
            pool.wait_ge(mcopy.sem, mcopy.at(NMOD - 1))
            root = float(D) ** 0.5
            mod = g["mod"]
            nc.gpsimd.tensor_tensor(mod[:], mod[:], bm[:].rearrange("p (n f) -> p n f", n=4), ALU.add).then_inc(gained.sem, 1)
            pool.wait_ge(gained.sem, 1)
            nc.gpsimd.tensor_scalar(mod[:, 2], mod[:, 2], 1.0, None, ALU.add).then_inc(gained.sem, 1)
            pool.wait_ge(gained.sem, 2)
            for n, row in enumerate((0, 2, 3)):
                nc.gpsimd.tensor_tensor(mod[:, row], mod[:, row], nrow[:, n], ALU.mult).then_inc(gained.sem, 1)
                pool.wait_ge(gained.sem, 3 + n)
                nc.gpsimd.tensor_scalar(mod[:, row], mod[:, row], root, None, ALU.mult)

        @block.tensor
        def _(pe):
            pe.sem_inc(mrow.sem, mrow.credit)
            pe.wait_ge(small_in.sem(0), small_in.at(0))
            pe.wait_ge(dstep.sem, 15)
            for d, tris in enumerate(((0, 1, 4), (2, 3, 4))):
                for n, tri in enumerate(tris):
                    m = nc.tensor.matmul(acc[:, d, n * NS:(n + 1) * NS], g["tri"][:, tri], da[:, d].rearrange("p t h -> p (t h)"), start=True, stop=True)
            m.then_inc(sums.sem, 1)
            pe.wait_ge(spread.sem, spread.at(0))
            for t, use, s in pairs(pe, 0, NMOD):
                pe.wait_ge(wm_in.sem(s), wm_in.at(use))
                pe.wait_ge(mcopy.sem, mcopy.at(t - 2))
                for k in range(KD):
                    m = nc.tensor.matmul(rows[:, s], lat[:, k], wm[:, s, k], start=(k == 0), stop=(k == KD - 1))
                m.then_inc(mrow.sem, 1)

        @block.scalar
        def _(act):
            act.sem_inc(silu.sem, silu.credit)
            act.sem_inc(mcopy.sem, mcopy.credit)
            nc.scalar.activation(lat[:], g["csil"][:, 0, :, None].to_broadcast([P, KD, P]), ACT.Copy).then_inc(spread.sem, 1)
            act.wait_ge(dstep.sem, 1)
            nc.scalar.activation(z[:], y[:], ACT.Abs).then_inc(dact.sem, 1)
            act.wait_ge(dact.sem, 1)
            nc.scalar.activation(r[:], z[:], ACT.Exp, scale=-1.0).then_inc(dact.sem, 1)
            act.wait_ge(small_in.sem(0), small_in.at(0))
            nc.scalar.activation(alog[:], alog[:], ACT.Exp).then_inc(dact.sem, 1)
            nc.scalar.activation(dec[:], dec[:], ACT.Exp).then_inc(dact.sem, 1)
            act.wait_ge(sums.sem, sums.at(0))
            for d in range(2):
                m = nc.scalar.activation(g["E"][:, :, 3 * d:3 * d + 3, :].rearrange("p t k h -> p k t h"),
                                         acc[:, d, 0:3 * NS].rearrange("p (k t h) -> p k t h", k=3, t=NT), ACT.Exp)
            m.then_inc(tabs.sem, 1)
            act.wait_ge(dstep.sem, 21)
            nc.scalar.activation(g["DT"][:], g["DT"][:], ACT.Exp)
            for h in range(RH):
                nc.scalar.activation(g["Dq"][:, 0, h], rel[:, 2], ACT.Exp, scale=lg[:, 0, h:h + 1])
                nc.scalar.activation(g["Dq"][:, 1, h], rel[:, 3], ACT.Exp, scale=lg[:, 1, h:h + 1])
            for d in range(2):
                nc.scalar.activation(g["Dk"][:, d], lg[:, d], ACT.Exp, scale=relk[:, d:d + 1])
                nc.scalar.activation(g["Dtot"][:, d], lg[:, d], ACT.Exp, scale=float(P)).then_inc(tabs.sem, 1)
            with act.Fori(0, NCH // 2) as i:
                for s in range(2):
                    t = i * 2 + s
                    act.wait_ge(tap.sem, tap.at(t))
                    act.wait_ge(u_out.sem(s), i * 32 + 32)
                    nc.scalar.activation(v[:, s, 2:W - 2], v[:, s, 2:W - 2], ACT.Silu).then_inc(silu.sem, 1)
                    act.wait_ge(mrow.sem, mrow.at(t))
                    nc.scalar.activation(g["mod"][:].rearrange("p a b -> p (a b)")[:, bass.ds(t * 512, 512)], rows[:, s], ACT.Copy).then_inc(mcopy.sem, 1)

        @block.vector
        def _(dve):
            dve.sem_inc(tap.sem, tap.credit)
            dve.wait_ge(small_in.sem(0), small_in.at(0))
            dve.wait_ge(raw_in.sem(0), raw_in.at(0))
            count = [0]

            def step(ins):
                count[0] += 1
                ins.then_inc(dstep.sem, 1)
                dve.wait_ge(dstep.sem, count[0])

            step(nc.vector.tensor_tensor(y[:], raw[:], bias[:].unsqueeze(1).to_broadcast([P, NT, 2, SH]), ALU.add))
            dve.wait_ge(dact.sem, 2)
            step(nc.vector.tensor_scalar(z[:], r[:], 2.0, None, ALU.add))
            step(nc.vector.reciprocal(z[:], z[:]))
            step(nc.vector.tensor_tensor(z[:], z[:], r[:], ALU.mult))
            step(nc.vector.tensor_tensor(raw[:], z[:], z[:], ALU.mult))
            step(nc.vector.tensor_scalar(r[:], raw[:], 1.0 / 15, None, ALU.mult))
            for k in range(6, 0, -1):
                step(nc.vector.scalar_tensor_tensor(out=r[:], in0=r[:], scalar=1.0 / (2 * k + 1), in1=raw[:], op0=ALU.add, op1=ALU.mult))
            step(nc.vector.scalar_tensor_tensor(out=r[:], in0=r[:], scalar=1.0, in1=z[:], op0=ALU.add, op1=ALU.mult))
            nc.vector.tensor_scalar(y[:], y[:], 0.0, None, ALU.max)
            dve.wait_ge(dact.sem, 4)
            step(nc.vector.tensor_scalar(alog[:], alog[:], -1.0, None, ALU.mult))
            dve.wait_ge(dstep.sem, count[0])
            nc.vector.scalar_tensor_tensor(out=dt[:], in0=r[:], scalar=2.0, in1=y[:], op0=ALU.mult, op1=ALU.add).then_inc(tabs.sem, 1)
            dve.wait_ge(tabs.sem, 1)
            step(nc.vector.tensor_tensor(da[:].rearrange("p d t h -> p t d h"), dt[:], alog[:].unsqueeze(1).to_broadcast([P, NT, 2, SH]), ALU.mult))
            dd = g["dd"]
            nc.vector.tensor_tensor(dd[:, :, 0], dt[:, :, 0], dt[:, :, 1], ALU.subtract)
            nc.vector.tensor_copy(dd[:, :, 1], dt[:, :, 1])
            nc.vector.tensor_copy(dd[:, :, 2:4], da[:].rearrange("p d t h -> p t d h"))
            step(nc.vector.tensor_scalar(lg[:], dec[:], -1.0, None, ALU.mult))
            for h in range(RH):
                step(nc.vector.tensor_scalar(g["DT"][:, h], rel[:, 1], lg[:, 1, h:h + 1], None, ALU.mult))
            for h in range(RH):
                last = nc.vector.scalar_tensor_tensor(out=g["DT"][:, h], in0=rel[:, 0], scalar=lg[:, 0, h:h + 1], in1=g["DT"][:, h], op0=ALU.mult, op1=ALU.add)
            step(last)
            dve.wait_ge(tabs.sem, 2)
            for d in range(2):
                w = g["E"][:, :, 3 * d + 1, :]
                m = nc.vector.tensor_tensor(w, w, dt[:, :, d], ALU.mult)
            m.then_inc(tabs.sem, 1)
            with dve.Fori(0, NCH // 2) as i:
                for s in range(2):
                    t = i * 2 + s
                    dve.wait_ge(u_in.sem(s), u_in.at(i))
                    dve.wait_ge(u_out.sem(s), i * 32 + 32)
                    n = W - 4
                    for k in range(CONV):
                        wk = conv_w(cw, t, k)
                        if k == 0:
                            nc.vector.tensor_scalar(v[:, s, 2:2 + n], u[:, s, 0:n], wk, conv_w(cb, t, None), ALU.mult, ALU.add).then_inc(tap.sem, 1)
                        else:
                            dve.wait_ge(tap.sem, tap.at(t, k))
                            nc.vector.scalar_tensor_tensor(out=v[:, s, 2:2 + n], in0=u[:, s, k:k + n], scalar=wk, in1=v[:, s, 2:2 + n], op0=ALU.mult, op1=ALU.add).then_inc(tap.sem, 1)


def conv_w(w, t, k):
    if k is None:
        return w[:, bass.ds(t, 1)]
    return w[:, k, bass.ds(t, 1)]


def heads(v, n):
    return v.unsqueeze(2).to_broadcast([P, v.shape[1], n])


def tile_row(t4, t, k):
    return t4[:, bass.ds(t, 1), k, :].rearrange("p o h -> p (o h)")


def states(nc, kit, io, g, dram):
    TURNS = NT + NCT
    with ExitStack() as st:
        kv = kit.sb("s_kv", [P, 2, D], stack=st)
        uc = kit.sb("s_u", [P, 2, 6, P], stack=st)
        kd = kit.sb("s_kd", [P, 2, 512], stack=st)
        xw = kit.sb("s_xw", [P, 2, 512], stack=st)
        bt = kit.sb("s_bt", [P, 2, SG * P], stack=st)
        sb = kit.sb("s_sb", [P, 2, 2, 512], stack=st)
        sd = kit.sb("s_sd", [P, 2, 512], stack=st)
        xT = kit.ps("s_xT", [P, 2, 512], st)
        bT = kit.ps("s_bT", [P, 2, 512], st)
        up = kit.ps("s_up", [P, 2, 2, 512], st)
        kv_in = kit.landing("s_kv_in", 2)
        u_in = kit.landing("s_u_in", 2)
        s_out = kit.landing("s_out", 2)
        turned = kit.counter("s_transposed", 2, credit=4)
        bts = kit.counter("s_b_ready", 1, credit=2)
        kds = kit.counter("s_k_decayed", 1, credit=2)
        xws = kit.counter("s_x_weighted", 1, credit=2)
        dec = kit.counter("s_decayed", 2, credit=4)
        ups = kit.counter("s_update_ready", 1, credit=2)
        news = kit.counter("s_state_ready", 2, credit=4)
        zero = kit.counter("s_zero")
        block = st.enter_context(nc.Block())

        def turns(eng, body):
            for t in range(NCT):
                body(t, t // 2, t % 2, NCT - 1 - t, True, sb, False)
            with eng.Fori(0, NL // 2) as i:
                for s in range(2):
                    t = i * 2 + (NCT + s)
                    body(t, i + 1, s, i * -2 + (NT - 1 - s), True, sb, True)
            for t in range(NT, TURNS):
                body(t, t // 2, t % 2, t - NT, False, g["sf"], False)

        @block.sync
        def _(sp):
            def load(t, use, s, tile, back, state, stored):
                sp.wait_ge(ups.sem, ups.at(t - 2))
                sp.wait_ge(kds.sem, kds.at(t - 2))
                sp.dma_start(kv[:, s], tile_of(dram["tok"], tile, 512, 3 * 512)).then_inc(kv_in.sem(s), 16)
                sp.wait_ge(turned.sem, turned.at(t - 2))
                sp.dma_start(uc[:, s], dram["u"][0:6, :, bass.ds(tile * P, P)].rearrange("c p t -> p c t")).then_inc(u_in.sem(s), 16)
            turns(sp, load)

        @block.gpsimd
        def _(pool):
            pool.sem_inc(kds.sem, kds.credit)
            pool.sem_inc(dec.sem, dec.credit)
            nc.gpsimd.memset(sb[:, 0], 0.0)
            nc.gpsimd.memset(g["sf"][:, 0], 0.0).then_inc(zero.sem, 1)
            pool.wait_ge(zero.sem, zero.at(0))

            def body(t, use, s, tile, back, state, stored):
                pool.wait_ge(kv_in.sem(s), kv_in.at(use))
                pool.wait_ge(ups.sem, ups.at(t - 2))
                nc.gpsimd.tensor_tensor(kd[:, s].rearrange("p (h e) -> p h e", h=RH), kv[:, s, 0:512].rearrange("p (h e) -> p h e", h=RH),
                                                heads(g["Dk"][:, int(back)], P), ALU.mult).then_inc(kds.sem, 1)
                pool.wait_ge(news.sem, news.at(t - 1))
                nc.gpsimd.tensor_tensor(sd[:, 0].rearrange("p (h e) -> p h e", h=RH), state[:, s, 0].rearrange("p (h e) -> p h e", h=RH),
                                                heads(g["Dtot"][:, int(back)], P), ALU.mult).then_inc(dec.sem, 1)
                nc.gpsimd.tensor_tensor(sd[:, 1].rearrange("p (h e) -> p h e", h=SH), state[:, s, 1].rearrange("p (h e) -> p h e", h=SH),
                                                heads(tile_row(g["E"], tile, 5 if back else 2), SP_), ALU.mult).then_inc(dec.sem, 1)
            turns(pool, body)

        @block.tensor
        def _(pe):
            pe.sem_inc(turned.sem, turned.credit)
            pe.sem_inc(ups.sem, ups.credit)

            def body(t, use, s, tile, back, state, stored):
                pe.wait_ge(u_in.sem(s), u_in.at(use))
                pe.wait_ge(xws.sem, xws.at(t - 2))
                for c in range(4):
                    m = nc.tensor.transpose(xT[:, s, c * P:(c + 1) * P], uc[:, s, c], g["ident"][:, :])
                m.then_inc(turned.sem, 1)
                pe.wait_ge(bts.sem, bts.at(t - 2))
                for c in range(SG):
                    m = nc.tensor.transpose(bT[:, s, c * P:(c + 1) * P], uc[:, s, 4 + c], g["ident"][:, :])
                m.then_inc(turned.sem, 1)
                pe.wait_ge(kds.sem, kds.at(t))
                pe.wait_ge(news.sem, news.at(t - 2))
                for h in range(RH):
                    nc.tensor.matmul(up[:, s, 0, h * P:(h + 1) * P], kd[:, s, h * P:(h + 1) * P], kv[:, s, 512 + h * P:512 + (h + 1) * P], start=True, stop=True)
                pe.wait_ge(xws.sem, xws.at(t))
                pe.wait_ge(bts.sem, bts.at(t))
                for c in range(SG):
                    m = nc.tensor.matmul(up[:, s, 1, c * 256:(c + 1) * 256], bt[:, s, c * P:(c + 1) * P], xw[:, s, c * 256:(c + 1) * 256], start=True, stop=True)
                m.then_inc(ups.sem, 1)
            turns(pe, body)

        @block.scalar
        def _(act):
            act.sem_inc(bts.sem, bts.credit)

            def body(t, use, s, tile, back, state, stored):
                if stored:
                    act.wait_ge(news.sem, news.at(t - 1))
                    act.dma_start(tile_of(dram["sb"], tile), state[:, s].rearrange("p a b -> p (a b)")).then_inc(s_out.sem(s), 16)
                act.wait_ge(turned.sem, turned.at(t, 2))
                act.wait_ge(ups.sem, ups.at(t - 2))
                nc.scalar.activation(bt[:, s], bT[:, s, 0:SG * P], ACT.Copy).then_inc(bts.sem, 1)
            turns(act, body)
            for s in range(2):
                act.wait_ge(s_out.sem(s), 16 * NL // 2)

        @block.vector
        def _(dve):
            dve.sem_inc(xws.sem, xws.credit)
            dve.sem_inc(news.sem, news.credit)

            def body(t, use, s, tile, back, state, stored):
                dve.wait_ge(turned.sem, turned.at(t, 1))
                dve.wait_ge(ups.sem, ups.at(t - 2))
                nc.vector.tensor_tensor(xw[:, s].rearrange("p (h e) -> p h e", h=SH), xT[:, s].rearrange("p (h e) -> p h e", h=SH),
                                                heads(tile_row(g["E"], tile, 4 if back else 1), SP_), ALU.mult).then_inc(xws.sem, 1)
                dve.wait_ge(dec.sem, dec.at(t))
                dve.wait_ge(ups.sem, ups.at(t))
                if stored:
                    dve.wait_ge(s_out.sem(1 - s), s_out.at(use - 1 if s else use - 2))
                for n in range(2):
                    nc.vector.tensor_tensor(state[:, 1 - s, n], sd[:, n], up[:, s, n], ALU.add).then_inc(news.sem, 1)
            turns(dve, body)


def mixing(nc, kit, io, g, dram):
    with ExitStack() as st:
        tok = kit.sb("m_tok", [P, 2, 5 * 512], stack=st)
        uc = kit.sb("m_u", [P, 2, NCH, P], stack=st)
        sb = kit.sb("m_sb", [P, 2, 2, 512], stack=st)
        qk = kit.sb("m_qk", [P, 2, 512], stack=st)
        qd = kit.sb("m_qd", [P, 2, 512], stack=st)
        xs = kit.sb("m_xs", [P, 512], stack=st)
        bt = kit.sb("m_bt", [P, SG * P], stack=st)
        kd = kit.sb("m_kd", [P, 512], stack=st)
        xw = kit.sb("m_xw", [P, 512], stack=st)
        dav = kit.sb("m_dav", [P, 2, SH * P], stack=st)
        sT = kit.sb("m_sT", [P, 512], stack=st)
        L = kit.sb("m_L", [P, SH, P], stack=st)
        G = kit.sb("m_G", [P, SH, P], stack=st)
        sd = kit.sb("m_sd", [P, 2, 512], stack=st)
        xd = kit.sb("m_xd", [P, 512], stack=st)
        t1 = kit.sb("m_t1", [P, 512], stack=st)
        t2 = kit.sb("m_t2", [P, 512], stack=st)
        t3 = kit.sb("m_t3", [P, 512], stack=st)
        yr = kit.sb("m_yr", [P, 512], stack=st)
        bn = kit.sb("m_bn", [P, RH, 6], stack=st)
        mv = kit.sb("m_mv", [P, RH, 2], stack=st)
        rs = kit.sb("m_rs", [P, 8], stack=st)
        sq = kit.sb("m_sq", [P, 512], stack=st)
        yc = kit.sb("m_y", [P, 2, D], stack=st)
        bank = kit.ps("m_bank", [P, 8, 512], st)
        tok_in = kit.landing("m_tok_in", 2)
        u_in = kit.landing("m_u_in", 2)
        sb_in = kit.landing("m_sb_in", 2)
        y_out = kit.landing("m_y_out", 2, credit=16)
        turned = kit.counter("m_transposed", 4, credit=4)
        left = kit.counter("m_transposed_copied", 4, credit=4)
        qdec = kit.counter("m_q_decayed", 2, credit=2)
        davs = kit.counter("m_da_spread", 2, credit=2)
        kds = kit.counter("m_k_decayed", 1, credit=1)
        xws = kit.counter("m_x_weighted", 1, credit=1)
        prod = kit.counter("m_products", 3, credit=3)
        exps = kit.counter("m_decays_exp", 1, credit=1)
        sTs = kit.counter("m_scores_decayed", 1, credit=1)
        gate = kit.counter("m_steps_spread", 3, credit=3)
        yret = kit.counter("m_y_ret", 1, credit=1)
        yssd = kit.counter("m_y_ssd", 2, credit=2)
        ups = kit.counter("m_update_ready", 1, credit=1)
        dec = kit.counter("m_state_decayed", 2, credit=2)
        news = kit.counter("m_state_ready", 2, credit=2)
        skip = kit.counter("m_skip_ready", 1, credit=1)
        stats = kit.counter("m_head_stats", 2)
        rstd = kit.counter("m_rstd", 2)
        eps_added = kit.counter("m_eps_added", 2)
        yrs = kit.counter("m_ret_normed", 2, credit=2)
        ysum = kit.counter("m_ssd_summed", 5, credit=5)
        ssq = kit.counter("m_ssd_ssq", 1, credit=1)
        gated = kit.counter("m_ssd_gated", 2, credit=2)
        yssdn = kit.counter("m_ssd_normed", 1, credit=1)
        w_out_in = kit.landing("w_out_in", dmas=KD)
        block = st.enter_context(nc.Block())

        def turns(eng, body):
            for t, use, s in pairs(eng, 0, NL):
                body(t, use, s, use * 2 + (s + NCT))

        def by(v, n):
            return v.rearrange("p (h e) -> p h e", h=n)

        @block.sync
        def _(sp):
            for s in range(2):
                sp.sem_inc(y_out.sem(s), y_out.credit)

            def load(t, use, s, tile):
                sp.wait_ge(ups.sem, ups.at(t - 2 + 1, 0))
                sp.wait_ge(yssd.sem, yssd.at(t - 2 + 1, 0))
                sp.wait_ge(gated.sem, gated.at(t - 2 + 1, 0))
                sp.wait_ge(yrs.sem, yrs.at(t - 2 + 1, 0))
                issue(t, use, s, tile)

            def issue(t, use, s, tile):
                sp.dma_start(uc[:, s], dram["u"][:, :, bass.ds(tile * P, P)].rearrange("c p t -> p c t")).then_inc(u_in.sem(s), 16)
                sp.dma_start(tok[:, s], tile_of(dram["tok"], tile, 0, 5 * 512)).then_inc(tok_in.sem(s), 16)
                sp.dma_start(sb[:, s].rearrange("p a b -> p (a b)"), tile_of(dram["sb"], tile)).then_inc(sb_in.sem(s), 16)

            for s in range(2):
                issue(s, 0, s, NCT + s)
            for k in range(KD):
                sp.dma_start(g["w_out"][:, k], io["w_out"][0, k * P:(k + 1) * P, :]).then_inc(w_out_in.sem(0), 16)
            with sp.Fori(0, NL // 2 - 1) as i:
                for s in range(2):
                    t = i * 2 + (2 + s)
                    load(t, i + 1, s, t + NCT)
            sp.wait_ge(w_out_in.sem(0), w_out_in.at(0))

        @block.gpsimd
        def _(pool):
            for x in (davs, kds, dec, skip, gated):
                pool.sem_inc(x.sem, x.credit)

            def body(t, use, s, tile):
                pool.wait_ge(prod.sem, prod.at(t - 1))
                for d in range(2):
                    nc.gpsimd.tensor_tensor(by(dav[:, d], SH), g["tri"][:, 2 * d].unsqueeze(1).to_broadcast([P, SH, P]),
                                                     heads(tile_row(g["dd"], tile, 2 + d), P), ALU.mult).then_inc(davs.sem, 1)
                pool.wait_ge(tok_in.sem(s), tok_in.at(use))
                pool.wait_ge(ups.sem, ups.at(t - 1))
                nc.gpsimd.tensor_tensor(by(kd[:], RH), by(tok[:, s, 512:1024], RH), heads(g["Dk"][:, 0], P), ALU.mult).then_inc(kds.sem, 1)
                pool.wait_ge(news.sem, news.at(t - 1))
                nc.gpsimd.tensor_tensor(by(sd[:, 0], RH), by(g["sf"][:, s, 0], RH), heads(g["Dtot"][:, 0], P), ALU.mult).then_inc(dec.sem, 1)
                nc.gpsimd.tensor_tensor(by(sd[:, 1], SH), by(g["sf"][:, s, 1], SH), heads(tile_row(g["E"], tile, 2), SP_), ALU.mult).then_inc(dec.sem, 1)
                pool.wait_ge(left.sem, left.at(t, 3))
                pool.wait_ge(ysum.sem, ysum.at(t - 1))
                nc.gpsimd.tensor_tensor(by(xd[:], SH), by(xs[:], SH), heads(g["dskip"][:], SP_), ALU.mult).then_inc(skip.sem, 1)
                pool.wait_ge(stats.sem, stats.at(t))
                rstd_root(nc, g, pool, eps_added, t, 1, rs[:, 0:4], mv[:, :, 1], 1).then_inc(rstd.sem, 1)
                pool.wait_ge(ysum.sem, ysum.at(t, 5))
                pool.wait_ge(yssdn.sem, yssdn.at(t - 1))
                nc.gpsimd.tensor_tensor(t1[:], t3[:], tok[:, s, 4 * 512:5 * 512], ALU.mult).then_inc(gated.sem, 1)
                pool.wait_ge(yrs.sem, yrs.at(t, 2))
                pool.wait_ge(y_out.sem(s), y_out.at(use - 1))
                nc.gpsimd.tensor_tensor(yc[:, s, 0:512], yr[:], tok[:, s, 3 * 512:4 * 512], ALU.mult).then_inc(gated.sem, 1)
                pool.wait_ge(ssq.sem, ssq.at(t))
                rstd_root(nc, g, pool, eps_added, t, 2, rs[:, 5:6], rs[:, 4:5], 512).then_inc(rstd.sem, 1)
            turns(pool, body)

        @block.tensor
        def _(pe):
            for x in (turned, prod, yret, yssd, ups):
                pe.sem_inc(x.sem, x.credit)

            def body(t, use, s, tile):
                ident = g["ident"][:, :]
                pe.wait_ge(tok_in.sem(s), tok_in.at(use))
                pe.wait_ge(yrs.sem, yrs.at(t - 1))
                for n in range(2):
                    if n:
                        pe.wait_ge(ysum.sem, ysum.at(t - 1))
                    for h in range(RH):
                        m = nc.tensor.transpose(bank[:, n, h * P:(h + 1) * P], tok[:, s, n * 512 + h * P:n * 512 + (h + 1) * P], ident)
                    m.then_inc(turned.sem, 1)
                pe.wait_ge(u_in.sem(s), u_in.at(use))
                for c in range(4):
                    m = nc.tensor.transpose(bank[:, 2, c * P:(c + 1) * P], uc[:, s, c], ident)
                m.then_inc(turned.sem, 1)
                pe.wait_ge(news.sem, news.at(t - 1))
                for c in range(SG):
                    m = nc.tensor.transpose(bank[:, 3, c * P:(c + 1) * P], uc[:, s, 4 + c], ident)
                m.then_inc(turned.sem, 1)
                pe.wait_ge(davs.sem, davs.at(t))
                pe.wait_ge(exps.sem, exps.at(t - 1))
                for half in range(2):
                    for d in range(2):
                        m = nc.tensor.matmul(bank[:, 5 + half], g["tri"][:, 1 + 2 * d], dav[:, d, half * 512:(half + 1) * 512], start=(d == 0), stop=(d == 1))
                m.then_inc(prod.sem, 1)
                pe.wait_ge(left.sem, left.at(t, 2))
                for h in range(RH):
                    m = nc.tensor.matmul(bank[:, 4, h * P:(h + 1) * P], qk[:, 1, h * P:(h + 1) * P], qk[:, 0, h * P:(h + 1) * P], start=True, stop=True)
                m.then_inc(prod.sem, 1)
                for c in range(SG):
                    m = nc.tensor.matmul(bank[:, 7, c * P:(c + 1) * P], uc[:, s, 4 + c], uc[:, s, 6 + c], start=True, stop=True)
                m.then_inc(prod.sem, 1)
                pe.wait_ge(sTs.sem, sTs.at(t))
                pe.wait_ge(qdec.sem, qdec.at(t))
                pe.wait_ge(sb_in.sem(s), sb_in.at(use))
                for h in range(RH):
                    e = slice(h * P, (h + 1) * P)
                    nc.tensor.matmul(bank[:, 0, e], sT[:, e], tok[:, s, 1024 + h * P:1024 + (h + 1) * P], start=True, stop=False)
                    nc.tensor.matmul(bank[:, 0, e], qd[:, 0, e], g["sf"][:, s, 0, e], start=False, stop=False)
                    m = nc.tensor.matmul(bank[:, 0, e], qd[:, 1, e], sb[:, s, 0, e], start=False, stop=True)
                m.then_inc(yret.sem, 1)
                pe.wait_ge(kds.sem, kds.at(t))
                for h in range(RH):
                    e = slice(h * P, (h + 1) * P)
                    nc.tensor.matmul(bank[:, 4, e], kd[:, e], tok[:, s, 1024 + h * P:1024 + (h + 1) * P], start=True, stop=True)
                pe.wait_ge(left.sem, left.at(t, 4))
                pe.wait_ge(xws.sem, xws.at(t))
                for c in range(SG):
                    m = nc.tensor.matmul(bank[:, 3, c * 256:(c + 1) * 256], bt[:, c * P:(c + 1) * P], xw[:, c * 256:(c + 1) * 256], start=True, stop=True)
                m.then_inc(ups.sem, 1)
                pe.wait_ge(gate.sem, gate.at(t))
                for n, state in ((2, g["sf"][:, s, 1]), (7, sb[:, s, 1])):
                    for c in range(SG):
                        m = nc.tensor.matmul(bank[:, n, c * 256:(c + 1) * 256], uc[:, s, 6 + c], state[:, c * 256:(c + 1) * 256], start=True, stop=True)
                m.then_inc(yssd.sem, 1)
                for h in range(SH):
                    m = nc.tensor.matmul(bank[:, 1, h * SP_:(h + 1) * SP_], L[:, h], xs[:, h * SP_:(h + 1) * SP_], start=True, stop=True)
                m.then_inc(yssd.sem, 1)
            turns(pe, body)

        @block.scalar
        def _(act):
            for x in (left, exps, ssq):
                act.sem_inc(x.sem, x.credit)

            def body(t, use, s, tile):
                act.wait_ge(turned.sem, turned.at(t, 1))
                act.wait_ge(prod.sem, prod.at(t - 1))
                act.wait_ge(qdec.sem, qdec.at(t - 1))
                nc.scalar.activation(qk[:, 0], bank[:, 0], ACT.Copy).then_inc(left.sem, 1)
                act.wait_ge(turned.sem, turned.at(t, 2))
                nc.scalar.activation(qk[:, 1], bank[:, 1], ACT.Copy).then_inc(left.sem, 1)
                act.wait_ge(turned.sem, turned.at(t, 3))
                act.wait_ge(yssd.sem, yssd.at(t - 1))
                act.wait_ge(skip.sem, skip.at(t - 1))
                nc.scalar.activation(xs[:], bank[:, 2], ACT.Copy).then_inc(left.sem, 1)
                act.wait_ge(turned.sem, turned.at(t, 4))
                act.wait_ge(ups.sem, ups.at(t - 1))
                nc.scalar.activation(bt[:], bank[:, 3, 0:SG * P], ACT.Copy).then_inc(left.sem, 1)
                act.wait_ge(prod.sem, prod.at(t, 1))
                nc.scalar.activation(L[:].rearrange("p h n -> p (h n)"), bank[:, 5:7].rearrange("p a b -> p (a b)"), ACT.Exp).then_inc(exps.sem, 1)
                act.wait_ge(gated.sem, gated.at(t, 1))
                nc.scalar.activation(sq[:], t1[:], ACT.Square, accum_out=rs[:, 4:5]).then_inc(ssq.sem, 1)
                act.wait_ge(gated.sem, gated.at(t, 2))
                act.wait_ge(yssdn.sem, yssdn.at(t))
                act.dma_start(tile_of(dram["y"], tile), yc[:, s]).then_inc(y_out.sem(s), 16)
            turns(act, body)
            for s in range(2):
                act.wait_ge(y_out.sem(s), y_out.at(NL // 2 - 1))

        @block.vector
        def _(dve):
            for x in (qdec, xws, sTs, gate, news, yrs, ysum, yssdn):
                dve.sem_inc(x.sem, x.credit)

            def body(t, use, s, tile):
                dve.wait_ge(left.sem, left.at(t, 1))
                dve.wait_ge(yret.sem, yret.at(t - 1))
                for d in range(2):
                    nc.vector.tensor_tensor(qd[:, d], qk[:, 0], g["Dq"][:, d].rearrange("p h n -> p (h n)"), ALU.mult).then_inc(qdec.sem, 1)
                dve.wait_ge(left.sem, left.at(t, 3))
                dve.wait_ge(ups.sem, ups.at(t - 1))
                nc.vector.tensor_tensor(by(xw[:], SH), by(xs[:], SH), heads(tile_row(g["E"], tile, 1), SP_), ALU.mult).then_inc(xws.sem, 1)
                for h in range(SH):
                    m = nc.vector.tensor_scalar(G[:, h], g["tri"][:, 0], g["dd"][:, bass.ds(tile, 1), 0, h:h + 1].rearrange("p a b -> p (a b)"),
                                                g["dd"][:, bass.ds(tile, 1), 1, h:h + 1].rearrange("p a b -> p (a b)"), ALU.mult, ALU.add)
                m.then_inc(gate.sem, 1)
                dve.wait_ge(prod.sem, prod.at(t, 2))
                nc.vector.tensor_tensor(sT[:], bank[:, 4], g["DT"][:].rearrange("p h n -> p (h n)"), ALU.mult).then_inc(sTs.sem, 1)
                dve.wait_ge(gate.sem, gate.at(t, 1))
                dve.wait_ge(exps.sem, exps.at(t))
                nc.vector.tensor_tensor(L[:], L[:], G[:], ALU.mult).then_inc(gate.sem, 1)
                dve.wait_ge(gate.sem, gate.at(t, 2))
                dve.wait_ge(prod.sem, prod.at(t, 3))
                nc.vector.tensor_tensor(L[:].rearrange("p (c r) n -> p c r n", c=SG), L[:].rearrange("p (c r) n -> p c r n", c=SG),
                                                 bank[:, 7, 0:SG * P].rearrange("p (c n) -> p c n", c=SG).unsqueeze(2).to_broadcast([P, SG, SH // SG, P]), ALU.mult).then_inc(gate.sem, 1)
                dve.wait_ge(yret.sem, yret.at(t))
                for h in range(RH):
                    m = nc.vector.bn_stats(bn[:, h], bank[:, 0, h * P:(h + 1) * P])
                m.then_inc(stats.sem, 1)
                dve.wait_ge(stats.sem, stats.at(t, 1))
                dve.wait_ge(ups.sem, ups.at(t))
                dve.wait_ge(dec.sem, dec.at(t))
                for n, b in ((0, 4), (1, 3)):
                    nc.vector.tensor_tensor(g["sf"][:, 1 - s, n], sd[:, n], bank[:, b], ALU.add).then_inc(news.sem, 1)
                for h in range(RH):
                    m = nc.vector.bn_aggr(mv[:, h], bn[:, h])
                m.then_inc(stats.sem, 1)
                dve.wait_ge(rstd.sem, rstd.at(t, 1))
                dve.wait_ge(gated.sem, gated.at(t - 1))
                for h in range(RH):
                    m = nc.vector.tensor_scalar(yr[:, h * P:(h + 1) * P], bank[:, 0, h * P:(h + 1) * P], mv[:, h, 0:1], rs[:, h:h + 1], ALU.subtract, ALU.mult)
                    if h % 2:
                        m.then_inc(yrs.sem, 1)
                dve.wait_ge(yssd.sem, yssd.at(t, 2))
                dve.wait_ge(gated.sem, gated.at(t - 1))
                nc.vector.tensor_tensor(by(t3[:], SH), by(bank[:, 2], SH), heads(tile_row(g["E"], tile, 0), SP_), ALU.mult).then_inc(ysum.sem, 1)
                nc.vector.tensor_tensor(by(t2[:], SH), by(bank[:, 7], SH), heads(tile_row(g["E"], tile, 3), SP_), ALU.mult).then_inc(ysum.sem, 1)
                dve.wait_ge(ysum.sem, ysum.at(t, 1))
                nc.vector.tensor_tensor(t3[:], t3[:], bank[:, 1], ALU.add).then_inc(ysum.sem, 1)
                dve.wait_ge(ysum.sem, ysum.at(t, 3))
                dve.wait_ge(skip.sem, skip.at(t))
                nc.vector.tensor_tensor(t2[:], t2[:], xd[:], ALU.add).then_inc(ysum.sem, 1)
                dve.wait_ge(ysum.sem, ysum.at(t, 4))
                nc.vector.tensor_tensor(t3[:], t3[:], t2[:], ALU.add).then_inc(ysum.sem, 1)
                dve.wait_ge(rstd.sem, rstd.at(t, 2))
                dve.wait_ge(y_out.sem(s), y_out.at(use - 1))
                nc.vector.tensor_scalar(yc[:, s, 512:D], t1[:], rs[:, 5:6], 512.0 ** 0.5, ALU.mult, ALU.mult).then_inc(yssdn.sem, 1)
            turns(dve, body)


def residual(nc, kit, io, g, dram):
    with ExitStack() as st:
        w = g["w_out"]
        wh = kit.sb("r_w_high", [P, KD, D], F32R, stack=st)
        wl = kit.sb("r_w_low", [P, KD, D], F32R, stack=st)
        wr = kit.sb("r_wr", [P, KD, NG + NE], stack=st)
        br = kit.sb("r_br", [P, NG + NE], stack=st)
        y = kit.sb("r_y", [P, 2, D], stack=st)
        x = kit.sb("r_x", [P, 2, D], stack=st)
        yT = kit.sb("r_yT", [P, 2, 2, KD, P], F32R, stack=st)
        hT = kit.sb("r_hT", [P, 2, KD, P], stack=st)
        sq = kit.sb("r_sq", [P, D], stack=st)
        ss = kit.sb("r_ss", [P, 4], stack=st)
        yn = kit.sb("r_yn", [P, D], stack=st)
        x1 = kit.sb("r_x1", [P, 2, D], stack=st)
        h2 = kit.sb("r_h2", [P, 2, D], stack=st)
        pT = kit.ps("r_pT", [P, KD, P], st)
        py = kit.ps("r_py", [P, 2, 2, 512], st)
        pl = kit.ps("r_pl", [P, 512], st)
        w_l = kit.landing("r_w_in", dmas=NG + 3)
        y_in = kit.landing("r_y_in", 2)
        x_in = kit.landing("r_x_in", 2)
        x1_out = kit.landing("r_x1_out", 2, credit=16)
        h2_out = kit.landing("r_h2_out", 2, credit=16)
        wsc = kit.counter("r_w_scaled")
        whs = kit.counter("r_w_high_ready")
        wls = kit.counter("r_w_low_ready")
        yTt = kit.counter("r_y_transposed")
        yTh = kit.counter("r_yT_high_ready")
        yTl = kit.counter("r_yT_low_ready")
        prod = kit.counter("r_product")
        ssq_y = kit.counter("r_ssq_y")
        ssq_x = kit.counter("r_ssq_x1")
        eps_y = kit.counter("r_eps_added_y")
        eps_x = kit.counter("r_eps_added_x1")
        rstd_y = kit.counter("r_rstd_y")
        rstd_x = kit.counter("r_rstd_x1")
        yns = kit.counter("r_y_normed")
        x1s = kit.counter("r_x1_ready")
        h2m = kit.counter("r_h2_scaled")
        h2s = kit.counter("r_h2_ready")
        hTt = kit.counter("r_h_transposed", credit=1)
        hTs = kit.counter("r_hT_ready")
        lgp = kit.counter("r_logits_product", credit=1)
        lgs = kit.counter("r_logits_ready", credit=1)
        block = st.enter_context(nc.Block())

        def turns(eng, body):
            for t in (-1, 0, 1):
                body(t, t // 2, t % 2)
            with eng.Fori(0, NL // 2 - 2) as i:
                for s in range(2):
                    body(i * 2 + (2 + s), i + 1, s)
            for t in range(NL - 2, NL + 2):
                body(t, t // 2, t % 2)

        def there(t):
            return not isinstance(t, int) or 0 <= t < NL

        @block.sync
        def _(sp):
            for s in range(2):
                sp.sem_inc(x1_out.sem(s), 16)
                sp.sem_inc(h2_out.sem(s), 16)

            def load_y(t, use, s):
                sp.dma_start(y[:, s], tile_of(dram["y"], t + NCT)).then_inc(y_in.sem(s), 16)

            def load_x(t, use, s):
                sp.dma_start(x[:, s], tile_of(io["x"].rearrange("o (t p) d -> (o t) p d", p=P), t)).then_inc(x_in.sem(s), 16)
            for t in range(2):
                load_y(t, 0, t)
                load_x(t, 0, t)
            one = w_l.sem(0)
            sp.dma_start(wr[:, :, 0:NG], io["moe_w_rg"].rearrange("o (k p) n -> p (o k) n", p=P)).then_inc(one, 16)
            for n in range(NG):
                sp.dma_start(wr[:, :, NG + n * EPG:NG + (n + 1) * EPG], io["moe_w_re"][0, n].rearrange("(k p) e -> p k e", p=P)).then_inc(one, 16)
            sp.dma_start(br[:, 0:NG], io["moe_b_rg"].to_broadcast([P, NG])).then_inc(one, 16)
            sp.dma_start(br[:, NG:NG + NE], io["moe_b_re"].rearrange("o g e -> o (g e)").to_broadcast([P, NE])).then_inc(one, 16)
            for t, use, s in pairs(sp, 2, NL):
                sp.wait_ge(yTt.sem, yTt.at(t - 2))
                load_y(t, use, s)
                sp.wait_ge(x1s.sem, x1s.at(t - 2))
                load_x(t, use, s)

        @block.gpsimd
        def _(pool):
            def body(t, use, s):
                if there(t - 1):
                    pool.wait_ge(ssq_x.sem, ssq_x.at(t - 1))
                    rstd_root(nc, g, pool, eps_x, t - 1, 1, ss[:, 3:4], ss[:, 1:2], D).then_inc(rstd_x.sem, 1)
                if there(t):
                    pool.wait_ge(ssq_y.sem, ssq_y.at(t))
                    rstd_root(nc, g, pool, eps_y, t, 1, ss[:, 2:3], ss[:, 0:1], D).then_inc(rstd_y.sem, 1)
            turns(pool, body)

        @block.tensor
        def _(pe):
            for x_ in (hTt, lgp):
                pe.sem_inc(x_.sem, x_.credit)
            ident = g["ident"][:, :]

            def body(t, use, s):
                if there(t + 1):
                    pe.wait_ge(y_in.sem(1 - s), y_in.at(use + s))
                    if there(t - 2):
                        pe.wait_ge(hTs.sem, hTs.at(t - 2))
                    elif there(t):
                        pe.wait_ge(yTl.sem, yTl.at(t))
                    for k in range(KD):
                        m = nc.tensor.transpose(pT[:, k], y[:, 1 - s, k * P:(k + 1) * P], ident)
                    m.then_inc(yTt.sem, 1)
                if there(t):
                    if there(t - 2):
                        pe.wait_ge(yns.sem, yns.at(t - 2))
                    pe.wait_ge(yTh.sem, yTh.at(t))
                    pe.wait_ge(yTl.sem, yTl.at(t))
                    for k in range(KD):
                        pe.wait_ge(wls.sem, wls.at(k))
                        for part, with_ in ((0, wh), (0, wl), (1, wh)):
                            for n in range(2):
                                m = nc.tensor.matmul(py[:, s, n], yT[:, s, part, k], with_[:, k, n * 512:(n + 1) * 512], start=(k == 0 and part == 0 and with_ is wh),
                                                     stop=(k == KD - 1 and part == 1))
                    m.then_inc(prod.sem, 1)
                if there(t - 1):
                    pe.wait_ge(h2s.sem, h2s.at(t - 1))
                    if there(t + 1):
                        pe.wait_ge(yTl.sem, yTl.at(t + 1))
                    else:
                        pe.wait_ge(hTs.sem, hTs.at(t - 2))
                    for k in range(KD):
                        m = nc.tensor.transpose(pT[:, k], h2[:, 1 - s, k * P:(k + 1) * P], ident)
                    m.then_inc(hTt.sem, 1)
                if there(t - 2):
                    pe.wait_ge(w_l.sem(0), w_l.at(0))
                    pe.wait_ge(hTs.sem, hTs.at(t - 2))
                    pe.wait_ge(lgs.sem, lgs.at(t - 3))
                    for k in range(KD):
                        m = nc.tensor.matmul(pl[:, 0:NG + NE], hT[:, s, k], wr[:, k], start=(k == 0), stop=(k == KD - 1))
                    m.then_inc(lgp.sem, 1)
            turns(pe, body)

        @block.scalar
        def _(act):
            def body(t, use, s):
                if there(t - 1):
                    act.wait_ge(x1s.sem, x1s.at(t - 1))
                    nc.scalar.activation(sq[:], x1[:, 1 - s], ACT.Square, accum_out=ss[:, 1:2]).then_inc(ssq_x.sem, 1)
                    act.dma_start(tile_of(dram["x1"], t - 1), x1[:, 1 - s]).then_inc(x1_out.sem(1 - s), 16)
                if there(t + 1):
                    act.wait_ge(yTt.sem, yTt.at(t + 1))
                    if there(t - 1):
                        act.wait_ge(prod.sem, prod.at(t - 1))
                    nc.scalar.activation(yT[:, 1 - s, 0], pT[:], ACT.Copy).then_inc(yTh.sem, 1)
                if isinstance(t, int) and t == -1:
                    for k in range(KD):
                        act.wait_ge(wsc.sem, wsc.at(k))
                        nc.scalar.activation(wh[:, k], w[:, k], ACT.Copy).then_inc(whs.sem, 1)
                if there(t):
                    act.wait_ge(prod.sem, prod.at(t))
                    if there(t - 1):
                        act.wait_ge(ssq_x.sem, ssq_x.at(t - 1))
                        act.wait_ge(yns.sem, yns.at(t - 1))
                    nc.scalar.activation(sq[:], py[:, s].rearrange("p a b -> p (a b)"), ACT.Square, accum_out=ss[:, 0:1]).then_inc(ssq_y.sem, 1)
                if there(t - 1):
                    act.wait_ge(hTt.sem, hTt.at(t - 1))
                    act.wait_ge(lgp.sem, lgp.at(t - 3)) if there(t - 3) else None
                    nc.scalar.activation(hT[:, 1 - s], pT[:], ACT.Copy).then_inc(hTs.sem, 1)
                    act.dma_start(tile_of(dram["h2"], t - 1), h2[:, 1 - s]).then_inc(h2_out.sem(1 - s), 16)
            turns(act, body)
            for s in range(2):
                act.wait_ge(x1_out.sem(s), x1_out.at(NL // 2 - 1))
                act.wait_ge(h2_out.sem(s), h2_out.at(NL // 2 - 1))

        @block.vector
        def _(dve):
            dve.sem_inc(lgs.sem, lgs.credit)

            def body(t, use, s):
                if there(t + 1):
                    dve.wait_ge(yTh.sem, yTh.at(t + 1))
                    nc.vector.tensor_tensor(yT[:, 1 - s, 1], pT[:], yT[:, 1 - s, 0].bitcast(F32), ALU.subtract).then_inc(yTl.sem, 1)
                if isinstance(t, int) and t == -1:
                    for k in range(KD + 1):
                        if k < KD:
                            nc.vector.tensor_scalar(w[:, k], w[:, k], g["wn"][:, k:k + 1], None, ALU.mult).then_inc(wsc.sem, 1)
                        if k:
                            dve.wait_ge(whs.sem, whs.at(k - 1))
                            nc.vector.tensor_tensor(wl[:, k - 1], w[:, k - 1], wh[:, k - 1].bitcast(F32), ALU.subtract).then_inc(wls.sem, 1)
                if there(t - 1):
                    dve.wait_ge(rstd_x.sem, rstd_x.at(t - 1))
                    dve.wait_ge(h2_out.sem(1 - s), h2_out.at(use + (s - 2)))
                    dve.wait_ge(hTt.sem, hTt.at(t - 3)) if there(t - 3) else None
                    nc.vector.scalar_tensor_tensor(out=h2[:, 1 - s], in0=x1[:, 1 - s], scalar=ss[:, 3:4], in1=g["mod"][:, 2], op0=ALU.mult, op1=ALU.mult).then_inc(h2m.sem, 1)
                    dve.wait_ge(h2m.sem, h2m.at(t - 1))
                    nc.vector.tensor_tensor(h2[:, 1 - s], h2[:, 1 - s], g["mod"][:, 1], ALU.add).then_inc(h2s.sem, 1)
                if there(t):
                    dve.wait_ge(rstd_y.sem, rstd_y.at(t))
                    if there(t - 1):
                        dve.wait_ge(x1s.sem, x1s.at(t - 1))
                    nc.vector.scalar_tensor_tensor(out=yn[:], in0=py[:, s].rearrange("p a b -> p (a b)"), scalar=ss[:, 2:3], in1=g["mod"][:, 0], op0=ALU.mult, op1=ALU.mult).then_inc(yns.sem, 1)
                    dve.wait_ge(yns.sem, yns.at(t))
                    dve.wait_ge(x_in.sem(s), x_in.at(use))
                    dve.wait_ge(x1_out.sem(s), x1_out.at(use - 1))
                    if there(t - 2):
                        dve.wait_ge(h2m.sem, h2m.at(t - 2))
                    nc.vector.tensor_tensor(x1[:, s], yn[:], x[:, s], ALU.add).then_inc(x1s.sem, 1)
                if there(t - 2):
                    dve.wait_ge(lgp.sem, lgp.at(t - 2))
                    nc.vector.tensor_tensor(g["logits"][:, bass.ds(t - 2, 1)].rearrange("p o n -> p (o n)"), pl[:, 0:NG + NE], br[:], ALU.add).then_inc(lgs.sem, 1)
            turns(dve, body)


def routing(nc, kit, io, g, dram):
    T4, T8, T32 = [P, NL, NG], [P, NL, EPG], [P, NL, NE]
    BIG = 1e30
    with ExitStack() as st:
        iota = kit.sb("o_iota", [P, EPG], stack=st)
        mult = kit.sb("o_mult", [P, NL - 1], stack=st)
        mg = kit.sb("o_mg", [P, NL], stack=st)
        e4 = kit.sb("o_e4", T4, stack=st)
        og = kit.sb("o_og", T4, stack=st)
        den = kit.sb("o_den", [P, NL], stack=st)
        w32 = kit.sb("o_w32", [P, NL, NG, EPG], stack=st)
        le = kit.sb("o_le", T8, stack=st)
        c8 = kit.sb("o_c8", T8, stack=st)
        m12 = kit.sb("o_m12", [P, 2, NL], stack=st)
        fi = kit.sb("o_fi", [P, NL], stack=st)
        o8 = kit.sb("o_o8", [P, 2, NL, EPG], stack=st)
        oh = kit.sb("o_oh", [P, 2, NL, NG, EPG], stack=st)
        both = kit.sb("o_both", T32, stack=st)
        rank = kit.sb("o_rank", T32, stack=st)
        tot = kit.sb("o_tot", [P, NL + 1, NE], stack=st)
        cnt = kit.sb("o_cnt", [P, NE], stack=st)
        zero = kit.sb("o_zero", [P, NE], stack=st)
        start = kit.sb("o_start", [P, NE], stack=st)
        cmp = kit.sb("o_cmp", [P, NE, NL - 1], stack=st)
        nb = kit.sb("o_nb", [P, NE], stack=st)
        sl = kit.sb("o_sl", [P, 2, NL], stack=st)
        ex = kit.sb("o_ex", [P, NL], stack=st)
        h2 = kit.sb("o_h2", [P, 4, D], stack=st)
        z = kit.sb("o_z", [P, D], stack=st)
        pr = kit.ps("o_pr", [P, 2, 512], st)
        c_in = kit.landing("o_const_in", dmas=2)
        h_in = kit.landing("o_h_in", 4)
        h_out = kit.landing("o_h_out", 4, dmas=2)
        z_out = kit.landing("o_z_out")
        step = kit.counter("o_step", 1)
        asked = kit.counter("o_exp_done", 2)
        counts = kit.counter("o_counts")
        zeroed = kit.counter("o_zeroed")
        marks = {}
        block = st.enter_context(nc.Block())

        @block.vector
        def _(dve):
            n = [0]
            V = nc.vector

            def link(ins):
                n[0] += 1
                ins.then_inc(step.sem, 1)
                dve.wait_ge(step.sem, n[0])

            def first_of(values, largest, out, width):
                link(V.tensor_tensor(out, values, largest.unsqueeze(2).to_broadcast([P, NL, width]), ALU.is_lt))
                link(V.scalar_tensor_tensor(out=out, in0=out, scalar=99.0, in1=iota[:, 0:width].unsqueeze(1).to_broadcast([P, NL, width]), op0=ALU.mult, op1=ALU.add))
                link(V.tensor_reduce(fi[:], out, AX, ALU.min))
                link(V.tensor_tensor(out, out, fi[:].unsqueeze(2).to_broadcast([P, NL, width]), ALU.is_equal))

            dve.wait_ge(c_in.sem(0), c_in.at(0))
            link(V.memset(zero[:], 0.0))
            lg4 = g["logits"][:, :, 0:NG]
            le32 = g["logits"][:, :, NG:].rearrange("p t (g e) -> p t g e", g=NG)
            link(V.tensor_reduce(mg[:], lg4, AX, ALU.max))
            link(V.tensor_tensor(e4[:], lg4, mg[:].unsqueeze(2).to_broadcast(T4), ALU.subtract))
            marks["shifted"] = n[0]
            first_of(lg4, mg[:], og[:], NG)
            link(V.tensor_tensor(w32[:], le32, og[:].unsqueeze(3).to_broadcast([P, NL, NG, EPG]), ALU.mult))
            link(V.tensor_reduce(le[:], w32[:].rearrange("p t g e -> p t e g"), AX, ALU.add))
            link(V.tensor_reduce(m12[:, 0], le[:], AX, ALU.max))
            first_of(le[:], m12[:, 0], o8[:, 0], EPG)
            link(V.scalar_tensor_tensor(out=c8[:], in0=o8[:, 0], scalar=-BIG, in1=le[:], op0=ALU.mult, op1=ALU.add))
            link(V.tensor_reduce(m12[:, 1], c8[:], AX, ALU.max))
            first_of(c8[:], m12[:, 1], o8[:, 1], EPG)
            link(V.tensor_tensor(ex[:], m12[:, 1], m12[:, 0], ALU.subtract))
            marks["difference"] = n[0]
            for k in range(2):
                link(V.tensor_tensor(oh[:, k], og[:].unsqueeze(3).to_broadcast([P, NL, NG, EPG]), o8[:, k].unsqueeze(2).to_broadcast([P, NL, NG, EPG]), ALU.mult))
            link(V.tensor_tensor(both[:], oh[:, 0].rearrange("p t g e -> p t (g e)"), oh[:, 1].rearrange("p t g e -> p t (g e)"), ALU.add))
            marks["chosen"] = n[0]
            dve.wait_ge(asked.sem, 2)
            link(V.tensor_reduce(den[:], e4[:], AX, ALU.add))
            link(V.scalar_tensor_tensor(out=den[:], in0=ex[:], scalar=1.0, in1=den[:], op0=ALU.add, op1=ALU.mult))
            link(V.reciprocal(g["wtop"][:, 0], den[:]))
            link(V.tensor_tensor(g["wtop"][:, 1], g["wtop"][:, 0], ex[:], ALU.mult))
            dve.wait_ge(counts.sem, counts.at(0))
            link(V.memset(tot[:, 0], 0.0))
            link(V.tensor_copy(rank[:], pr[:, 0].rearrange("p (t e) -> p t e", e=NE)))
            for t in range(NL):
                link(V.tensor_tensor(tot[:, t + 1], tot[:, t], pr[:, 1, t * NE:(t + 1) * NE], ALU.add))
            link(V.tensor_tensor_scan(start[:], tot[:, NL], zero[:], 0.0, ALU.add, ALU.add))
            link(V.tensor_tensor(start[:], start[:], tot[:, NL], ALU.subtract))
            link(V.tensor_tensor(rank[:], rank[:], tot[:, 0:NL], ALU.add))
            link(V.tensor_tensor(rank[:], rank[:], start[:].unsqueeze(1).to_broadcast(T32), ALU.add))
            for k in range(2):
                link(V.tensor_tensor(w32[:].rearrange("p t g e -> p t (g e)"), oh[:, k].rearrange("p t g e -> p t (g e)"), rank[:], ALU.mult))
                link(V.tensor_reduce(sl[:, k], w32[:].rearrange("p t g e -> p t (g e)"), AX, ALU.add))
            link(V.tensor_copy(g["slots"][:], sl[:]))
            marks["slots"] = n[0]
            link(V.tensor_tensor(cmp[:], tot[:, NL].unsqueeze(2).to_broadcast([P, NE, NL - 1]), mult[:].unsqueeze(1).to_broadcast([P, NE, NL - 1]), ALU.is_gt))
            link(V.tensor_reduce(nb[:], cmp[:], AX, ALU.add))
            link(V.tensor_scalar(nb[:], nb[:], 1.0, None, ALU.add))
            link(V.tensor_copy(g["spans"][:, 0], start[0:1]))
            link(V.tensor_copy(g["spans"][:, 1], nb[0:1]))

        @block.scalar
        def _(act):
            act.wait_ge(step.sem, marks["shifted"])
            nc.scalar.activation(e4[:], e4[:], ACT.Exp).then_inc(asked.sem, 1)
            act.wait_ge(step.sem, marks["difference"])
            nc.scalar.activation(ex[:], ex[:], ACT.Exp).then_inc(asked.sem, 1)

        @block.tensor
        def _(pe):
            pe.wait_ge(step.sem, marks["chosen"])
            flat = both[:].rearrange("p t e -> p (t e)")
            nc.tensor.matmul(pr[:, 0], g["tri"][:, 3], flat, start=True, stop=True)
            nc.tensor.matmul(pr[:, 1], g["tri"][:, 4], flat, start=True, stop=True).then_inc(counts.sem, 1)

        @block.sync
        def _(sp):
            sp.dma_start(iota[:], io["iota8"]).then_inc(c_in.sem(0), 16)
            sp.dma_start(mult[:], io["multiples"]).then_inc(c_in.sem(0), 16)
            for t in range(NL):
                if t >= 4:
                    sp.wait_ge(h_out.sem(t % 4), 32 * (t // 4))
                sp.dma_start(h2[:, t % 4], dram["h2"][t]).then_inc(h_in.sem(t % 4), 16)

        @block.gpsimd
        def _(pool):
            nc.gpsimd.memset(z[:], 0.0).then_inc(zeroed.sem, 1)
            pool.wait_ge(zeroed.sem, 1)
            for rows in ("hs", "ys"):
                pool.dma_start(dram[rows][2 * SEQ:ROWS, :], z[:]).then_inc(z_out.sem(0), 16)
            pool.wait_ge(step.sem, marks["slots"])
            for t in range(NL):
                pool.wait_ge(h_in.sem(t % 4), 16 * (t // 4 + 1))
                for k in range(2):
                    pool.indirect_dma_start(dram["hs"], bass.IndirectOffsetOnAxis(ap=g["slots"][:, k, t:t + 1], axis=0), h2[:, t % 4], None).then_inc(h_out.sem(t % 4), 16)
            for s in range(4):
                pool.wait_ge(h_out.sem(s), 32 * NL // 4)
            pool.wait_ge(z_out.sem(0), 32)


def experts(nc, kit, io, g, dram):
    MAXB = NL
    THIRD = 2 * KD * DE // 2
    HALF = THIRD // 2
    with ExitStack() as st:
        raw = kit.sb("e_w_raw", [P, 3, THIRD], stack=st)
        wh = kit.sb("e_w_high", [P, 3, THIRD], F32R, stack=st)
        wl = kit.sb("e_w_low", [P, 3, THIRD], F32R, stack=st)
        xb = kit.sb("e_x", [P, D], stack=st)
        xT = kit.sb("e_xT", [P, 2, KD, P], F32R, stack=st)
        sg = kit.sb("e_sg", [P, 2, 256], stack=st)
        hid = kit.sb("e_hid", [P, DE], stack=st)
        hT = kit.sb("e_hT", [P, 2, DE // P, P], F32R, stack=st)
        y = kit.sb("e_y", [P, D], stack=st)
        pX = kit.ps("e_pX", [P, KD, P], st)
        pG = kit.ps("e_pG", [P, 2, 2, 256], st)
        pH = kit.ps("e_pH", [P, 2, 4, P], st)
        pY = kit.ps("e_pY", [P, 2, 512], st)
        w_in = kit.landing("e_w_in", 3, dmas=2)
        x_in = kit.landing("e_x_in")
        y_out = kit.landing("e_y_out", credit=16)
        whs = kit.counter("e_w_high_ready", 6)
        wls = kit.counter("e_w_low_ready", 6, credit=6)
        xTt = kit.counter("e_x_transposed", 1, credit=1)
        xTs = kit.counter("e_xT_high_ready", 1, credit=1)
        xTl = kit.counter("e_xT_low_ready", 1, credit=1)
        prodG = kit.counter("e_gate_up", 2, credit=2)
        sgs = kit.counter("e_silu", 2, credit=2)
        hids = kit.counter("e_hidden", 2, credit=2)
        hTt = kit.counter("e_hidden_transposed", 2, credit=2)
        hTs = kit.counter("e_hT_high_ready", 2, credit=2)
        hTl = kit.counter("e_hT_low_ready", 2, credit=2)
        prodY = kit.counter("e_down", 1, credit=1)
        ya = kit.counter("e_y_act", 1, credit=1)
        yd = kit.counter("e_y_dve", 1, credit=1)
        junk = kit.counter("e_paused")
        block = st.enter_context(nc.Block())

        def over_blocks(eng, body, enter=None):
            count = eng.alloc_register("e_block")
            eng.reg_mov(count, 0)
            at = eng.alloc_register("e_row")
            left = eng.alloc_register("e_blocks_left")

            def one(following):
                body(eng.snap(count, min_val=0, max_val=2 * NE), eng.snap(at, min_val=0, max_val=2 * SEQ), following)
                eng.reg_add(count, count, 1)
                eng.reg_add(at, at, P)

            def expert(e, following):
                blocks = eng.value_load(g["spans"][0:1, 1, bass.ds(e, 1)], min_val=1, max_val=MAXB)
                row0 = eng.value_load(g["spans"][0:1, 0, bass.ds(e, 1)], min_val=0, max_val=2 * SEQ)
                eng.reg_mov(at, row0)
                if enter:
                    enter(e)
                if following is None:
                    with eng.Fori(0, blocks) as j:
                        one(None)
                else:
                    eng.reg_mov(left, blocks)
                    with eng.If_ne(left, 1):
                        with eng.Fori(1, blocks) as j:
                            one(None)
                    one(following)

            with eng.Fori(0, NE - 1) as e:
                expert(e, e + 1)
            expert(NE - 1, None)
            return count

        @block.sync
        def _(sp):
            with sp.Fori(0, NE) as e:
                for third in range(3):
                    sp.wait_ge(wls.sem, wls.at(e - 1, 2 * third + 2))
                    for n, src in enumerate(("moe_w_gate", "moe_w_up")):
                        if third < 2:
                            to = raw[:, third].rearrange("p (k n f) -> p k n f", k=KD, n=2)[:, :, n]
                            sp.dma_start(to, io[src][0, bass.ds(e, 1), :, third * 256:(third + 1) * 256].rearrange("o (k p) f -> p (o k) f", p=P)).then_inc(w_in.sem(third), 16)
                        else:
                            to = raw[:, third, n * HALF:(n + 1) * HALF].rearrange("p (k f) -> p k f", k=2)
                            sp.dma_start(to, io["moe_w_down"][0, bass.ds(e, 1), n * 256:(n + 1) * 256].rearrange("o (k p) f -> p (o k) f", p=P)).then_inc(w_in.sem(third), 16)

        @block.gpsimd
        def _(pool):
            def load(b, row, following):
                pool.wait_ge(xTt.sem, xTt.at(b - 1))
                pool.sem_inc(junk.sem, 1)
                pool.dma_start(xb[:], dram["hs"][bass.ds(row, P), :]).then_inc(x_in.sem(0), 16)
            count = over_blocks(pool, load)
            b = pool.snap(count, min_val=0, max_val=2 * NE)
            pool.wait_ge(xTt.sem, xTt.at(b - 1))
            pool.sem_inc(junk.sem, 1)
            pool.dma_start(xb[:], dram["hs"][0:P, :]).then_inc(x_in.sem(0), 16)

        @block.tensor
        def _(pe):
            for x_ in (xTt, prodG, hTt, prodY):
                pe.sem_inc(x_.sem, x_.credit)
            ident = g["ident"][:, :]

            def turn_x(b):
                pe.wait_ge(x_in.sem(0), x_in.at(b))
                pe.wait_ge(xTl.sem, xTl.at(b - 1))
                for k in range(KD):
                    m = nc.tensor.transpose(pX[:, k], xb[:, k * P:(k + 1) * P], ident)
                m.then_inc(xTt.sem, 1)

            def turn_h(b, half):
                pe.wait_ge(hids.sem, hids.at(b, half + 1))
                pe.wait_ge(hTl.sem, hTl.at(b - 1, half + 1))
                for c in range(2):
                    m = nc.tensor.transpose(pH[:, half, c], hid[:, (2 * half + c) * P:(2 * half + c + 1) * P], ident)
                m.then_inc(hTt.sem, 1)

            def body(b, row, following, e=None):
                for half in range(2):
                    pe.wait_ge(hids.sem, hids.at(b - 1, half + 1))
                    pe.wait_ge(xTs.sem, xTs.at(b))
                    pe.wait_ge(wls.sem, wls.at(expert_of[0], 2 * half + 2))
                    for k in range(KD):
                        w = slice(k * 512, (k + 1) * 512)
                        nc.tensor.matmul(pG[:, half], xT[:, 0, k], wh[:, half, w], start=(k == 0), stop=False)
                        nc.tensor.matmul(pG[:, half], xT[:, 0, k], wl[:, half, w], start=False, stop=False)
                    pe.wait_ge(xTl.sem, xTl.at(b))
                    for k in range(KD):
                        m = nc.tensor.matmul(pG[:, half], xT[:, 1, k], wh[:, half, k * 512:(k + 1) * 512], start=False, stop=(k == KD - 1))
                    m.then_inc(prodG.sem, 1)
                turn_h(b, 0)
                turn_x(b + 1)
                turn_h(b, 1)
                pe.wait_ge(ya.sem, ya.at(b - 1))
                pe.wait_ge(yd.sem, yd.at(b - 1))
                pe.wait_ge(wls.sem, wls.at(expert_of[0], 6))
                for k in range(DE // P):
                    for part, with_ in ((0, wh), (0, wl), (1, wh)):
                        if k % 2 == 0:
                            part_ready = hTl if part else hTs
                            pe.wait_ge(part_ready.sem, part_ready.at(b, k // 2 + 1))
                        for n in range(2):
                            c0 = k * D + n * 512
                            m = nc.tensor.matmul(pY[:, n], hT[:, part, k], with_[:, 2, c0:c0 + 512], start=(k == 0 and part == 0 and with_ is wh),
                                                 stop=(k == DE // P - 1 and part == 1))
                m.then_inc(prodY.sem, 1)

            expert_of = [None]

            def enter(e):
                expert_of[0] = e
            turn_x(0)
            over_blocks(pe, body, enter)

        @block.scalar
        def _(act):
            for x_ in (xTs, sgs, hTs, ya):
                act.sem_inc(x_.sem, x_.credit)
            act.sem_inc(y_out.sem(0), 16)

            def xT_copy(b):
                act.wait_ge(xTt.sem, xTt.at(b))
                act.wait_ge(prodG.sem, prodG.at(b - 1))
                nc.scalar.activation(xT[:, 0], pX[:], ACT.Copy).then_inc(xTs.sem, 1)

            def high(e, third):
                act.wait_ge(w_in.sem(third), w_in.at(e))
                for n in range(2):
                    part = slice(n * HALF, (n + 1) * HALF)
                    nc.scalar.activation(wh[:, third, part], raw[:, third, part], ACT.Copy).then_inc(whs.sem, 1)

            def body(b, row, following):
                for half in range(2):
                    act.wait_ge(prodG.sem, prodG.at(b, half + 1))
                    nc.scalar.activation(sg[:, half], pG[:, half, 0], ACT.Silu).then_inc(sgs.sem, 1)
                    if following is not None and half == 0:
                        high(following, 0)
                for half in range(2):
                    act.wait_ge(hTt.sem, hTt.at(b, half + 1))
                    act.wait_ge(prodY.sem, prodY.at(b - 1))
                    nc.scalar.activation(hT[:, 0, 2 * half:2 * half + 2], pH[:, half, 0:2], ACT.Copy).then_inc(hTs.sem, 1)
                    if half == 0:
                        xT_copy(b + 1)
                if following is not None:
                    high(following, 1)
                act.wait_ge(prodY.sem, prodY.at(b))
                act.wait_ge(y_out.sem(0), b * 16 + 16)
                nc.scalar.activation(y[:, 0:512], pY[:, 0], ACT.Copy).then_inc(ya.sem, 1)
                act.wait_ge(ya.sem, ya.at(b))
                act.wait_ge(yd.sem, yd.at(b))
                act.dma_start(dram["ys"][bass.ds(row, P), :], y[:]).then_inc(y_out.sem(0), 16)
                if following is not None:
                    high(following, 2)
            for third in range(3):
                high(0, third)
            xT_copy(0)
            count = over_blocks(act, body)
            b = act.snap(count, min_val=0, max_val=2 * NE)
            act.wait_ge(y_out.sem(0), b * 16 + 16)
            act.sem_inc(junk.sem, 1)

        @block.vector
        def _(dve):
            for x_ in (xTl, hids, hTl, yd, wls):
                dve.sem_inc(x_.sem, x_.credit)

            def xT_low(b):
                dve.wait_ge(xTs.sem, xTs.at(b))
                nc.vector.tensor_tensor(xT[:, 1], pX[:], xT[:, 0].bitcast(F32), ALU.subtract).then_inc(xTl.sem, 1)

            def low(e, third):
                for n in range(2):
                    part = slice(n * HALF, (n + 1) * HALF)
                    dve.wait_ge(whs.sem, whs.at(e, 2 * third + n + 1))
                    nc.vector.tensor_tensor(wl[:, third, part], raw[:, third, part], wh[:, third, part].bitcast(F32), ALU.subtract).then_inc(wls.sem, 1)

            def body(b, row, following):
                for half in range(2):
                    dve.wait_ge(sgs.sem, sgs.at(b, half + 1))
                    dve.wait_ge(hTt.sem, hTt.at(b - 1, half + 1))
                    nc.vector.tensor_tensor(hid[:, half * 256:(half + 1) * 256], sg[:, half], pG[:, half, 1], ALU.mult).then_inc(hids.sem, 1)
                    if following is not None and half == 0:
                        low(following, 0)
                for half in range(2):
                    dve.wait_ge(hTs.sem, hTs.at(b, half + 1))
                    nc.vector.tensor_tensor(hT[:, 1, 2 * half:2 * half + 2], pH[:, half, 0:2], hT[:, 0, 2 * half:2 * half + 2].bitcast(F32), ALU.subtract).then_inc(hTl.sem, 1)
                    if half == 0:
                        xT_low(b + 1)
                if following is not None:
                    low(following, 1)
                dve.wait_ge(prodY.sem, prodY.at(b))
                dve.wait_ge(y_out.sem(0), b * 16 + 16)
                nc.vector.tensor_copy(y[:, 512:D], pY[:, 1]).then_inc(yd.sem, 1)
                if following is not None:
                    low(following, 2)
            for third in range(3):
                low(0, third)
            xT_low(0)
            over_blocks(dve, body)


def combine(nc, kit, io, g, dram):
    B = 3
    with ExitStack() as st:
        yy = kit.sb("c_yy", [P, B, 2, D], stack=st)
        x1 = kit.sb("c_x1", [P, B, D], stack=st)
        v = kit.sb("c_v", [P, B, D], stack=st)
        sq = kit.sb("c_sq", [P, B, D], stack=st)
        ss = kit.sb("c_ss", [P, B, 2], stack=st)
        y_in = kit.landing("c_y_in", B, dmas=2)
        x_in = kit.landing("c_x_in", B)
        o_out = kit.landing("c_out", B)
        summed = kit.counter("c_summed", 2)
        ssq = kit.counter("c_ssq")
        eps_added = kit.counter("c_eps_added")
        rstd = kit.counter("c_rstd")
        outs = kit.counter("c_out_ready", 2)
        block = st.enter_context(nc.Block())

        @block.gpsimd
        def _(pool):
            def gather(t):
                if t >= B:
                    pool.wait_ge(summed.sem, summed.at(t - B))
                for k in range(2):
                    pool.indirect_dma_start(yy[:, t % B, k], None, dram["ys"], bass.IndirectOffsetOnAxis(ap=g["slots"][:, k, t:t + 1], axis=0)).then_inc(y_in.sem(t % B), 16)

            def root(t):
                pool.wait_ge(ssq.sem, ssq.at(t))
                rstd_root(nc, g, pool, eps_added, t, 1, ss[:, t % B, 1:2], ss[:, t % B, 0:1], D).then_inc(rstd.sem, 1)
            for t in range(NL + 2):
                if t < NL:
                    gather(t)
                if t >= 2:
                    root(t - 2)

        @block.sync
        def _(sp):
            def load(t):
                if t >= B:
                    sp.wait_ge(outs.sem, outs.at(t - B))
                sp.dma_start(x1[:, t % B], dram["x1"][t]).then_inc(x_in.sem(t % B), 16)

            def store(t):
                sp.wait_ge(outs.sem, outs.at(t))
                sp.dma_start(io["out0"][0, t * P:(t + 1) * P, :], v[:, t % B]).then_inc(o_out.sem(t % B), 16)
            for t in range(NL + B - 1):
                if t >= B - 1:
                    store(t - B + 1)
                if t < NL:
                    load(t)
            for s in range(B):
                sp.wait_ge(o_out.sem(s), 16 * len(range(s, NL, B)))

        @block.scalar
        def _(act):
            for t in range(NL):
                act.wait_ge(summed.sem, summed.at(t))
                if t >= B:
                    act.wait_ge(outs.sem, outs.at(t - B))
                nc.scalar.activation(sq[:, t % B], v[:, t % B], ACT.Square, accum_out=ss[:, t % B, 0:1]).then_inc(ssq.sem, 1)

        @block.vector
        def _(dve):
            def add(t):
                s = t % B
                dve.wait_ge(y_in.sem(s), y_in.at(t // B))
                if t >= B:
                    dve.wait_ge(o_out.sem(s), 16 * (t // B))
                nc.vector.tensor_scalar(v[:, s], yy[:, s, 0], g["wtop"][:, 0, t:t + 1], None, ALU.mult).then_inc(summed.sem, 1)
                dve.wait_ge(summed.sem, summed.at(t, 1))
                nc.vector.scalar_tensor_tensor(out=v[:, s], in0=yy[:, s, 1], scalar=g["wtop"][:, 1, t:t + 1], in1=v[:, s], op0=ALU.mult, op1=ALU.add).then_inc(summed.sem, 1)

            def finish(t):
                s = t % B
                dve.wait_ge(rstd.sem, rstd.at(t))
                nc.vector.scalar_tensor_tensor(out=v[:, s], in0=v[:, s], scalar=ss[:, s, 1:2], in1=g["mod"][:, 3], op0=ALU.mult, op1=ALU.mult).then_inc(outs.sem, 1)
                dve.wait_ge(outs.sem, outs.at(t, 1))
                dve.wait_ge(x_in.sem(s), x_in.at(t // B))
                nc.vector.tensor_tensor(v[:, s], v[:, s], x1[:, s], ALU.add).then_inc(outs.sem, 1)
            for t in range(NL + 1):
                if t < NL:
                    add(t)
                if t >= 1:
                    finish(t - 1)


def program(nc, io):
    kit = Kit(nc)
    g = globals_of(kit)

    def scratch(name, shape):
        return nc.dram_tensor(name, shape, F32).ap()
    dram = {
        "tok": scratch("by_token", (NT, P, NTOK)),
        "ch": scratch("by_channel", (NCH, P, NT * P)),
        "u": scratch("convolved", (NCH, P, NT * P)),
        "sb": scratch("backward_states", (NT, P, D)),
        "y": scratch("mixed", (NT, P, D)),
        "x1": scratch("after_mixing", (NL, P, D)),
        "h2": scratch("second_norm", (NL, P, D)),
        "hs": scratch("rows_sorted", (ROWS, D)),
        "ys": scratch("rows_done", (ROWS, D)),
    }
    for stage in (modulation, projection, convolution, states, mixing, residual, routing, experts, combine):
        if stage is convolution:
            g.update(routing_globals_of(kit))
            mixing_only = ExitStack()
            g.update(mixing_globals_of(kit, mixing_only))
        if stage is mixing:
            g["w_out"] = kit.sb("w_out_sb", [P, KD, D], stack=mixing_only)
        if stage is residual or stage is routing:
            kit.retire()
        if stage is routing:
            mixing_only.close()
        stage(nc, kit, io, g, dram)
    kit.keep.close()


_INS = ['x', 'c', 'ctx', 'c_ctx', 'w_mod', 'b_mod', 'norm_pre_mix', 'norm_post_mix', 'norm_pre_ffn',
        'norm_post_ffn', 'w_in', 'w_out', 'ret_decay_f', 'ret_decay_b', 'ret_gn_w', 'ssd_conv_w',
        'ssd_conv_b', 'ssd_dt_bias_f', 'ssd_dt_bias_b', 'ssd_a_log_f', 'ssd_a_log_b', 'ssd_d',
        'ssd_norm_w', 'moe_w_rg', 'moe_b_rg', 'moe_w_re', 'moe_b_re', 'moe_w_gate', 'moe_w_up', 'moe_w_down']
_OUTS = [((1, SEQ, D), 'float32')]


def constants():
    f = np.float32
    quarter = P // 4
    freq = 10000.0 ** (-np.arange(quarter) / quarter)
    t = np.arange(SEQ)
    ang = np.stack([(t // 64)[:, None] * freq, (t % 64)[:, None] * freq], 1)
    cos = np.repeat(np.cos(ang)[:, :, None], 2, 2).reshape(SEQ, P)
    sin = np.stack([-np.sin(ang), np.sin(ang)], 2).reshape(SEQ, P)
    cos = np.concatenate([np.ones((CTX, P)), cos])
    sin = np.concatenate([np.zeros((CTX, P)), sin])
    s = float(P) ** -0.5
    rope = np.stack([cos, sin, cos * s, sin * s], 1).reshape(NT, P, 4 * P).astype(f)
    i = np.arange(P)
    rel = i[None, :] - i[:, None]
    return {
        "rope": rope,
        "ident": np.eye(P, dtype=f),
        "tri": np.stack([rel >= 0, rel < 0, rel <= 0, rel > 0, rel < 9999], 1).astype(f),
        "rel": np.stack([np.maximum(rel, 0), np.maximum(-rel, 0), np.tile(i + 1, (P, 1)), np.tile(P - i, (P, 1))], 1).astype(f),
        "relk": np.stack([P - 1 - i, i], 1).astype(f),
        "iota8": np.tile(np.arange(EPG).astype(f), (P, 1)),
        "multiples": np.tile(np.arange(1, NL).astype(f) * P, (P, 1)),
    }


def kernel(**inputs):
    import concourse.bacc as _bacc
    from concourse import mybir as _mybir
    from concourse.bass_utils import run_bass_kernel_spmd as _run

    nc = _bacc.Bacc("TRN2", target_bir_lowering=False, num_devices=1)
    arrays, io = {}, {}
    given = {name: np.ascontiguousarray(inputs[name]) for name in _INS}
    for name, a in {**given, **constants()}.items():
        arrays[f"in_{name}_dram"] = a
        io[name] = nc.dram_tensor(f"in_{name}_dram", a.shape, _mybir.dt.from_np(a.dtype), kind="ExternalInput").ap()
    for i, (shape, dtype) in enumerate(_OUTS):
        dt = _mybir.dt.from_np(np.dtype(dtype))
        io[f"out{i}"] = nc.dram_tensor(f"out_{i}_dram", shape, dt, kind="ExternalOutput").ap()
    program(nc, io)
    r = _run(nc, [arrays], core_ids=[0])
    got = tuple(r.results[0][f"out_{i}_dram"] for i in range(len(_OUTS)))
    return got[0]
```

```python
from contextlib import ExitStack

import numpy as np
import concourse.bass as bass
from concourse import mybir

F32 = mybir.dt.float32
I32 = mybir.dt.int32
F32R = mybir.dt.float32r
ALU = mybir.AluOpType
ACT = mybir.ActivationFunctionType
AX = mybir.AxisListType.X

P = 128
D = 1024
KD = D // P
SEQ = 2048
CTX = 256
NT = (SEQ + CTX) // P
NCT = CTX // P
NL = SEQ // P
RH = 4
RW = 512
SH = 8
SP_ = 64
SG = 2
DPROJ = 3600
NTOK = 5 * 512 + 16
NCH = 8
CONV = 5
NG = 4
EPG = 8
NE = 32
DE = 512
ROWS = 2 * SEQ + P
EPS = 1e-6
EPS_OF = {1: 0, 512: 4, D: 8}


class Counter:

    def __init__(self, sem, per=1, credit=0):
        self.sem, self.per, self.credit = sem, per, credit

    def at(self, turn, n=None):
        return turn * self.per + (self.credit + (self.per if n is None else n))


class Landing:

    def __init__(self, sems, dmas=1, credit=0):
        self.sems, self.dmas, self.credit = sems, dmas, credit

    def sem(self, slot):
        return self.sems[slot]

    def at(self, use):
        return use * (16 * self.dmas) + (16 * self.dmas + self.credit)


class Kit:

    def __init__(self, nc):
        self.nc = nc
        self.keep = ExitStack()
        self.sems = []

    def semaphore(self, name):
        self.sems.append(self.nc.alloc_semaphore(name))
        return self.sems[-1]

    def counter(self, name, per=1, credit=0):
        return Counter(self.semaphore(name), per, credit)

    def landing(self, name, slots=1, dmas=1, credit=0):
        return Landing([self.semaphore(f"{name}{s}") for s in range(slots)], dmas, credit)

    def retire(self):
        self.nc.clear_and_free_semaphores(self.sems)
        self.nc.all_engine_barrier()
        self.sems = []

    def sb(self, name, shape, dt=F32, stack=None):
        return (stack or self.keep).enter_context(self.nc.sbuf_tensor(name, shape, dt))

    def ps(self, name, shape, stack):
        return stack.enter_context(self.nc.psum_tensor(name, shape, F32))


def pairs(eng, first, last):
    with eng.Fori(0, (last - first) // 2) as i:
        for s in range(2):
            yield i * 2 + (first + s), i, s


def globals_of(kit):
    return {
        "ident": kit.sb("ident", [P, P]),
        "csil": kit.sb("csil", [P, 2, KD]),
        "cols": kit.sb("cols", [P, 2, KD, 2]),
        "neghalf": kit.sb("neghalf", [P, 16]),
        "eps": kit.sb("eps", [P, 12]),
    }


def mixing_globals_of(kit, st):
    return {
        "E": kit.sb("E", [P, NT, 6, SH], stack=st),
        "dd": kit.sb("dd", [P, NT, 4, SH], stack=st),
        "dskip": kit.sb("dskip", [P, SH], stack=st),
        "wn": kit.sb("wn", [P, KD], stack=st),
        "DT": kit.sb("DT", [P, RH, P], stack=st),
        "Dq": kit.sb("Dq", [P, 2, RH, P], stack=st),
        "Dk": kit.sb("Dk", [P, 2, RH], stack=st),
        "Dtot": kit.sb("Dtot", [P, 2, RH], stack=st),
        "sf": kit.sb("sf", [P, 2, 2, 512], stack=st),
    }


def routing_globals_of(kit):
    return {
        "tri": kit.sb("tri", [P, 5, P]),
        "mod": kit.sb("mod", [P, 4, D]),
        "logits": kit.sb("logits", [P, NL, NG + NE]),
        "slots": kit.sb("slots", [P, 2, NL], I32),
        "wtop": kit.sb("wtop", [P, 2, NL]),
        "spans": kit.sb("spans", [1, 2, NE], I32),
    }


def tile_of(dram, t, lo=None, hi=None):
    v = dram[bass.ds(t, 1), :, :] if lo is None else dram[bass.ds(t, 1), :, lo:hi]
    return v.rearrange("o p f -> p (o f)")


def modulation(nc, kit, io, g, dram):
    NMOD = 4
    with ExitStack() as st:
        raw = kit.sb("w_in_whole", [P, 2, KD // 2, 512], stack=st)
        raw_in = kit.landing("w_first_in", 2)
        raw_high = kit.counter("w_first_high_ready")
        raw_low = kit.counter("w_first_low_ready")
        halves = [(n // 2, slice(n % 2 * 4, n % 2 * 4 + 4)) for n in range(6)]
        ccol = kit.sb("ccol", [P, 2, KD], stack=st)
        csil = g["csil"]
        shift_scale = kit.sb("shift_scale", [P, 2 * D], stack=st)
        both = kit.sb("both", [P, KD, P], stack=st)
        wm = kit.sb("wm", [P, 2, KD, 512], stack=st)
        bm = kit.sb("bm", [P, 2, 512], stack=st)
        ncol = kit.sb("ncol", [P, KD], stack=st)
        acc = kit.ps("mod_acc", [P, 2, 512], st)
        colT = kit.ps("mod_colT", [P, 4, 4, P], st)
        c_in = kit.landing("c_in", dmas=2)
        w_in = kit.landing("wmod_in", 2, dmas=2)
        n_in = kit.landing("norm_cols_in", dmas=2)
        silu = kit.counter("c_silu")
        spread = kit.counter("c_spread", 2)
        row_acc = kit.counter("mod_row_acc", 1, credit=2)
        row = kit.counter("mod_row", 1, credit=2)
        cols_t = kit.counter("mod_cols_t")
        fin = kit.counter("mod_final")
        block = st.enter_context(nc.Block())

        @block.sync
        def _(sp):
            for n, src in enumerate((io["c"].rearrange("a d -> (a d)"), io["c_ctx"])):
                sp.dma_start(ccol[:, n, :], src.rearrange("(k p) -> p k", p=P), allow_slow_non_contiguous=True).then_inc(c_in.sem(0), 16)
            sp.dma_start(ncol[:, :], io["norm_pre_mix"].rearrange("o (k p) -> p (o k)", p=P), allow_slow_non_contiguous=True).then_inc(n_in.sem(0), 16)
            sp.dma_start(g["ident"][:, :], io["ident"]).then_inc(n_in.sem(0), 16)
            wsrc = io["w_mod"].rearrange("o (k p) (n f) -> n p (o k) f", p=P, f=512)
            bsrc = io["b_mod"].rearrange("o (n f) -> n o f", f=512)
            w_src = io["w_in"].rearrange("o (k p) f -> p (o k) f", p=P)

            def load_mod(t):
                if t >= 2:
                    sp.wait_ge(row_acc.sem, row_acc.at(t - 2))
                    sp.wait_ge(row.sem, row.at(t - 2))
                sp.dma_start(wm[:, t % 2], wsrc[t]).then_inc(w_in.sem(t % 2), 16)
                sp.dma_start(bm[:, t % 2], bsrc[t].to_broadcast([P, 512])).then_inc(w_in.sem(t % 2), 16)

            def load_first(n):
                if n >= 2:
                    sp.wait_ge(raw_low.sem, raw_low.at(n - 2))
                c, ks = halves[n]
                sp.dma_start(raw[:, n % 2], w_src[:, ks, c * 512:(c + 1) * 512]).then_inc(raw_in.sem(n % 2), 16)
            load_mod(0)
            load_mod(1)
            for t in range(2, NMOD):
                load_first(2 * t - 4)
                load_first(2 * t - 3)
                load_mod(t)
            load_first(4)
            load_first(5)

        @block.gpsimd
        def _(pool):
            nc.gpsimd.memset(g["neghalf"][:], -0.5)
            for count, at in EPS_OF.items():
                nc.gpsimd.memset(g["eps"][:, at:at + 4], count * EPS)

        @block.scalar
        def _(act):
            act.wait_ge(c_in.sem(0), c_in.at(0))
            nc.scalar.activation(csil[:], ccol[:], ACT.Silu).then_inc(silu.sem, 1)
            for n, (c, ks) in enumerate(halves):
                act.wait_ge(raw_in.sem(n % 2), raw_in.at(n // 2))
                nc.scalar.activation(g["w_high"][:, c, ks], raw[:, n % 2], ACT.Copy).then_inc(raw_high.sem, 1)

        @block.tensor
        def _(pe):
            pe.sem_inc(row_acc.sem, row_acc.credit)
            pe.wait_ge(spread.sem, spread.at(0))

            for t, use, s in pairs(pe, 0, NMOD):
                pe.wait_ge(w_in.sem(s), w_in.at(use))
                pe.wait_ge(row.sem, row.at(t - 2))
                for k in range(KD):
                    m = nc.tensor.matmul(acc[:, s], both[:, k], wm[:, s, k], start=(k == 0), stop=(k == KD - 1))
                m.then_inc(row_acc.sem, 1)
            pe.wait_ge(row.sem, row.at(NMOD - 1))
            pe.wait_ge(n_in.sem(0), n_in.at(0))
            for b in range(16):
                m = nc.tensor.transpose(colT[:, b // 4, b % 4], shift_scale[:, b * P:(b + 1) * P], g["ident"][:, :])
            m.then_inc(cols_t.sem, 1)

        @block.vector
        def _(dve):
            dve.sem_inc(row.sem, row.credit)
            dve.wait_ge(silu.sem, silu.at(0))
            nc.vector.tensor_copy(both[:, :, 0:64], csil[:, 0, :, None].to_broadcast([P, KD, 64])).then_inc(spread.sem, 1)
            nc.vector.tensor_copy(both[:, :, 64:P], csil[:, 1, :, None].to_broadcast([P, KD, 64])).then_inc(spread.sem, 1)

            def low(n):
                c, ks = halves[n]
                dve.wait_ge(raw_high.sem, raw_high.at(n))
                nc.vector.tensor_tensor(g["w_low"][:, c, ks], raw[:, n % 2], g["w_high"][:, c, ks].bitcast(F32), ALU.subtract).then_inc(raw_low.sem, 1)
            for t, splits in enumerate(((0,), (1, 2), (3,), ())):
                dve.wait_ge(row_acc.sem, row_acc.at(t))
                dve.wait_ge(w_in.sem(t % 2), w_in.at(t // 2))
                nc.vector.tensor_tensor(shift_scale[:, t * 512:(t + 1) * 512], acc[:, t % 2], bm[:, t % 2], ALU.add).then_inc(row.sem, 1)
                for n in splits:
                    low(n)
            dve.wait_ge(n_in.sem(0), n_in.at(0))
            dve.wait_ge(row.sem, row.at(NMOD - 1))
            dve.wait_ge(cols_t.sem, cols_t.at(0))
            nc.vector.tensor_copy(g["cols"][:, 0], colT[:, 0:2, :, 0:65:64].rearrange("p a b c -> p (a b) c"))
            nc.vector.tensor_copy(g["cols"][:, 1], colT[:, 2:4, :, 0:65:64].rearrange("p a b c -> p (a b) c")).then_inc(fin.sem, 1)
            dve.wait_ge(fin.sem, fin.at(0))
            nc.vector.scalar_tensor_tensor(out=g["cols"][:, 1], in0=g["cols"][:, 1], scalar=1.0,
                                           in1=ncol[:, :, None].to_broadcast([P, KD, 2]), op0=ALU.add, op1=ALU.mult)
            low(4)
            low(5)


def rstd_root(nc, g, pool, eps_added, turn, n, out, ssq, count):
    w = out.shape[-1]
    nc.gpsimd.tensor_tensor(out, ssq, g["eps"][:, EPS_OF[count]:EPS_OF[count] + w], ALU.add).then_inc(eps_added.sem, 1)
    pool.wait_ge(eps_added.sem, eps_added.at(turn, n))
    return nc.gpsimd.tensor_tensor(out, out, g["neghalf"][:, 0:w], ALU.pow)


def projection(nc, kit, io, g, dram):
    NGR = NT // 2
    HALF = KD * 512 // 2
    NB = 6
    SPLIT = ("g", "dt", "z", "ch0", "ch1")
    COLUMN = {"q": 0, "k": 1, "v": 2, "g": 3, "z": 4, "ch0": 5, "ch1": 6, "dt": 7}
    PLACE = {"q": 0, "k": 1, "v": 2, "g": 3, "z": 0, "ch0": 1, "ch1": 2}
    LEAVES = {"z": 2, "ch0": 4, "ch1": 6}
    PIECES = [(c, ks) for c in SPLIT for ks in ([slice(0, KD)] if c == "dt" else [slice(k, k + 2) for k in range(0, KD, 2)])]
    LAST = {c: n for n, (c, _) in enumerate(PIECES)}
    OUTS = ([(c, j) for c in ("q", "k", "v") for j in range(2)],
            [(c, j) for c in ("g", "z", "ch0", "ch1") for j in range(2)] + [("dt", 0)])
    DVE_TAKES = ([c in "qk" for c, _ in OUTS[0]], [c[:2] == "ch" and j == 0 for c, j in OUTS[1]])
    TURN_X = ({2: 0, 4: 1}, {4: 0, 6: 1})
    SKIPPED = (2, 4)

    def ordinal(p, o):
        return sum(1 for q in range(o + 1) if DVE_TAKES[p][q] == DVE_TAKES[p][o])

    with ExitStack() as st:
        wh, wl = g["w_high"], g["w_low"]
        dh = kit.sb("w_dt_high", [P, KD, 16], F32R, stack=st)
        dl = kit.sb("w_dt_low", [P, KD, 16], F32R, stack=st)
        xt = kit.sb("xt", [P, 2, D], stack=st)
        xn = kit.sb("xn", [P, 2, D], stack=st)
        hh = kit.sb("hT_high", [P, 2, KD, 2 * P], F32R, stack=st)
        hl = kit.sb("hT_low", [P, 2, KD, 2 * P], F32R, stack=st)
        hraw = kit.sb("hT_whole", [P, KD, P], stack=st)
        rope = kit.sb("rope", [P, 2, 4, P], stack=st)
        tok = kit.sb("tok", [P, 2, 3 * 512], stack=st)
        ch = kit.sb("ch", [P, NCH, 2 * P], stack=st)
        raw = ch[:].rearrange("p c t -> p (c t)").rearrange("p (s f) -> p s f", s=2)
        ra = kit.sb("rope_sine_part", [P, 512], stack=st)
        stat = kit.sb("stat", [P, 2, 2], stack=st)
        xT = kit.ps("xT", [P, KD, P], st)
        acc = kit.ps("proj_acc", [P, NB, 512], st)
        w_in = kit.landing("w_in_in", 2)
        x_in = kit.landing("x_in", 2)
        rope_in = kit.landing("rope_in", 2)
        tok_out = kit.landing("tok_out", 2, credit=16)
        ch_out = kit.landing("ch_out", 1, credit=16)
        whs = kit.counter("w_high_ready")
        wls = kit.counter("w_low_ready")
        ssq = kit.counter("x_ssq", 2)
        rstd = kit.counter("x_rstd", 2)
        eps_added = kit.counter("x_eps_added", 2)
        xnorm = kit.counter("x_normed", 2, credit=2)
        xTd = kit.counter("x_transposed", 2, credit=2)
        hTm = kit.counter("hT_modulated", 2, credit=2)
        hTh = kit.counter("hT_high_ready", 2)
        hTl = kit.counter("hT_low_ready", 2, credit=2)
        accd = [kit.counter(f"proj_acc_ready{p}", len(OUTS[p]), credit=len(OUTS[p])) for p in range(2)]
        rtmp = kit.counter("rope_products", 4, credit=2)
        edve = [kit.counter(f"proj_out_dve{p}", sum(DVE_TAKES[p]), credit=sum(DVE_TAKES[p])) for p in range(2)]
        eact = [kit.counter(f"proj_out_act{p}", len(OUTS[p]) - sum(DVE_TAKES[p]), credit=len(OUTS[p]) - sum(DVE_TAKES[p])) for p in range(2)]
        block = st.enter_context(nc.Block())

        def turns(eng, body, between=None):
            body(0, 0, 0, 0, True, False)
            with eng.Fori(0, NGR // 2) as i:
                for s in range(2):
                    t = i * 2 + (1 + s)
                    body(t, 0, t, 1 - s, False, False)
            if between:
                between()
            with eng.Fori(0, NGR // 2 - 1) as i:
                for s in range(2):
                    body(i * 2 + (NGR + s), 1, i * 2 + s, 1 - s, False, False)
            body(2 * NGR - 3, 1, NGR - 3, 1, False, False)
            body(2 * NGR - 2, 1, NGR - 2, 0, False, True)
            body(2 * NGR - 1, 1, NGR - 1, 1, True, None)

        def piece(n):
            c, ks = PIECES[n]
            if c == "dt":
                return raw[:, n % 2, 0:KD * 16].rearrange("p (k f) -> p k f", k=KD), dh[:], dl[:]
            return raw[:, n % 2].rearrange("p (k f) -> p k f", k=2), wh[:, PLACE[c], ks], wl[:, PLACE[c], ks]

        def number(p, o, ctx):
            return o + 1 - (SKIPPED[p] if ctx and p else 0)

        def taken(p, o, ctx):
            skipped = sum(1 for q in range(SKIPPED[p]) if DVE_TAKES[p][q] == DVE_TAKES[p][o]) if ctx and p else 0
            return ordinal(p, o) - skipped

        @block.sync
        def _(sp):
            xsrc = io["x"].rearrange("o (t p) d -> (o t) p d", p=P)
            wsrc = io["w_in"].rearrange("o (k p) f -> p (o k) f", p=P)

            def load_x(t, pair):
                for j in range(2):
                    sp.wait_ge(xnorm.sem, xnorm.at(t - 1, j + 1))
                    src = io["ctx"][0, j * P:(j + 1) * P, :] if pair is None else tile_of(xsrc, pair * 2 + j)
                    sp.dma_start(xt[:, j], src).then_inc(x_in.sem(j), 16)

            def load_w(chunk):
                for n, (c, ks) in enumerate(PIECES):
                    if c != chunk:
                        continue
                    if n >= 2:
                        sp.wait_ge(wls.sem, wls.at(n - 2))
                    if c in LEAVES:
                        sp.wait_ge(accd[0].sem, accd[0].at(NGR - 1, LEAVES[c]))
                    c0 = DPROJ - 16 if c == "dt" else COLUMN[c] * 512
                    sp.dma_start(piece(n)[0], wsrc[:, ks, c0:c0 + (16 if c == "dt" else 512)]).then_inc(w_in.sem(n % 2), 16)

            def load_rope(t):
                for j in range(2):
                    sp.wait_ge(edve[0].sem, edve[0].at(t - 1))
                    sp.dma_start(rope[:, j].rearrange("p a b -> p (a b)"), tile_of(io["rope"], t * 2 + j)).then_inc(rope_in.sem(j), 16)

            def store(p, turn, pair, ctx):
                if ctx and p:
                    sp.wait_ge(edve[p].sem, edve[p].at(turn, taken(p, 6, ctx)))
                    sp.wait_ge(eact[p].sem, eact[p].at(turn, taken(p, 8, ctx)))
                else:
                    sp.wait_ge(edve[p].sem, edve[p].at(turn))
                    sp.wait_ge(eact[p].sem, eact[p].at(turn))
                if p:
                    sp.dma_start(dram["ch"][:, :, bass.ds(pair * (2 * P), 2 * P)].rearrange("c p t -> p c t"), ch[:]).then_inc(ch_out.sem(0), 16)
                first = (0, 3 * 512)[p]
                lo, hi = (SKIPPED[p] * 256 if ctx else 0), (3 * 512, 2 * 512 + 16)[p]
                for j in range(2):
                    sp.dma_start(tile_of(dram["tok"], pair * 2 + j, first + lo, first + hi), tok[:, j, lo:hi]).then_inc(tok_out.sem(j), 16)

            for j in range(2):
                sp.sem_inc(tok_out.sem(j), tok_out.credit)
            sp.sem_inc(ch_out.sem(0), ch_out.credit)
            load_x(0, None)
            load_rope(0)
            load_x(1, 0)
            for c in ("g", "dt"):
                load_w(c)
            store(0, 0, 0, True)
            with sp.Fori(1, NGR - 1) as t:
                load_rope(t)
                load_x(t + 1, t)
                store(0, t, t, False)
            load_rope(NGR - 1)
            load_x(NGR, 0)
            for c in LEAVES:
                load_w(c)
            store(0, NGR - 1, NGR - 1, False)
            with sp.Fori(0, NGR - 2) as t:
                load_x(t + (NGR + 1), t + 1)
                store(1, t, t + 1, False)
            load_x(2 * NGR - 1, None)
            store(1, NGR - 2, NGR - 1, False)
            store(1, NGR - 1, 0, True)
            for j in range(2):
                sp.wait_ge(tok_out.sem(j), tok_out.at(2 * NGR - 1))
            sp.wait_ge(ch_out.sem(0), ch_out.at(NGR - 1))

        @block.gpsimd
        def _(pool):
            with pool.Fori(0, 2 * NGR) as t:
                for j in range(2):
                    pool.wait_ge(ssq.sem, ssq.at(t, j + 1))
                    rstd_root(nc, g, pool, eps_added, t, j + 1, stat[:, j, 1:2], stat[:, j, 0:1], D).then_inc(rstd.sem, 1)

        @block.scalar
        def _(act):
            for p in range(2):
                act.sem_inc(eact[p].sem, eact[p].credit)
            act.sem_inc(hTm.sem, hTm.credit)

            def square(t, j):
                act.wait_ge(x_in.sem(j), x_in.at(t))
                act.wait_ge(xTd.sem, xTd.at(t - 1, j + 1))
                nc.scalar.activation(xn[:, j], xt[:, j], ACT.Square, accum_out=stat[:, j, 0:1]).then_inc(ssq.sem, 1)

            def modulate(t, s, j, ctx):
                act.wait_ge(xTd.sem, xTd.at(t, j + 1))
                act.wait_ge(hTl.sem, hTl.at(t, j) if j else hTl.at(t - 1))
                c = 1 if ctx else 0
                span = slice(j * P, (j + 1) * P)
                for k in range(KD):
                    m = nc.scalar.activation(hraw[:, k], xT[:, k], ACT.Identity,
                                             bias=g["cols"][:, 0, k, c:c + 1], scale=g["cols"][:, 1, k, c:c + 1])
                m.then_inc(hTm.sem, 1)
                act.wait_ge(hTm.sem, hTm.at(t, j + 1))
                nc.scalar.activation(hh[:, s, :, span], hraw[:], ACT.Copy).then_inc(hTh.sem, 1)

            def high(chunk):
                for n, (c, ks) in enumerate(PIECES):
                    if c == chunk:
                        act.wait_ge(w_in.sem(n % 2), w_in.at(n // 2))
                        nc.scalar.activation(piece(n)[1], piece(n)[0], ACT.Copy).then_inc(whs.sem, 1)

            def body(t, p, turn, s, ctx, following):
                if following is not None:
                    for j in range(2):
                        square(t + 1, j)
                for o, (c, j) in enumerate(OUTS[p]):
                    if not (DVE_TAKES[p][o] or ctx and o < SKIPPED[p]):
                        act.wait_ge(accd[p].sem, accd[p].at(turn, number(p, o, ctx)))
                        if c[:2] == "ch":
                            act.wait_ge(ch_out.sem(0), ch_out.at(turn - 1))
                            b = 4 * int(c[2]) + 2 * j
                            m = nc.scalar.activation(ch[:, b:b + 2], acc[:, o % NB].rearrange("p (a b) -> p a b", a=2), ACT.Copy)
                        elif c == "dt":
                            for jj in range(2):
                                act.wait_ge(tok_out.sem(jj), tok_out.at(t - 1))
                            m = nc.scalar.activation(tok[:, :, 1024:1040], acc[:, o % NB, 0:32].rearrange("p (a b) -> p a b", a=2), ACT.Copy)
                        else:
                            act.wait_ge(tok_out.sem(j), tok_out.at(t - 1))
                            at = {"v": 1024, "g": 0, "z": 512}[c]
                            m = nc.scalar.activation(tok[:, j, at:at + 512], acc[:, o % NB], ACT.Copy if c == "v" else ACT.Silu)
                        m.then_inc(eact[p].sem, 1)
                    if following is not None and o in TURN_X[p]:
                        modulate(t + 1, 1 - s, TURN_X[p][o], following)
                if ctx and p == 0:
                    for c in ("g", "dt"):
                        high(c)

            for j in range(2):
                square(0, j)
            for j in range(2):
                modulate(0, 0, j, True)
            turns(act, body, lambda: [high(c) for c in LEAVES])

        @block.tensor
        def _(pe):
            pe.sem_inc(xTd.sem, xTd.credit)
            for p in range(2):
                pe.sem_inc(accd[p].sem, accd[p].credit + (0 if p else SKIPPED[0]))

            def turn_x(t, j):
                pe.wait_ge(xnorm.sem, xnorm.at(t, j + 1))
                pe.wait_ge(hTm.sem, hTm.at(t, j) if j else hTm.at(t - 1, 2))
                for k in range(KD):
                    m = nc.tensor.transpose(xT[:, k], xn[:, j, k * P:(k + 1) * P], g["ident"][:, :])
                m.then_inc(xTd.sem, 1)

            def free(p, turn, o, ctx):
                same = o >= NB and not (ctx and p)
                q = o - NB if same else (o + NB if p and not ctx and o + NB < len(OUTS[p]) else o)
                e = edve[p] if DVE_TAKES[p][q] else eact[p]
                pe.wait_ge(e.sem, e.at(turn, ordinal(p, q)) if same else e.at(turn - 1, ordinal(p, q)))

            def products(t, p, turn, s, ctx, o):
                c, j = OUTS[p][o]
                bank = acc[:, o % NB]
                if c in LAST:
                    pe.wait_ge(wls.sem, wls.at(LAST[c]))
                if c[:2] == "ch":
                    for b in range(2):
                        w = slice((2 * j + b) * P, (2 * j + b + 1) * P)
                        for k in range(KD):
                            for n, (a, h) in enumerate(((wh, hh), (wh, hl), (wl, hh))):
                                m = nc.tensor.matmul(bank[:, b * 2 * P:(b + 1) * 2 * P], a[:, PLACE[c], k, w], h[:, s, k], start=(k == 0 and n == 0), stop=(k == KD - 1 and n == 2))
                    return m
                for jj in (range(2) if c == "dt" else (j,)):
                    span = slice(jj * P, (jj + 1) * P)
                    for k in range(KD):
                        for n, (h, high_) in enumerate(((hh, True), (hh, False), (hl, True))):
                            if c == "dt":
                                m = nc.tensor.matmul(bank[:, jj * 16:(jj + 1) * 16], h[:, s, k, span], (dh if high_ else dl)[:, k], start=(k == 0 and n == 0), stop=(k == KD - 1 and n == 2))
                            else:
                                m = nc.tensor.matmul(bank, h[:, s, k, span], (wh if high_ else wl)[:, PLACE[c], k], start=(k == 0 and n == 0), stop=(k == KD - 1 and n == 2))
                return m

            def body(t, p, turn, s, ctx, following):
                pe.wait_ge(hTl.sem, hTl.at(t))
                for o in range(len(OUTS[p])):
                    if not (ctx and o < SKIPPED[p]):
                        free(p, turn, o, ctx)
                        products(t, p, turn, s, ctx, o).then_inc(accd[p].sem, 1)
                    if following is not None and o in TURN_X[p]:
                        turn_x(t + 1, TURN_X[p][o])

            def between():
                pe.wait_ge(edve[0].sem, edve[0].at(NGR - 1))
                pe.wait_ge(eact[0].sem, eact[0].at(NGR - 1))
            for j in range(2):
                turn_x(0, j)
            turns(pe, body, between)

        @block.vector
        def _(dve):
            dve.sem_inc(xnorm.sem, xnorm.credit)
            for p in range(2):
                dve.sem_inc(edve[p].sem, edve[p].credit + (0 if p else SKIPPED[0]))
            dve.sem_inc(rtmp.sem, rtmp.credit)
            dve.sem_inc(hTl.sem, hTl.credit)

            def norm(t, j):
                dve.wait_ge(rstd.sem, rstd.at(t, j + 1))
                nc.vector.tensor_scalar(xn[:, j], xt[:, j], stat[:, j, 1:2], float(D) ** 0.5, ALU.mult, ALU.mult).then_inc(xnorm.sem, 1)

            def low_h(t, s, j):
                dve.wait_ge(hTh.sem, hTh.at(t, j + 1))
                part, high_ = (h[:, s, :, j * P:(j + 1) * P] for h in (hl, hh))
                nc.vector.tensor_tensor(part, hraw[:], high_.bitcast(F32), ALU.subtract).then_inc(hTl.sem, 1)

            def low(chunk):
                for n, (c, ks) in enumerate(PIECES):
                    if c == chunk:
                        whole, high_, low_ = piece(n)
                        dve.wait_ge(whs.sem, whs.at(n))
                        nc.vector.tensor_tensor(low_, whole, high_.bitcast(F32), ALU.subtract).then_inc(wls.sem, 1)

            def turned(t, turn, j, n, o):
                dve.wait_ge(rope_in.sem(j), rope_in.at(turn))
                dve.wait_ge(edve[0].sem, edve[0].at(turn, o) if o else edve[0].at(turn - 1))
                a = acc[:, o % NB].rearrange("p (h e q i) -> p h e q i", h=RH, e=2, q=2)
                sin = rope[:, j, 2 * n + 1].rearrange("p (e q i) -> p e q i", e=2, q=2)
                dve.wait_ge(tok_out.sem(j), tok_out.at(t - 1))
                to = tok[:, j, n * 512:(n + 1) * 512]
                nc.vector.tensor_tensor(to.rearrange("p (h f) -> p h f", h=RH), acc[:, o % NB].rearrange("p (h f) -> p h f", h=RH),
                                        rope[:, j, 2 * n].unsqueeze(1).to_broadcast([P, RH, P]), ALU.mult)
                b = ra[:].rearrange("p (h e q i) -> p h e q i", h=RH, e=2, q=2)
                for q in range(2):
                    m = nc.vector.tensor_tensor(b[:, :, :, q], a[:, :, :, 1 - q], sin[:, :, q].unsqueeze(1).to_broadcast([P, RH, 2, 32]), ALU.mult)
                m.then_inc(rtmp.sem, 1)
                dve.wait_ge(rtmp.sem, turn * 4 + (o + 1))
                nc.vector.tensor_tensor(to, to, ra[:], ALU.add).then_inc(edve[0].sem, 1)

            def body(t, p, turn, s, ctx, following):
                if following is not None:
                    for j in range(2):
                        norm(t + 1, j)
                for o, (c, j) in enumerate(OUTS[p]):
                    if DVE_TAKES[p][o] and not (ctx and o < SKIPPED[p]):
                        dve.wait_ge(accd[p].sem, accd[p].at(turn, number(p, o, ctx)))
                        if p == 0:
                            turned(t, turn, j, o // 2, o)
                        else:
                            dve.wait_ge(ch_out.sem(0), ch_out.at(turn - 1))
                            b = 4 * int(c[2]) + 2 * j
                            nc.vector.tensor_copy(ch[:, b:b + 2], acc[:, o % NB].rearrange("p (a b) -> p a b", a=2)).then_inc(edve[p].sem, 1)
                    if following is not None and o in TURN_X[p]:
                        low_h(t + 1, 1 - s, TURN_X[p][o])
                if ctx and p == 0:
                    for c in ("g", "dt"):
                        low(c)

            for j in range(2):
                norm(0, j)
            for j in range(2):
                low_h(0, 0, j)

            def between():
                for c in LEAVES:
                    low(c)
                dve.wait_ge(wls.sem, wls.at(len(PIECES) - 1))
            turns(dve, body, between)


def convolution(nc, kit, io, g, dram):
    NMOD = 8
    W = CTX + SEQ + 8
    LAT = CTX + 4
    NS = NT * SH
    with ExitStack() as st:
        u = kit.sb("cu", [P, 2, W], stack=st)
        v = kit.sb("cv", [P, 2, W], stack=st)
        cw = kit.sb("cw", [P, CONV, NCH], stack=st)
        cb = kit.sb("cb", [P, NCH], stack=st)
        raw = kit.sb("dt_raw", [P, NT, 2, SH], stack=st)
        bias = kit.sb("dt_bias", [P, 2, SH], stack=st)
        alog = kit.sb("a_log", [P, 2, SH], stack=st)
        y = kit.sb("dt_y", [P, NT, 2, SH], stack=st)
        z = kit.sb("dt_z", [P, NT, 2, SH], stack=st)
        r = kit.sb("dt_r", [P, NT, 2, SH], stack=st)
        dt = kit.sb("dt_dt", [P, NT, 2, SH], stack=st)
        da = kit.sb("dt_da", [P, 2, NT, SH], stack=st)
        rel = kit.sb("rel", [P, 4, P], stack=st)
        relk = kit.sb("relk", [P, 2], stack=st)
        lg = kit.sb("lg", [P, 2, RH], stack=st)
        dec = kit.sb("ret_decay", [P, 2, RH], stack=st)
        lat = kit.sb("c_lat", [P, KD, P], stack=st)
        wm = kit.sb("wm_rest", [P, 2, KD, 512], stack=st)
        bm = kit.sb("bm_rest", [P, NMOD * 512], stack=st)
        nrow = kit.sb("nrow", [P, 3, D], stack=st)
        acc = kit.ps("dt_sums", [P, 2, 512], st)
        rows = kit.ps("mod_rows", [P, 2, 512], st)
        m_in = kit.landing("mod_small_in", dmas=4)
        wm_in = kit.landing("wmod_rest_in", 2)
        spread = kit.counter("c_lat_spread")
        mrow = kit.counter("mod_rest_acc", 1, credit=2)
        mcopy = kit.counter("mod_rest_left", 1, credit=2)
        gained = kit.counter("mod_rest_gained", 8)
        small_in = kit.landing("conv_small_in", dmas=18)
        raw_in = kit.landing("dt_raw_in")
        u_in = kit.landing("conv_in", 2, dmas=2)
        u_out = kit.landing("conv_out", 2, dmas=2, credit=32)
        padded = kit.counter("conv_padded", 6)
        tap = kit.counter("conv_tap", CONV, credit=CONV)
        silu = kit.counter("conv_silu", 1, credit=1)
        dstep = kit.counter("dt_step", 20)
        dact = kit.counter("dt_act", 4)
        sums = kit.counter("dt_sums_ready")
        tabs = kit.counter("decay_tables", 5)
        block = st.enter_context(nc.Block())

        @block.sync
        def _(sp):
            for s in range(2):
                sp.sem_inc(u_out.sem(s), u_out.credit)
            one = small_in.sem(0)
            for k in range(CONV):
                sp.dma_start(cw[:, k], io["ssd_conv_w"][0, k, :].rearrange("(c p) -> p c", p=P), allow_slow_non_contiguous=True).then_inc(one, 16)
            sp.dma_start(cb[:], io["ssd_conv_b"].rearrange("o (c p) -> p (o c)", p=P), allow_slow_non_contiguous=True).then_inc(one, 16)
            for n, d in enumerate("fb"):
                sp.dma_start(bias[:, n], io[f"ssd_dt_bias_{d}"].to_broadcast([P, SH])).then_inc(one, 16)
                sp.dma_start(alog[:, n], io[f"ssd_a_log_{d}"].to_broadcast([P, SH])).then_inc(one, 16)
                sp.dma_start(dec[:, n], io[f"ret_decay_{d}"].to_broadcast([P, RH])).then_inc(one, 16)
            sp.dma_start(g["tri"][:], io["tri"]).then_inc(one, 16)
            sp.dma_start(rel[:], io["rel"]).then_inc(one, 16)
            sp.dma_start(relk[:], io["relk"]).then_inc(one, 16)
            sp.dma_start(g["dskip"][:], io["ssd_d"].to_broadcast([P, SH])).then_inc(one, 16)
            sp.dma_start(g["wn"][:, 0:4], io["ret_gn_w"].rearrange("o (k p) -> p (o k)", p=P), allow_slow_non_contiguous=True).then_inc(one, 16)
            sp.dma_start(g["wn"][:, 4:8], io["ssd_norm_w"].rearrange("o (k p) -> p (o k)", p=P), allow_slow_non_contiguous=True).then_inc(one, 16)
            sp.dma_start(raw[:].rearrange("p t d h -> p t (d h)"), dram["tok"][:, :, 5 * 512:NTOK].rearrange("t p f -> p t f")).then_inc(raw_in.sem(0), 16)
            sp.wait_ge(padded.sem, padded.at(0))

            def load(t, use, s):
                sp.wait_ge(tap.sem, tap.at(t - 2 + 1, 0))
                src = tile_of(dram["ch"], t)
                sp.dma_start(u[:, s, 2:2 + CTX], src[:, 0:CTX]).then_inc(u_in.sem(s), 16)
                sp.dma_start(u[:, s, LAT + 2:LAT + 2 + SEQ], src[:, CTX:CTX + SEQ]).then_inc(u_in.sem(s), 16)

            def store(t, use, s):
                sp.wait_ge(silu.sem, silu.at(t))
                dst = tile_of(dram["u"], t)
                sp.dma_start(dst[:, 0:CTX], v[:, s, 2:2 + CTX]).then_inc(u_out.sem(s), 16)
                sp.dma_start(dst[:, CTX:CTX + SEQ], v[:, s, LAT + 2:LAT + 2 + SEQ]).then_inc(u_out.sem(s), 16)

            for s in range(2):
                src = tile_of(dram["ch"], s)
                sp.dma_start(u[:, s, 2:2 + CTX], src[:, 0:CTX]).then_inc(u_in.sem(s), 16)
                sp.dma_start(u[:, s, LAT + 2:LAT + 2 + SEQ], src[:, CTX:CTX + SEQ]).then_inc(u_in.sem(s), 16)
            with sp.Fori(0, NCH // 2 - 1) as i:
                for s in range(2):
                    store(i * 2 + s, i, s)
                    load(i * 2 + (s + 2), i, s)
            for s in range(2):
                store(NCH - 2 + s, NCH // 2 - 1, s)
                sp.wait_ge(u_out.sem(s), u_out.at(NCH // 2 - 1))

        @block.gpsimd
        def _(pool):
            for s in range(2):
                for a, b in ((0, 2), (CTX + 2, LAT + 2), (W - 2, W)):
                    nc.gpsimd.memset(u[:, s, a:b], 0.0).then_inc(padded.sem, 1)
            pool.wait_ge(small_in.sem(0), small_in.at(0))
            pool.wait_ge(raw_in.sem(0), raw_in.at(0))
            for n, src in enumerate(("norm_post_mix", "norm_pre_ffn", "norm_post_ffn")):
                pool.dma_start(nrow[:, n, :], io[src].to_broadcast([P, D])).then_inc(m_in.sem(0), 16)
            pool.dma_start(bm[:], io["b_mod"][:, 4 * 512:].to_broadcast([P, NMOD * 512])).then_inc(m_in.sem(0), 16)
            wsrc = io["w_mod"].rearrange("o (k p) (n f) -> n p (o k) f", p=P, f=512)
            for t in range(2):
                pool.dma_start(wm[:, t], wsrc[t + 4]).then_inc(wm_in.sem(t), 16)
            pool.wait_ge(m_in.sem(0), m_in.at(0))
            nc.gpsimd.tensor_scalar(nrow[:], nrow[:], float(D) ** 0.5, None, ALU.mult).then_inc(gained.sem, 1)
            pool.wait_ge(gained.sem, 1)
            done = 1
            for t in range(NMOD):
                if t + 2 < NMOD:
                    pool.wait_ge(mrow.sem, mrow.at(t))
                    pool.dma_start(wm[:, t % 2], wsrc[t + 6]).then_inc(wm_in.sem(t % 2), 16)
                pool.wait_ge(mcopy.sem, mcopy.at(t))
                row, half = t // 2, slice(t % 2 * 512, (t % 2 + 1) * 512)
                part = g["mod"][:, row, half]
                nc.gpsimd.tensor_tensor(part, part, bm[:, t * 512:(t + 1) * 512], ALU.add).then_inc(gained.sem, 1)
                done += 1
                if row == 2:
                    pool.wait_ge(gained.sem, done)
                    nc.gpsimd.tensor_scalar(part, part, 1.0, None, ALU.add).then_inc(gained.sem, 1)
                    done += 1
                if row != 1:
                    pool.wait_ge(gained.sem, done)
                    nc.gpsimd.tensor_tensor(part, part, nrow[:, {0: 0, 2: 1, 3: 2}[row], half], ALU.mult).then_inc(gained.sem, 1)
                    done += 1

        @block.tensor
        def _(pe):
            pe.sem_inc(mrow.sem, mrow.credit)
            pe.wait_ge(small_in.sem(0), small_in.at(0))
            pe.wait_ge(dstep.sem, 15)
            for d, tris in enumerate(((0, 1, 4), (2, 3, 4))):
                for n, tri in enumerate(tris):
                    m = nc.tensor.matmul(acc[:, d, n * NS:(n + 1) * NS], g["tri"][:, tri], da[:, d].rearrange("p t h -> p (t h)"), start=True, stop=True)
            m.then_inc(sums.sem, 1)
            pe.wait_ge(spread.sem, spread.at(0))
            for t, use, s in pairs(pe, 0, NMOD):
                pe.wait_ge(wm_in.sem(s), wm_in.at(use))
                pe.wait_ge(mcopy.sem, mcopy.at(t - 2))
                for k in range(KD):
                    m = nc.tensor.matmul(rows[:, s], lat[:, k], wm[:, s, k], start=(k == 0), stop=(k == KD - 1))
                m.then_inc(mrow.sem, 1)

        @block.scalar
        def _(act):
            act.sem_inc(silu.sem, silu.credit)
            act.sem_inc(mcopy.sem, mcopy.credit)
            nc.scalar.activation(lat[:], g["csil"][:, 0, :, None].to_broadcast([P, KD, P]), ACT.Copy).then_inc(spread.sem, 1)
            act.wait_ge(dstep.sem, 1)
            nc.scalar.activation(z[:], y[:], ACT.Abs).then_inc(dact.sem, 1)
            act.wait_ge(dact.sem, 1)
            nc.scalar.activation(r[:], z[:], ACT.Exp, scale=-1.0).then_inc(dact.sem, 1)
            act.wait_ge(small_in.sem(0), small_in.at(0))
            nc.scalar.activation(alog[:], alog[:], ACT.Exp).then_inc(dact.sem, 1)
            nc.scalar.activation(dec[:], dec[:], ACT.Exp).then_inc(dact.sem, 1)
            act.wait_ge(sums.sem, sums.at(0))
            for d in range(2):
                m = nc.scalar.activation(g["E"][:, :, 3 * d:3 * d + 3, :].rearrange("p t k h -> p k t h"),
                                         acc[:, d, 0:3 * NS].rearrange("p (k t h) -> p k t h", k=3, t=NT), ACT.Exp)
            m.then_inc(tabs.sem, 1)
            act.wait_ge(dstep.sem, 21)
            nc.scalar.activation(g["DT"][:], g["DT"][:], ACT.Exp)
            for h in range(RH):
                nc.scalar.activation(g["Dq"][:, 0, h], rel[:, 2], ACT.Exp, scale=lg[:, 0, h:h + 1])
                nc.scalar.activation(g["Dq"][:, 1, h], rel[:, 3], ACT.Exp, scale=lg[:, 1, h:h + 1])
            for d in range(2):
                nc.scalar.activation(g["Dk"][:, d], lg[:, d], ACT.Exp, scale=relk[:, d:d + 1])
                nc.scalar.activation(g["Dtot"][:, d], lg[:, d], ACT.Exp, scale=float(P)).then_inc(tabs.sem, 1)
            with act.Fori(0, NCH // 2) as i:
                for s in range(2):
                    t = i * 2 + s
                    act.wait_ge(mrow.sem, mrow.at(t))
                    nc.scalar.activation(g["mod"][:].rearrange("p a b -> p (a b)")[:, bass.ds(t * 512, 512)], rows[:, s], ACT.Copy).then_inc(mcopy.sem, 1)
                    act.wait_ge(tap.sem, tap.at(t))
                    act.wait_ge(u_out.sem(s), i * 32 + 32)
                    nc.scalar.activation(v[:, s, 2:W - 2], v[:, s, 2:W - 2], ACT.Silu).then_inc(silu.sem, 1)

        @block.vector
        def _(dve):
            dve.sem_inc(tap.sem, tap.credit)
            dve.wait_ge(small_in.sem(0), small_in.at(0))
            dve.wait_ge(raw_in.sem(0), raw_in.at(0))
            count = [0]

            def step(ins):
                count[0] += 1
                ins.then_inc(dstep.sem, 1)
                dve.wait_ge(dstep.sem, count[0])

            step(nc.vector.tensor_tensor(y[:], raw[:], bias[:].unsqueeze(1).to_broadcast([P, NT, 2, SH]), ALU.add))
            dve.wait_ge(dact.sem, 2)
            step(nc.vector.tensor_scalar(z[:], r[:], 2.0, None, ALU.add))
            step(nc.vector.reciprocal(z[:], z[:]))
            step(nc.vector.tensor_tensor(z[:], z[:], r[:], ALU.mult))
            step(nc.vector.tensor_tensor(raw[:], z[:], z[:], ALU.mult))
            step(nc.vector.tensor_scalar(r[:], raw[:], 1.0 / 15, None, ALU.mult))
            for k in range(6, 0, -1):
                step(nc.vector.scalar_tensor_tensor(out=r[:], in0=r[:], scalar=1.0 / (2 * k + 1), in1=raw[:], op0=ALU.add, op1=ALU.mult))
            step(nc.vector.scalar_tensor_tensor(out=r[:], in0=r[:], scalar=1.0, in1=z[:], op0=ALU.add, op1=ALU.mult))
            nc.vector.tensor_scalar(y[:], y[:], 0.0, None, ALU.max)
            dve.wait_ge(dact.sem, 4)
            step(nc.vector.tensor_scalar(alog[:], alog[:], -1.0, None, ALU.mult))
            dve.wait_ge(dstep.sem, count[0])
            nc.vector.scalar_tensor_tensor(out=dt[:], in0=r[:], scalar=2.0, in1=y[:], op0=ALU.mult, op1=ALU.add).then_inc(tabs.sem, 1)
            dve.wait_ge(tabs.sem, 1)
            step(nc.vector.tensor_tensor(da[:].rearrange("p d t h -> p t d h"), dt[:], alog[:].unsqueeze(1).to_broadcast([P, NT, 2, SH]), ALU.mult))
            dd = g["dd"]
            nc.vector.tensor_tensor(dd[:, :, 0], dt[:, :, 0], dt[:, :, 1], ALU.subtract)
            nc.vector.tensor_copy(dd[:, :, 1], dt[:, :, 1])
            nc.vector.tensor_copy(dd[:, :, 2:4], da[:].rearrange("p d t h -> p t d h"))
            step(nc.vector.tensor_scalar(lg[:], dec[:], -1.0, None, ALU.mult))
            for h in range(RH):
                step(nc.vector.tensor_scalar(g["DT"][:, h], rel[:, 1], lg[:, 1, h:h + 1], None, ALU.mult))
            for h in range(RH):
                last = nc.vector.scalar_tensor_tensor(out=g["DT"][:, h], in0=rel[:, 0], scalar=lg[:, 0, h:h + 1], in1=g["DT"][:, h], op0=ALU.mult, op1=ALU.add)
            step(last)
            dve.wait_ge(tabs.sem, 2)
            for d in range(2):
                w = g["E"][:, :, 3 * d + 1, :]
                m = nc.vector.tensor_tensor(w, w, dt[:, :, d], ALU.mult)
            m.then_inc(tabs.sem, 1)
            with dve.Fori(0, NCH // 2) as i:
                for s in range(2):
                    t = i * 2 + s
                    dve.wait_ge(u_in.sem(s), u_in.at(i))
                    dve.wait_ge(u_out.sem(s), i * 32 + 32)
                    n = W - 4
                    for k in range(CONV):
                        wk = conv_w(cw, t, k)
                        if k == 0:
                            nc.vector.tensor_scalar(v[:, s, 2:2 + n], u[:, s, 0:n], wk, conv_w(cb, t, None), ALU.mult, ALU.add).then_inc(tap.sem, 1)
                        else:
                            dve.wait_ge(tap.sem, tap.at(t, k))
                            nc.vector.scalar_tensor_tensor(out=v[:, s, 2:2 + n], in0=u[:, s, k:k + n], scalar=wk, in1=v[:, s, 2:2 + n], op0=ALU.mult, op1=ALU.add).then_inc(tap.sem, 1)


def conv_w(w, t, k):
    if k is None:
        return w[:, bass.ds(t, 1)]
    return w[:, k, bass.ds(t, 1)]


def heads(v, n):
    return v.unsqueeze(2).to_broadcast([P, v.shape[1], n])


def tile_row(t4, t, k):
    return t4[:, bass.ds(t, 1), k, :].rearrange("p o h -> p (o h)")


def states(nc, kit, io, g, dram):
    TURNS = NT + NCT
    with ExitStack() as st:
        kv = kit.sb("s_kv", [P, 4, D], stack=st)
        uc = kit.sb("s_u", [P, 4, 6, P], stack=st)
        kd = kit.sb("s_kd", [P, 2, 512], stack=st)
        xw = kit.sb("s_xw", [P, 2, 512], stack=st)
        bt = kit.sb("s_bt", [P, 2, SG * P], stack=st)
        sb = kit.sb("s_sb", [P, 2, 2, 512], stack=st)
        sd = kit.sb("s_sd", [P, 2, 512], stack=st)
        xT = kit.ps("s_xT", [P, 2, 512], st)
        bT = kit.ps("s_bT", [P, 2, 512], st)
        up = kit.ps("s_up", [P, 2, 2, 512], st)
        kv_in = kit.landing("s_kv_in", 4)
        u_in = kit.landing("s_u_in", 4)
        s_out = kit.landing("s_out", 2)
        turned = kit.counter("s_transposed", 2, credit=8)
        bts = kit.counter("s_b_ready", 1, credit=2)
        kds = kit.counter("s_k_decayed", 1, credit=4)
        xws = kit.counter("s_x_weighted", 1, credit=2)
        dec_r = kit.counter("s_ret_decayed")
        dec = kit.counter("s_ssd_decayed")
        ups = kit.counter("s_update_ready", 1, credit=4)
        news = kit.counter("s_state_ready", 2, credit=4)
        zero = kit.counter("s_zero")
        block = st.enter_context(nc.Block())

        def turns(eng, body):
            for t in range(NCT):
                body(t, (0, t), t // 2, t % 2, NCT - 1 - t, True, sb, False)
            with eng.Fori(0, NL // 4) as i:
                for q in range(4):
                    body(i * 4 + (NCT + q), (i + (NCT + q) // 4, (NCT + q) % 4), i * 2 + (1 + q // 2), q % 2, i * -4 + (NT - 1 - q), True, sb, True)
            for t in range(NT, TURNS):
                body(t, (t // 4, t % 4), t // 2, t % 2, t - NT, False, g["sf"], False)

        @block.sync
        def _(sp):
            def load(t, ring, use, s, tile, back, state, stored):
                n = ring[1]
                sp.wait_ge(ups.sem, ups.at(t - 4))
                sp.wait_ge(kds.sem, kds.at(t - 4))
                sp.dma_start(kv[:, n], tile_of(dram["tok"], tile, 512, 3 * 512)).then_inc(kv_in.sem(n), 16)
                sp.wait_ge(turned.sem, turned.at(t - 4))
                sp.dma_start(uc[:, n], dram["u"][0:6, :, bass.ds(tile * P, P)].rearrange("c p t -> p c t")).then_inc(u_in.sem(n), 16)
            turns(sp, load)

        @block.gpsimd
        def _(pool):
            pool.sem_inc(kds.sem, kds.credit)
            nc.gpsimd.memset(sb[:, 0], 0.0)
            nc.gpsimd.memset(g["sf"][:, 0], 0.0).then_inc(zero.sem, 1)
            pool.wait_ge(zero.sem, zero.at(0))

            def body(t, ring, use, s, tile, back, state, stored):
                pool.wait_ge(kv_in.sem(ring[1]), kv_in.at(ring[0]))
                pool.wait_ge(ups.sem, ups.at(t - 2))
                nc.gpsimd.tensor_tensor(kd[:, s].rearrange("p (h e) -> p h e", h=RH), kv[:, ring[1], 0:512].rearrange("p (h e) -> p h e", h=RH),
                                                heads(g["Dk"][:, int(back)], P), ALU.mult).then_inc(kds.sem, 1)
                pool.wait_ge(news.sem, news.at(t - 1, 1))
                nc.gpsimd.tensor_tensor(sd[:, 1].rearrange("p (h e) -> p h e", h=SH), state[:, s, 1].rearrange("p (h e) -> p h e", h=SH),
                                                heads(tile_row(g["E"], tile, 5 if back else 2), SP_), ALU.mult).then_inc(dec.sem, 1)
            turns(pool, body)

        @block.tensor
        def _(pe):
            pe.sem_inc(turned.sem, turned.credit)
            pe.sem_inc(ups.sem, ups.credit)

            def body(t, ring, use, s, tile, back, state, stored):
                pe.wait_ge(u_in.sem(ring[1]), u_in.at(ring[0]))
                pe.wait_ge(xws.sem, xws.at(t - 2))
                for c in range(4):
                    m = nc.tensor.transpose(xT[:, s, c * P:(c + 1) * P], uc[:, ring[1], c], g["ident"][:, :])
                m.then_inc(turned.sem, 1)
                pe.wait_ge(bts.sem, bts.at(t - 2))
                for c in range(SG):
                    m = nc.tensor.transpose(bT[:, s, c * P:(c + 1) * P], uc[:, ring[1], 4 + c], g["ident"][:, :])
                m.then_inc(turned.sem, 1)
                pe.wait_ge(kds.sem, kds.at(t))
                pe.wait_ge(news.sem, news.at(t - 2))
                for h in range(RH):
                    nc.tensor.matmul(up[:, s, 0, h * P:(h + 1) * P], kd[:, s, h * P:(h + 1) * P], kv[:, ring[1], 512 + h * P:512 + (h + 1) * P], start=True, stop=True)
                pe.wait_ge(xws.sem, xws.at(t))
                pe.wait_ge(bts.sem, bts.at(t))
                for c in range(SG):
                    m = nc.tensor.matmul(up[:, s, 1, c * 256:(c + 1) * 256], bt[:, s, c * P:(c + 1) * P], xw[:, s, c * 256:(c + 1) * 256], start=True, stop=True)
                m.then_inc(ups.sem, 1)
            turns(pe, body)

        @block.scalar
        def _(act):
            act.sem_inc(bts.sem, bts.credit)

            def body(t, ring, use, s, tile, back, state, stored):
                if stored:
                    act.wait_ge(news.sem, news.at(t - 1))
                    act.dma_start(tile_of(dram["sb"], tile), state[:, s].rearrange("p a b -> p (a b)")).then_inc(s_out.sem(s), 16)
                act.wait_ge(turned.sem, turned.at(t, 2))
                act.wait_ge(ups.sem, ups.at(t - 2))
                nc.scalar.activation(bt[:, s], bT[:, s, 0:SG * P], ACT.Copy).then_inc(bts.sem, 1)
            turns(act, body)
            for s in range(2):
                act.wait_ge(s_out.sem(s), 16 * NL // 2)

        @block.vector
        def _(dve):
            dve.sem_inc(xws.sem, xws.credit)
            dve.sem_inc(news.sem, news.credit)

            def body(t, ring, use, s, tile, back, state, stored):
                dve.wait_ge(turned.sem, turned.at(t, 1))
                dve.wait_ge(ups.sem, ups.at(t - 2))
                nc.vector.tensor_tensor(xw[:, s].rearrange("p (h e) -> p h e", h=SH), xT[:, s].rearrange("p (h e) -> p h e", h=SH),
                                                heads(tile_row(g["E"], tile, 4 if back else 1), SP_), ALU.mult).then_inc(xws.sem, 1)
                dve.wait_ge(zero.sem, zero.at(0))
                dve.wait_ge(news.sem, news.at(t - 1))
                nc.vector.tensor_tensor(sd[:, 0].rearrange("p (h e) -> p h e", h=RH), state[:, s, 0].rearrange("p (h e) -> p h e", h=RH),
                                                heads(g["Dtot"][:, int(back)], P), ALU.mult).then_inc(dec_r.sem, 1)
                dve.wait_ge(dec_r.sem, dec_r.at(t))
                dve.wait_ge(dec.sem, dec.at(t))
                dve.wait_ge(ups.sem, ups.at(t))
                if stored:
                    dve.wait_ge(s_out.sem(1 - s), s_out.at(use - 1 if s else use - 2))
                for n in (1, 0):
                    nc.vector.tensor_tensor(state[:, 1 - s, n], sd[:, n], up[:, s, n], ALU.add).then_inc(news.sem, 1)
            turns(dve, body)


def mixing(nc, kit, io, g, dram):
    with ExitStack() as st:
        tok = kit.sb("m_tok", [P, 2, 5 * 512], stack=st)
        uc = kit.sb("m_u", [P, 2, NCH, P], stack=st)
        sb = kit.sb("m_sb", [P, 2, 2, 512], stack=st)
        qk = kit.sb("m_qk", [P, 2, 512], stack=st)
        qd = kit.sb("m_qd", [P, 2, 512], stack=st)
        xs = kit.sb("m_xs", [P, 512], stack=st)
        bt = kit.sb("m_bt", [P, SG * P], stack=st)
        kd = kit.sb("m_kd", [P, 512], stack=st)
        xw = kit.sb("m_xw", [P, 512], stack=st)
        dav = kit.sb("m_dav", [P, 2, SH * P], stack=st)
        sT = kit.sb("m_sT", [P, 512], stack=st)
        L = kit.sb("m_L", [P, SH, P], stack=st)
        G = kit.sb("m_G", [P, SH, P], stack=st)
        sd = kit.sb("m_sd", [P, 2, 512], stack=st)
        xd = kit.sb("m_xd", [P, 512], stack=st)
        t1 = kit.sb("m_t1", [P, 512], stack=st)
        t2 = kit.sb("m_t2", [P, 512], stack=st)
        t3 = kit.sb("m_t3", [P, 512], stack=st)
        yr = kit.sb("m_yr", [P, 512], stack=st)
        bn = kit.sb("m_bn", [P, RH, 6], stack=st)
        mv = kit.sb("m_mv", [P, RH, 2], stack=st)
        rs = kit.sb("m_rs", [P, 8], stack=st)
        sq = kit.sb("m_sq", [P, 512], stack=st)
        yc = kit.sb("m_y", [P, 2, D], stack=st)
        bank = kit.ps("m_bank", [P, 8, 512], st)
        tok_in = kit.landing("m_tok_in", 2)
        u_in = kit.landing("m_u_in", 2)
        sb_in = kit.landing("m_sb_in", 2)
        y_out = kit.landing("m_y_out", 2, credit=16)
        turned = kit.counter("m_transposed", 4, credit=4)
        left = kit.counter("m_transposed_copied", 4, credit=4)
        qdec = kit.counter("m_q_decayed", 2, credit=2)
        davs = kit.counter("m_da_spread", 2, credit=2)
        kds = kit.counter("m_k_decayed", 1, credit=1)
        xws = kit.counter("m_x_weighted", 1, credit=1)
        prod = kit.counter("m_products", 3, credit=3)
        exps = kit.counter("m_decays_exp", 1, credit=1)
        sTs = kit.counter("m_scores_decayed", 1, credit=1)
        gate = kit.counter("m_steps_spread", 3, credit=3)
        yret = kit.counter("m_y_ret", 1, credit=1)
        yssd = kit.counter("m_y_ssd", 2, credit=2)
        upr = kit.counter("m_ret_update_ready", 1, credit=1)
        ups = kit.counter("m_ssd_update_ready", 1, credit=1)
        dec = kit.counter("m_state_decayed", 2, credit=2)
        news = kit.counter("m_state_ready", 2, credit=2)
        skip = kit.counter("m_skip_ready", 1, credit=1)
        stats = kit.counter("m_head_stats", 2)
        rstd = kit.counter("m_rstd", 2)
        eps_added = kit.counter("m_eps_added", 2)
        yrs = kit.counter("m_ret_normed", 2, credit=2)
        ysum = kit.counter("m_ssd_summed", 5, credit=5)
        ssq = kit.counter("m_ssd_ssq", 1, credit=1)
        ssd_gated = kit.counter("m_ssd_gated", 1, credit=1)
        ret_gated = kit.counter("m_ret_gated", 1, credit=1)
        yssdn = kit.counter("m_ssd_normed", 1, credit=1)
        w_out_in = kit.landing("w_out_in", dmas=KD)
        block = st.enter_context(nc.Block())

        def turns(eng, body):
            body(-1, -1, 1)
            with eng.Fori(0, NL // 2 - 1) as i:
                for s in range(2):
                    body(i * 2 + s, i, s)
            for s in range(2):
                body(NL - 2 + s, NL // 2 - 1, s)

        def there(t):
            return not isinstance(t, int) or 0 <= t < NL

        def by(v, n):
            return v.rearrange("p (h e) -> p h e", h=n)

        @block.sync
        def _(sp):
            for s in range(2):
                sp.sem_inc(y_out.sem(s), y_out.credit)

            def load(t, use, s, tile):
                sp.wait_ge(ups.sem, ups.at(t - 2))
                sp.wait_ge(yssd.sem, yssd.at(t - 2))
                sp.wait_ge(ssd_gated.sem, ssd_gated.at(t - 2))
                sp.wait_ge(ret_gated.sem, ret_gated.at(t - 2))
                issue(t, use, s, tile)

            def issue(t, use, s, tile):
                sp.dma_start(uc[:, s], dram["u"][:, :, bass.ds(tile * P, P)].rearrange("c p t -> p c t")).then_inc(u_in.sem(s), 16)
                sp.dma_start(tok[:, s], tile_of(dram["tok"], tile, 0, 5 * 512)).then_inc(tok_in.sem(s), 16)
                sp.dma_start(sb[:, s].rearrange("p a b -> p (a b)"), tile_of(dram["sb"], tile)).then_inc(sb_in.sem(s), 16)

            for s in range(2):
                issue(s, 0, s, NCT + s)
            for k in range(KD):
                sp.dma_start(g["w_out"][:, k], io["w_out"][0, k * P:(k + 1) * P, :]).then_inc(w_out_in.sem(0), 16)
            with sp.Fori(0, NL // 2 - 1) as i:
                for s in range(2):
                    t = i * 2 + (2 + s)
                    load(t, i + 1, s, t + NCT)
            sp.wait_ge(w_out_in.sem(0), w_out_in.at(0))

        @block.gpsimd
        def _(pool):
            for x in (davs, kds, dec, skip, ssd_gated, ret_gated):
                pool.sem_inc(x.sem, x.credit)

            def spread(t, d):
                pool.wait_ge(prod.sem, prod.at(t - 1))
                nc.gpsimd.tensor_tensor(by(dav[:, d], SH), g["tri"][:, 2 * d].unsqueeze(1).to_broadcast([P, SH, P]),
                                        heads(tile_row(g["dd"], t + NCT, 2 + d), P), ALU.mult).then_inc(davs.sem, 1)

            def body(t, use, s):
                if there(t + 1):
                    spread(t + 1, 0)
                if there(t):
                    pool.wait_ge(stats.sem, stats.at(t))
                    rstd_root(nc, g, pool, eps_added, t, 1, rs[:, 0:4], mv[:, :, 1], 1).then_inc(rstd.sem, 1)
                if there(t + 1):
                    spread(t + 1, 1)
                    pool.wait_ge(tok_in.sem(1 - s), tok_in.at(use + s))
                    pool.wait_ge(upr.sem, upr.at(t))
                    nc.gpsimd.tensor_tensor(by(kd[:], RH), by(tok[:, 1 - s, 512:1024], RH), heads(g["Dk"][:, 0], P), ALU.mult).then_inc(kds.sem, 1)
                if there(t):
                    pool.wait_ge(yrs.sem, yrs.at(t, 2))
                    pool.wait_ge(y_out.sem(s), y_out.at(use - 1))
                    nc.gpsimd.tensor_tensor(yc[:, s, 0:512], yr[:], tok[:, s, 3 * 512:4 * 512], ALU.mult).then_inc(ret_gated.sem, 1)
                    pool.wait_ge(ysum.sem, ysum.at(t, 5))
                    pool.wait_ge(yssdn.sem, yssdn.at(t - 1))
                    nc.gpsimd.tensor_tensor(t1[:], t3[:], tok[:, s, 4 * 512:5 * 512], ALU.mult).then_inc(ssd_gated.sem, 1)
                    pool.wait_ge(ssq.sem, ssq.at(t))
                    rstd_root(nc, g, pool, eps_added, t, 2, rs[:, 5:6], rs[:, 4:5], 512).then_inc(rstd.sem, 1)
                if there(t + 1):
                    pool.wait_ge(news.sem, news.at(t))
                    nc.gpsimd.tensor_tensor(by(sd[:, 0], RH), by(g["sf"][:, 1 - s, 0], RH), heads(g["Dtot"][:, 0], P), ALU.mult).then_inc(dec.sem, 1)
                    nc.gpsimd.tensor_tensor(by(sd[:, 1], SH), by(g["sf"][:, 1 - s, 1], SH), heads(tile_row(g["E"], t + (1 + NCT), 2), SP_), ALU.mult).then_inc(dec.sem, 1)
                    pool.wait_ge(left.sem, left.at(t + 1, 3))
                    pool.wait_ge(ysum.sem, ysum.at(t))
                    nc.gpsimd.tensor_tensor(by(xd[:], SH), by(xs[:], SH), heads(g["dskip"][:], SP_), ALU.mult).then_inc(skip.sem, 1)
            turns(pool, body)

        @block.tensor
        def _(pe):
            for x in (turned, prod, yret, yssd, upr, ups):
                pe.sem_inc(x.sem, x.credit)
            ident = g["ident"][:, :]

            def turn(t, s, n, src, count):
                b, which = 2 + n % 2, n + 1
                if n >= 2:
                    pe.wait_ge(left.sem, left.at(t, which - 2))
                else:
                    pe.wait_ge(left.sem, left.at(t - 1, which + 2))
                for c in range(count):
                    m = nc.tensor.transpose(bank[:, b, c * P:(c + 1) * P], src(c), ident)
                m.then_inc(turned.sem, 1)

            def body(t, use, s):
                n, nuse = 1 - s, use + s
                if there(t):
                    pe.wait_ge(sTs.sem, sTs.at(t))
                    pe.wait_ge(qdec.sem, qdec.at(t))
                    pe.wait_ge(sb_in.sem(s), sb_in.at(use))
                    pe.wait_ge(news.sem, news.at(t - 1))
                    pe.wait_ge(yrs.sem, yrs.at(t - 1))
                    for h in range(RH):
                        e = slice(h * P, (h + 1) * P)
                        nc.tensor.matmul(bank[:, 0, e], sT[:, e], tok[:, s, 1024 + h * P:1024 + (h + 1) * P], start=True, stop=False)
                        nc.tensor.matmul(bank[:, 0, e], qd[:, 0, e], g["sf"][:, s, 0, e], start=False, stop=False)
                        m = nc.tensor.matmul(bank[:, 0, e], qd[:, 1, e], sb[:, s, 0, e], start=False, stop=True)
                    m.then_inc(yret.sem, 1)
                    pe.wait_ge(kds.sem, kds.at(t))
                    for h in range(RH):
                        e = slice(h * P, (h + 1) * P)
                        m = nc.tensor.matmul(bank[:, 4, e], kd[:, e], tok[:, s, 1024 + h * P:1024 + (h + 1) * P], start=True, stop=True)
                    m.then_inc(upr.sem, 1)
                if there(t + 1):
                    pe.wait_ge(tok_in.sem(n), tok_in.at(nuse))
                    for which in range(2):
                        turn(t + 1, n, which, lambda h: tok[:, n, which * 512 + h * P:which * 512 + (h + 1) * P], RH)
                if there(t):
                    pe.wait_ge(exps.sem, exps.at(t))
                    for b, state in ((5, g["sf"][:, s, 1]), (6, sb[:, s, 1])):
                        for c in range(SG):
                            m = nc.tensor.matmul(bank[:, b, c * 256:(c + 1) * 256], uc[:, s, 6 + c], state[:, c * 256:(c + 1) * 256], start=True, stop=True)
                    m.then_inc(yssd.sem, 1)
                    pe.wait_ge(xws.sem, xws.at(t))
                    pe.wait_ge(left.sem, left.at(t, 4))
                    pe.wait_ge(gate.sem, gate.at(t))
                    for c in range(SG):
                        m = nc.tensor.matmul(bank[:, 7, c * 256:(c + 1) * 256], bt[:, c * P:(c + 1) * P], xw[:, c * 256:(c + 1) * 256], start=True, stop=True)
                    m.then_inc(ups.sem, 1)
                    pe.wait_ge(ysum.sem, ysum.at(t - 1))
                    for h in range(SH):
                        m = nc.tensor.matmul(bank[:, 1, h * SP_:(h + 1) * SP_], L[:, h], xs[:, h * SP_:(h + 1) * SP_], start=True, stop=True)
                    m.then_inc(yssd.sem, 1)
                if there(t + 1):
                    pe.wait_ge(u_in.sem(n), u_in.at(nuse))
                    turn(t + 1, n, 2, lambda c: uc[:, n, c], 4)
                    turn(t + 1, n, 3, lambda c: uc[:, n, 4 + c], SG)
                    pe.wait_ge(news.sem, news.at(t, 1))
                    for h in range(RH):
                        m = nc.tensor.matmul(bank[:, 4, h * P:(h + 1) * P], qk[:, 1, h * P:(h + 1) * P], qk[:, 0, h * P:(h + 1) * P], start=True, stop=True)
                    m.then_inc(prod.sem, 1)
                    pe.wait_ge(news.sem, news.at(t))
                    for c in range(SG):
                        m = nc.tensor.matmul(bank[:, 7, c * P:(c + 1) * P], uc[:, n, 4 + c], uc[:, n, 6 + c], start=True, stop=True)
                    m.then_inc(prod.sem, 1)
                    pe.wait_ge(davs.sem, davs.at(t + 1))
                    pe.wait_ge(ysum.sem, ysum.at(t, 2))
                    for half in range(2):
                        for d in range(2):
                            m = nc.tensor.matmul(bank[:, 5 + half], g["tri"][:, 1 + 2 * d], dav[:, d, half * 512:(half + 1) * 512], start=(d == 0), stop=(d == 1))
                    m.then_inc(prod.sem, 1)
            turns(pe, body)

        @block.scalar
        def _(act):
            for x in (left, exps, ssq):
                act.sem_inc(x.sem, x.credit)

            def body(t, use, s):
                if there(t + 1):
                    for n in range(2):
                        act.wait_ge(turned.sem, turned.at(t + 1, n + 1))
                        act.wait_ge(prod.sem, prod.at(t, 1))
                        act.wait_ge(qdec.sem, qdec.at(t))
                        nc.scalar.activation(qk[:, n], bank[:, 2 + n], ACT.Copy).then_inc(left.sem, 1)
                    act.wait_ge(turned.sem, turned.at(t + 1, 3))
                    act.wait_ge(yssd.sem, yssd.at(t))
                    act.wait_ge(skip.sem, skip.at(t))
                    nc.scalar.activation(xs[:], bank[:, 2], ACT.Copy).then_inc(left.sem, 1)
                    act.wait_ge(turned.sem, turned.at(t + 1, 4))
                    act.wait_ge(ups.sem, ups.at(t))
                    nc.scalar.activation(bt[:], bank[:, 3, 0:SG * P], ACT.Copy).then_inc(left.sem, 1)
                if there(t):
                    act.wait_ge(ssd_gated.sem, ssd_gated.at(t))
                    nc.scalar.activation(sq[:], t1[:], ACT.Square, accum_out=rs[:, 4:5]).then_inc(ssq.sem, 1)
                if there(t + 1):
                    act.wait_ge(prod.sem, prod.at(t + 1))
                    nc.scalar.activation(L[:].rearrange("p h n -> p (h n)"), bank[:, 5:7].rearrange("p a b -> p (a b)"), ACT.Exp).then_inc(exps.sem, 1)
                if there(t):
                    act.wait_ge(ret_gated.sem, ret_gated.at(t))
                    act.wait_ge(yssdn.sem, yssdn.at(t))
                    act.dma_start(tile_of(dram["y"], t + NCT), yc[:, s]).then_inc(y_out.sem(s), 16)
            turns(act, body)
            for s in range(2):
                act.wait_ge(y_out.sem(s), y_out.at(NL // 2 - 1))

        @block.vector
        def _(dve):
            for x in (qdec, xws, sTs, gate, news, yrs, ysum, yssdn):
                dve.sem_inc(x.sem, x.credit)

            def body(t, use, s):
                if there(t):
                    tile = t + NCT
                    dve.wait_ge(gate.sem, gate.at(t, 1))
                    dve.wait_ge(exps.sem, exps.at(t))
                    nc.vector.tensor_tensor(L[:], L[:], G[:], ALU.mult).then_inc(gate.sem, 1)
                    dve.wait_ge(gate.sem, gate.at(t, 2))
                    dve.wait_ge(prod.sem, prod.at(t, 2))
                    nc.vector.tensor_tensor(L[:].rearrange("p (c r) n -> p c r n", c=SG), L[:].rearrange("p (c r) n -> p c r n", c=SG),
                                            bank[:, 7, 0:SG * P].rearrange("p (c n) -> p c n", c=SG).unsqueeze(2).to_broadcast([P, SG, SH // SG, P]), ALU.mult).then_inc(gate.sem, 1)
                    dve.wait_ge(yret.sem, yret.at(t))
                    for h in range(RH):
                        m = nc.vector.bn_stats(bn[:, h], bank[:, 0, h * P:(h + 1) * P])
                    m.then_inc(stats.sem, 1)
                    dve.wait_ge(stats.sem, stats.at(t, 1))
                    dve.wait_ge(upr.sem, upr.at(t))
                    dve.wait_ge(dec.sem, dec.at(t))
                    nc.vector.tensor_tensor(g["sf"][:, 1 - s, 0], sd[:, 0], bank[:, 4], ALU.add).then_inc(news.sem, 1)
                    for h in range(RH):
                        m = nc.vector.bn_aggr(mv[:, h], bn[:, h])
                    m.then_inc(stats.sem, 1)
                    dve.wait_ge(yssd.sem, yssd.at(t, 1))
                    dve.wait_ge(ssd_gated.sem, ssd_gated.at(t - 1))
                    nc.vector.tensor_tensor(by(t3[:], SH), by(bank[:, 5], SH), heads(tile_row(g["E"], tile, 0), SP_), ALU.mult).then_inc(ysum.sem, 1)
                    nc.vector.tensor_tensor(by(t2[:], SH), by(bank[:, 6], SH), heads(tile_row(g["E"], tile, 3), SP_), ALU.mult).then_inc(ysum.sem, 1)
                    dve.wait_ge(ups.sem, ups.at(t))
                    nc.vector.tensor_tensor(g["sf"][:, 1 - s, 1], sd[:, 1], bank[:, 7], ALU.add).then_inc(news.sem, 1)
                    dve.wait_ge(rstd.sem, rstd.at(t, 1))
                    dve.wait_ge(ret_gated.sem, ret_gated.at(t - 1))
                    for h in range(RH):
                        m = nc.vector.tensor_scalar(yr[:, h * P:(h + 1) * P], bank[:, 0, h * P:(h + 1) * P], mv[:, h, 0:1], rs[:, h:h + 1], ALU.subtract, ALU.mult)
                        if h % 2:
                            m.then_inc(yrs.sem, 1)
                    dve.wait_ge(yssd.sem, yssd.at(t, 2))
                    dve.wait_ge(ysum.sem, ysum.at(t, 1))
                    nc.vector.tensor_tensor(t3[:], t3[:], bank[:, 1], ALU.add).then_inc(ysum.sem, 1)
                    dve.wait_ge(ysum.sem, ysum.at(t, 3))
                    dve.wait_ge(skip.sem, skip.at(t))
                    nc.vector.tensor_tensor(t2[:], t2[:], xd[:], ALU.add).then_inc(ysum.sem, 1)
                    dve.wait_ge(ysum.sem, ysum.at(t, 4))
                    nc.vector.tensor_tensor(t3[:], t3[:], t2[:], ALU.add).then_inc(ysum.sem, 1)
                if there(t + 1):
                    tile = t + (1 + NCT)
                    dve.wait_ge(left.sem, left.at(t + 1, 1))
                    dve.wait_ge(yret.sem, yret.at(t))
                    for d in range(2):
                        nc.vector.tensor_tensor(qd[:, d], qk[:, 0], g["Dq"][:, d].rearrange("p h n -> p (h n)"), ALU.mult).then_inc(qdec.sem, 1)
                    dve.wait_ge(left.sem, left.at(t + 1, 3))
                    dve.wait_ge(ups.sem, ups.at(t))
                    nc.vector.tensor_tensor(by(xw[:], SH), by(xs[:], SH), heads(tile_row(g["E"], tile, 1), SP_), ALU.mult).then_inc(xws.sem, 1)
                    dve.wait_ge(prod.sem, prod.at(t + 1, 1))
                    nc.vector.tensor_tensor(sT[:], bank[:, 4], g["DT"][:].rearrange("p h n -> p (h n)"), ALU.mult).then_inc(sTs.sem, 1)
                    for h in range(SH):
                        m = nc.vector.tensor_scalar(G[:, h], g["tri"][:, 0], g["dd"][:, bass.ds(tile, 1), 0, h:h + 1].rearrange("p a b -> p (a b)"),
                                                    g["dd"][:, bass.ds(tile, 1), 1, h:h + 1].rearrange("p a b -> p (a b)"), ALU.mult, ALU.add)
                    m.then_inc(gate.sem, 1)
                if there(t):
                    dve.wait_ge(rstd.sem, rstd.at(t, 2))
                    dve.wait_ge(y_out.sem(s), y_out.at(use - 1))
                    nc.vector.tensor_scalar(yc[:, s, 512:D], t1[:], rs[:, 5:6], 512.0 ** 0.5, ALU.mult, ALU.mult).then_inc(yssdn.sem, 1)
            turns(dve, body)


def residual(nc, kit, io, g, dram):
    with ExitStack() as st:
        w = g["w_out"]
        wh = kit.sb("r_w_high", [P, KD, D], F32R, stack=st)
        wl = kit.sb("r_w_low", [P, KD, D], F32R, stack=st)
        wr = kit.sb("r_wr", [P, KD, NG + NE], stack=st)
        br = kit.sb("r_br", [P, NG + NE], stack=st)
        y = kit.sb("r_y", [P, 2, D], stack=st)
        x = kit.sb("r_x", [P, 2, D], stack=st)
        yT = kit.sb("r_yT", [P, 2, 2, KD, P], F32R, stack=st)
        hT = kit.sb("r_hT", [P, 2, KD, P], stack=st)
        sq = kit.sb("r_sq", [P, D], stack=st)
        ss = kit.sb("r_ss", [P, 4], stack=st)
        yn = kit.sb("r_yn", [P, D], stack=st)
        x1 = kit.sb("r_x1", [P, 2, D], stack=st)
        h2 = kit.sb("r_h2", [P, 2, D], stack=st)
        pT = kit.ps("r_pT", [P, KD, P], st)
        py = kit.ps("r_py", [P, 2, 2, 512], st)
        pl = kit.ps("r_pl", [P, 512], st)
        w_l = kit.landing("r_w_in", dmas=NG + 3)
        y_in = kit.landing("r_y_in", 2)
        x_in = kit.landing("r_x_in", 2)
        x1_out = kit.landing("r_x1_out", 2, credit=16)
        h2_out = kit.landing("r_h2_out", 2, credit=16)
        wsc = kit.counter("r_w_scaled")
        whs = kit.counter("r_w_high_ready")
        wls = kit.counter("r_w_low_ready")
        yTt = kit.counter("r_y_transposed")
        yTh = kit.counter("r_yT_high_ready")
        yTl = kit.counter("r_yT_low_ready")
        prod = kit.counter("r_product")
        ssq_y = kit.counter("r_ssq_y")
        ssq_x = kit.counter("r_ssq_x1")
        eps_y = kit.counter("r_eps_added_y")
        eps_x = kit.counter("r_eps_added_x1")
        rstd_y = kit.counter("r_rstd_y")
        rstd_x = kit.counter("r_rstd_x1")
        yns = kit.counter("r_y_normed")
        x1s = kit.counter("r_x1_ready")
        h2m = kit.counter("r_h2_scaled")
        h2s = kit.counter("r_h2_ready")
        hTt = kit.counter("r_h_transposed", credit=1)
        hTs = kit.counter("r_hT_ready")
        lgp = kit.counter("r_logits_product", credit=1)
        lgs = kit.counter("r_logits_ready", credit=1)
        block = st.enter_context(nc.Block())

        def turns(eng, body):
            for t in (-1, 0, 1):
                body(t, t // 2, t % 2)
            with eng.Fori(0, NL // 2 - 2) as i:
                for s in range(2):
                    body(i * 2 + (2 + s), i + 1, s)
            for t in range(NL - 2, NL + 2):
                body(t, t // 2, t % 2)

        def there(t):
            return not isinstance(t, int) or 0 <= t < NL

        @block.sync
        def _(sp):
            for s in range(2):
                sp.sem_inc(x1_out.sem(s), 16)
                sp.sem_inc(h2_out.sem(s), 16)

            def load_y(t, use, s):
                sp.dma_start(y[:, s], tile_of(dram["y"], t + NCT)).then_inc(y_in.sem(s), 16)

            def load_x(t, use, s):
                sp.dma_start(x[:, s], tile_of(io["x"].rearrange("o (t p) d -> (o t) p d", p=P), t)).then_inc(x_in.sem(s), 16)
            for t in range(2):
                load_y(t, 0, t)
                load_x(t, 0, t)
            one = w_l.sem(0)
            sp.dma_start(wr[:, :, 0:NG], io["moe_w_rg"].rearrange("o (k p) n -> p (o k) n", p=P)).then_inc(one, 16)
            for n in range(NG):
                sp.dma_start(wr[:, :, NG + n * EPG:NG + (n + 1) * EPG], io["moe_w_re"][0, n].rearrange("(k p) e -> p k e", p=P)).then_inc(one, 16)
            sp.dma_start(br[:, 0:NG], io["moe_b_rg"].to_broadcast([P, NG])).then_inc(one, 16)
            sp.dma_start(br[:, NG:NG + NE], io["moe_b_re"].rearrange("o g e -> o (g e)").to_broadcast([P, NE])).then_inc(one, 16)
            for t, use, s in pairs(sp, 2, NL):
                sp.wait_ge(yTt.sem, yTt.at(t - 2))
                load_y(t, use, s)
                sp.wait_ge(x1s.sem, x1s.at(t - 2))
                load_x(t, use, s)

        @block.gpsimd
        def _(pool):
            def body(t, use, s):
                if there(t - 1):
                    pool.wait_ge(ssq_x.sem, ssq_x.at(t - 1))
                    rstd_root(nc, g, pool, eps_x, t - 1, 1, ss[:, 3:4], ss[:, 1:2], D).then_inc(rstd_x.sem, 1)
                if there(t):
                    pool.wait_ge(ssq_y.sem, ssq_y.at(t))
                    rstd_root(nc, g, pool, eps_y, t, 1, ss[:, 2:3], ss[:, 0:1], D).then_inc(rstd_y.sem, 1)
            turns(pool, body)

        @block.tensor
        def _(pe):
            for x_ in (hTt, lgp):
                pe.sem_inc(x_.sem, x_.credit)
            ident = g["ident"][:, :]

            def body(t, use, s):
                if there(t + 1):
                    pe.wait_ge(y_in.sem(1 - s), y_in.at(use + s))
                    if there(t - 2):
                        pe.wait_ge(hTs.sem, hTs.at(t - 2))
                    elif there(t):
                        pe.wait_ge(yTl.sem, yTl.at(t))
                    for k in range(KD):
                        m = nc.tensor.transpose(pT[:, k], y[:, 1 - s, k * P:(k + 1) * P], ident)
                    m.then_inc(yTt.sem, 1)
                if there(t):
                    if there(t - 2):
                        pe.wait_ge(yns.sem, yns.at(t - 2))
                    pe.wait_ge(yTh.sem, yTh.at(t))
                    pe.wait_ge(yTl.sem, yTl.at(t))
                    for k in range(KD):
                        pe.wait_ge(wls.sem, wls.at(k))
                        for part, with_ in ((0, wh), (0, wl), (1, wh)):
                            for n in range(2):
                                m = nc.tensor.matmul(py[:, s, n], yT[:, s, part, k], with_[:, k, n * 512:(n + 1) * 512], start=(k == 0 and part == 0 and with_ is wh),
                                                     stop=(k == KD - 1 and part == 1))
                    m.then_inc(prod.sem, 1)
                if there(t - 1):
                    pe.wait_ge(h2s.sem, h2s.at(t - 1))
                    if there(t + 1):
                        pe.wait_ge(yTl.sem, yTl.at(t + 1))
                    else:
                        pe.wait_ge(hTs.sem, hTs.at(t - 2))
                    for k in range(KD):
                        m = nc.tensor.transpose(pT[:, k], h2[:, 1 - s, k * P:(k + 1) * P], ident)
                    m.then_inc(hTt.sem, 1)
                if there(t - 2):
                    pe.wait_ge(w_l.sem(0), w_l.at(0))
                    pe.wait_ge(hTs.sem, hTs.at(t - 2))
                    pe.wait_ge(lgs.sem, lgs.at(t - 3))
                    for k in range(KD):
                        m = nc.tensor.matmul(pl[:, 0:NG + NE], hT[:, s, k], wr[:, k], start=(k == 0), stop=(k == KD - 1))
                    m.then_inc(lgp.sem, 1)
            turns(pe, body)

        @block.scalar
        def _(act):
            def body(t, use, s):
                if there(t - 1):
                    act.wait_ge(x1s.sem, x1s.at(t - 1))
                    nc.scalar.activation(sq[:], x1[:, 1 - s], ACT.Square, accum_out=ss[:, 1:2]).then_inc(ssq_x.sem, 1)
                    act.dma_start(tile_of(dram["x1"], t - 1), x1[:, 1 - s]).then_inc(x1_out.sem(1 - s), 16)
                if there(t + 1):
                    act.wait_ge(yTt.sem, yTt.at(t + 1))
                    if there(t - 1):
                        act.wait_ge(prod.sem, prod.at(t - 1))
                    nc.scalar.activation(yT[:, 1 - s, 0], pT[:], ACT.Copy).then_inc(yTh.sem, 1)
                if isinstance(t, int) and t == -1:
                    for k in range(KD):
                        act.wait_ge(wsc.sem, wsc.at(k))
                        nc.scalar.activation(wh[:, k], w[:, k], ACT.Copy).then_inc(whs.sem, 1)
                if there(t):
                    act.wait_ge(prod.sem, prod.at(t))
                    if there(t - 1):
                        act.wait_ge(ssq_x.sem, ssq_x.at(t - 1))
                        act.wait_ge(yns.sem, yns.at(t - 1))
                    nc.scalar.activation(sq[:], py[:, s].rearrange("p a b -> p (a b)"), ACT.Square, accum_out=ss[:, 0:1]).then_inc(ssq_y.sem, 1)
                if there(t - 1):
                    act.wait_ge(hTt.sem, hTt.at(t - 1))
                    act.wait_ge(lgp.sem, lgp.at(t - 3)) if there(t - 3) else None
                    nc.scalar.activation(hT[:, 1 - s], pT[:], ACT.Copy).then_inc(hTs.sem, 1)
                    act.dma_start(tile_of(dram["h2"].rearrange("(t p) d -> t p d", p=P), t - 1), h2[:, 1 - s]).then_inc(h2_out.sem(1 - s), 16)
            turns(act, body)
            for s in range(2):
                act.wait_ge(x1_out.sem(s), x1_out.at(NL // 2 - 1))
                act.wait_ge(h2_out.sem(s), h2_out.at(NL // 2 - 1))

        @block.vector
        def _(dve):
            dve.sem_inc(lgs.sem, lgs.credit)

            def body(t, use, s):
                if there(t + 1):
                    dve.wait_ge(yTh.sem, yTh.at(t + 1))
                    nc.vector.tensor_tensor(yT[:, 1 - s, 1], pT[:], yT[:, 1 - s, 0].bitcast(F32), ALU.subtract).then_inc(yTl.sem, 1)
                if isinstance(t, int) and t == -1:
                    for k in range(KD + 1):
                        if k < KD:
                            nc.vector.tensor_scalar(w[:, k], w[:, k], g["wn"][:, k:k + 1], None, ALU.mult).then_inc(wsc.sem, 1)
                        if k:
                            dve.wait_ge(whs.sem, whs.at(k - 1))
                            nc.vector.tensor_tensor(wl[:, k - 1], w[:, k - 1], wh[:, k - 1].bitcast(F32), ALU.subtract).then_inc(wls.sem, 1)
                if there(t - 1):
                    dve.wait_ge(rstd_x.sem, rstd_x.at(t - 1))
                    dve.wait_ge(h2_out.sem(1 - s), h2_out.at(use + (s - 2)))
                    dve.wait_ge(hTt.sem, hTt.at(t - 3)) if there(t - 3) else None
                    nc.vector.scalar_tensor_tensor(out=h2[:, 1 - s], in0=x1[:, 1 - s], scalar=ss[:, 3:4], in1=g["mod"][:, 2], op0=ALU.mult, op1=ALU.mult).then_inc(h2m.sem, 1)
                    dve.wait_ge(h2m.sem, h2m.at(t - 1))
                    nc.vector.tensor_tensor(h2[:, 1 - s], h2[:, 1 - s], g["mod"][:, 1], ALU.add).then_inc(h2s.sem, 1)
                if there(t):
                    dve.wait_ge(rstd_y.sem, rstd_y.at(t))
                    if there(t - 1):
                        dve.wait_ge(x1s.sem, x1s.at(t - 1))
                    nc.vector.scalar_tensor_tensor(out=yn[:], in0=py[:, s].rearrange("p a b -> p (a b)"), scalar=ss[:, 2:3], in1=g["mod"][:, 0], op0=ALU.mult, op1=ALU.mult).then_inc(yns.sem, 1)
                    dve.wait_ge(yns.sem, yns.at(t))
                    dve.wait_ge(x_in.sem(s), x_in.at(use))
                    dve.wait_ge(x1_out.sem(s), x1_out.at(use - 1))
                    if there(t - 2):
                        dve.wait_ge(h2m.sem, h2m.at(t - 2))
                    nc.vector.tensor_tensor(x1[:, s], yn[:], x[:, s], ALU.add).then_inc(x1s.sem, 1)
                if there(t - 2):
                    dve.wait_ge(lgp.sem, lgp.at(t - 2))
                    nc.vector.tensor_tensor(g["logits"][:, bass.ds(t - 2, 1)].rearrange("p o n -> p (o n)"), pl[:, 0:NG + NE], br[:], ALU.add).then_inc(lgs.sem, 1)
            turns(dve, body)


def routing(nc, kit, io, g, dram):
    T4, T8, T32 = [P, NL, NG], [P, NL, EPG], [P, NL, NE]
    BIG = 1e30
    with ExitStack() as st:
        iota = kit.sb("o_iota", [P, EPG], stack=st)
        mult = kit.sb("o_mult", [P, NL - 1], stack=st)
        mg = kit.sb("o_mg", [P, NL], stack=st)
        e4 = kit.sb("o_e4", T4, stack=st)
        og = kit.sb("o_og", T4, stack=st)
        den = kit.sb("o_den", [P, NL], stack=st)
        w32 = kit.sb("o_w32", [P, NL, NG, EPG], stack=st)
        le = kit.sb("o_le", T8, stack=st)
        c8 = kit.sb("o_c8", T8, stack=st)
        m12 = kit.sb("o_m12", [P, 2, NL], stack=st)
        fi = kit.sb("o_fi", [P, NL], stack=st)
        o8 = kit.sb("o_o8", [P, 2, NL, EPG], stack=st)
        oh = kit.sb("o_oh", [P, 2, NL, NG, EPG], stack=st)
        both = kit.sb("o_both", T32, stack=st)
        rank = kit.sb("o_rank", T32, stack=st)
        tot = kit.sb("o_tot", [P, NL + 1, NE], stack=st)
        cnt = kit.sb("o_cnt", [P, NE], stack=st)
        zero = kit.sb("o_zero", [P, NE], stack=st)
        start = kit.sb("o_start", [P, NE], stack=st)
        cmp = kit.sb("o_cmp", [P, NE, NL - 1], stack=st)
        nb = kit.sb("o_nb", [P, NE], stack=st)
        sl = kit.sb("o_sl", [P, 2, NL], stack=st)
        ex = kit.sb("o_ex", [P, NL], stack=st)
        token = kit.sb("o_token", [P, NL], I32, stack=st)
        z = kit.sb("o_z", [P, D], stack=st)
        pr = kit.ps("o_pr", [P, 2, 512], st)
        c_in = kit.landing("o_const_in", dmas=2)
        token_in = kit.landing("o_token_in")
        w_in = kit.landing("o_w_in", 3, dmas=2)
        w_high = kit.counter("o_w_high_ready", 2)
        zeroed = kit.counter("o_zeroed")
        ids_out = kit.landing("o_ids_out", dmas=2 * NL + 2)
        step = kit.counter("o_step", 1)
        asked = kit.counter("o_exp_done", 2)
        counts = kit.counter("o_counts")
        marks = {}
        block = st.enter_context(nc.Block())

        @block.vector
        def _(dve):
            n = [0]
            V = nc.vector

            def link(ins):
                n[0] += 1
                ins.then_inc(step.sem, 1)
                dve.wait_ge(step.sem, n[0])

            def first_of(values, largest, out, width):
                link(V.tensor_tensor(out, values, largest.unsqueeze(2).to_broadcast([P, NL, width]), ALU.is_lt))
                link(V.scalar_tensor_tensor(out=out, in0=out, scalar=99.0, in1=iota[:, 0:width].unsqueeze(1).to_broadcast([P, NL, width]), op0=ALU.mult, op1=ALU.add))
                link(V.tensor_reduce(fi[:], out, AX, ALU.min))
                link(V.tensor_tensor(out, out, fi[:].unsqueeze(2).to_broadcast([P, NL, width]), ALU.is_equal))

            dve.wait_ge(c_in.sem(0), c_in.at(0))
            link(V.memset(zero[:], 0.0))
            lg4 = g["logits"][:, :, 0:NG]
            le32 = g["logits"][:, :, NG:].rearrange("p t (g e) -> p t g e", g=NG)
            link(V.tensor_reduce(mg[:], lg4, AX, ALU.max))
            link(V.tensor_tensor(e4[:], lg4, mg[:].unsqueeze(2).to_broadcast(T4), ALU.subtract))
            marks["shifted"] = n[0]
            first_of(lg4, mg[:], og[:], NG)
            link(V.tensor_tensor(w32[:], le32, og[:].unsqueeze(3).to_broadcast([P, NL, NG, EPG]), ALU.mult))
            link(V.tensor_reduce(le[:], w32[:].rearrange("p t g e -> p t e g"), AX, ALU.add))
            link(V.tensor_reduce(m12[:, 0], le[:], AX, ALU.max))
            first_of(le[:], m12[:, 0], o8[:, 0], EPG)
            link(V.scalar_tensor_tensor(out=c8[:], in0=o8[:, 0], scalar=-BIG, in1=le[:], op0=ALU.mult, op1=ALU.add))
            link(V.tensor_reduce(m12[:, 1], c8[:], AX, ALU.max))
            first_of(c8[:], m12[:, 1], o8[:, 1], EPG)
            link(V.tensor_tensor(ex[:], m12[:, 1], m12[:, 0], ALU.subtract))
            marks["difference"] = n[0]
            for k in range(2):
                link(V.tensor_tensor(oh[:, k], og[:].unsqueeze(3).to_broadcast([P, NL, NG, EPG]), o8[:, k].unsqueeze(2).to_broadcast([P, NL, NG, EPG]), ALU.mult))
            link(V.tensor_tensor(both[:], oh[:, 0].rearrange("p t g e -> p t (g e)"), oh[:, 1].rearrange("p t g e -> p t (g e)"), ALU.add))
            marks["chosen"] = n[0]
            dve.wait_ge(asked.sem, 2)
            link(V.tensor_reduce(den[:], e4[:], AX, ALU.add))
            link(V.scalar_tensor_tensor(out=den[:], in0=ex[:], scalar=1.0, in1=den[:], op0=ALU.add, op1=ALU.mult))
            link(V.reciprocal(g["wtop"][:, 0], den[:]))
            link(V.tensor_tensor(g["wtop"][:, 1], g["wtop"][:, 0], ex[:], ALU.mult))
            dve.wait_ge(counts.sem, counts.at(0))
            link(V.memset(tot[:, 0], 0.0))
            link(V.tensor_copy(rank[:], pr[:, 0].rearrange("p (t e) -> p t e", e=NE)))
            for t in range(NL):
                link(V.tensor_tensor(tot[:, t + 1], tot[:, t], pr[:, 1, t * NE:(t + 1) * NE], ALU.add))
            link(V.tensor_tensor_scan(start[:], tot[:, NL], zero[:], 0.0, ALU.add, ALU.add))
            link(V.tensor_tensor(start[:], start[:], tot[:, NL], ALU.subtract))
            link(V.tensor_tensor(rank[:], rank[:], tot[:, 0:NL], ALU.add))
            link(V.tensor_tensor(rank[:], rank[:], start[:].unsqueeze(1).to_broadcast(T32), ALU.add))
            for k in range(2):
                link(V.tensor_tensor(w32[:].rearrange("p t g e -> p t (g e)"), oh[:, k].rearrange("p t g e -> p t (g e)"), rank[:], ALU.mult))
                link(V.tensor_reduce(sl[:, k], w32[:].rearrange("p t g e -> p t (g e)"), AX, ALU.add))
            link(V.tensor_copy(g["slots"][:], sl[:]))
            marks["slots"] = n[0]
            link(V.tensor_tensor(cmp[:], tot[:, NL].unsqueeze(2).to_broadcast([P, NE, NL - 1]), mult[:].unsqueeze(1).to_broadcast([P, NE, NL - 1]), ALU.is_gt))
            link(V.tensor_reduce(nb[:], cmp[:], AX, ALU.add))
            link(V.tensor_scalar(nb[:], nb[:], 1.0, None, ALU.add))
            link(V.tensor_copy(g["spans"][:, 0], start[0:1]))
            link(V.tensor_copy(g["spans"][:, 1], nb[0:1]))
            for third in range(3):
                dve.wait_ge(w_high.sem, w_high.at(third))
                V.tensor_tensor(g["e_low"][:, third], g["e_raw"][:, third], g["e_high"][:, third].bitcast(F32), ALU.subtract)

        @block.scalar
        def _(act):
            act.wait_ge(step.sem, marks["shifted"])
            nc.scalar.activation(e4[:], e4[:], ACT.Exp).then_inc(asked.sem, 1)
            act.wait_ge(step.sem, marks["difference"])
            nc.scalar.activation(ex[:], ex[:], ACT.Exp).then_inc(asked.sem, 1)
            for third in range(3):
                act.wait_ge(w_in.sem(third), w_in.at(0))
                for n in range(2):
                    part = slice(n * THIRD // 2, (n + 1) * THIRD // 2)
                    nc.scalar.activation(g["e_high"][:, third, part], g["e_raw"][:, third, part], ACT.Copy).then_inc(w_high.sem, 1)

        @block.tensor
        def _(pe):
            pe.wait_ge(step.sem, marks["chosen"])
            flat = both[:].rearrange("p t e -> p (t e)")
            nc.tensor.matmul(pr[:, 0], g["tri"][:, 3], flat, start=True, stop=True)
            nc.tensor.matmul(pr[:, 1], g["tri"][:, 4], flat, start=True, stop=True).then_inc(counts.sem, 1)

        @block.sync
        def _(sp):
            sp.dma_start(iota[:], io["iota8"]).then_inc(c_in.sem(0), 16)
            sp.dma_start(mult[:], io["multiples"]).then_inc(c_in.sem(0), 16)
            sp.dma_start(token[:], io["tokens"]).then_inc(token_in.sem(0), 16)
            for third in range(3):
                load_third(sp, io, g["e_raw"], 0, third, w_in.sem(third))

        @block.gpsimd
        def _(pool):
            nc.gpsimd.memset(z[:], 0.0).then_inc(zeroed.sem, 1)
            pool.wait_ge(zeroed.sem, zeroed.at(0))
            pool.dma_start(dram["ys"][2 * SEQ:ROWS, :], z[:]).then_inc(ids_out.sem(0), 16)
            pool.wait_ge(token_in.sem(0), token_in.at(0))
            pool.dma_start(dram["ids"][2 * SEQ:ROWS, :], token[:, 0:1]).then_inc(ids_out.sem(0), 16)
            pool.wait_ge(step.sem, marks["slots"])
            for t in range(NL):
                for k in range(2):
                    pool.indirect_dma_start(dram["ids"], bass.IndirectOffsetOnAxis(ap=g["slots"][:, k, t:t + 1], axis=0), token[:, t:t + 1], None).then_inc(ids_out.sem(0), 16)
            pool.wait_ge(ids_out.sem(0), ids_out.at(0))


THIRD = KD * DE


def load_third(eng, io, raw, e, third, landed):
    for n, src in enumerate(("moe_w_gate", "moe_w_up")):
        if third < 2:
            to = raw[:, third].rearrange("p (k n f) -> p k n f", k=KD, n=2)[:, :, n]
            eng.dma_start(to, io[src][0, bass.ds(e, 1), :, third * 256:(third + 1) * 256].rearrange("o (k p) f -> p (o k) f", p=P)).then_inc(landed, 16)
        else:
            to = raw[:, third, n * THIRD // 2:(n + 1) * THIRD // 2].rearrange("p (k f) -> p k f", k=2)
            eng.dma_start(to, io["moe_w_down"][0, bass.ds(e, 1), n * 256:(n + 1) * 256].rearrange("o (k p) f -> p (o k) f", p=P)).then_inc(landed, 16)


def experts(nc, kit, io, g, dram):
    MAXB = NL
    HALF = THIRD // 2
    with ExitStack() as st:
        raw, wh, wl = g["e_raw"], g["e_high"], g["e_low"]
        ids = kit.sb("e_ids", [P, 1], I32, stack=st)
        xb = kit.sb("e_x", [P, D], stack=st)
        xT = kit.sb("e_xT", [P, 2, KD, P], F32R, stack=st)
        sg = kit.sb("e_sg", [P, 2, 256], stack=st)
        hid = kit.sb("e_hid", [P, DE], stack=st)
        hT = kit.sb("e_hT", [P, 2, DE // P, P], F32R, stack=st)
        y = kit.sb("e_y", [P, D], stack=st)
        pX = kit.ps("e_pX", [P, KD, P], st)
        pG = kit.ps("e_pG", [P, 2, 2, 256], st)
        pH = kit.ps("e_pH", [P, 2, 4, P], st)
        pY = kit.ps("e_pY", [P, 2, 512], st)
        w_in = kit.landing("e_w_in", 3, dmas=2)
        ids_in = kit.landing("e_ids_in")
        x_in = kit.landing("e_x_in")
        y_out = kit.landing("e_y_out", credit=16)
        whs = kit.counter("e_w_high_ready", 6)
        wls = kit.counter("e_w_low_ready", 6, credit=6)
        xTt = kit.counter("e_x_transposed", 1, credit=1)
        xTs = kit.counter("e_xT_high_ready", 1, credit=1)
        xTl = kit.counter("e_xT_low_ready", 1, credit=1)
        prodG = kit.counter("e_gate_up", 2, credit=2)
        sgs = kit.counter("e_silu", 2, credit=2)
        hids = kit.counter("e_hidden", 2, credit=2)
        hTt = kit.counter("e_hidden_transposed", 2, credit=2)
        hTs = kit.counter("e_hT_high_ready", 2, credit=2)
        hTl = kit.counter("e_hT_low_ready", 2, credit=2)
        prodY = kit.counter("e_down", 1, credit=1)
        ya = kit.counter("e_y_act", 1, credit=1)
        yd = kit.counter("e_y_dve", 1, credit=1)
        junk = kit.counter("e_paused")
        block = st.enter_context(nc.Block())

        def over_blocks(eng, body, enter=None):
            count = eng.alloc_register("e_block")
            eng.reg_mov(count, 0)
            at = eng.alloc_register("e_row")
            left = eng.alloc_register("e_blocks_left")

            def one(following):
                body(eng.snap(count, min_val=0, max_val=2 * NE), eng.snap(at, min_val=0, max_val=2 * SEQ), following)
                eng.reg_add(count, count, 1)
                eng.reg_add(at, at, P)

            def expert(e, following):
                blocks = eng.value_load(g["spans"][0:1, 1, bass.ds(e, 1)], min_val=1, max_val=MAXB)
                row0 = eng.value_load(g["spans"][0:1, 0, bass.ds(e, 1)], min_val=0, max_val=2 * SEQ)
                eng.reg_mov(at, row0)
                if enter:
                    enter(e)
                if following is None:
                    with eng.Fori(0, blocks) as j:
                        one(None)
                else:
                    eng.reg_mov(left, blocks)
                    with eng.If_ne(left, 1):
                        with eng.Fori(1, blocks) as j:
                            one(None)
                    one(following)

            with eng.Fori(0, NE - 1) as e:
                expert(e, e + 1)
            expert(NE - 1, None)
            return count

        @block.sync
        def _(sp):
            with sp.Fori(1, NE) as e:
                for third in range(3):
                    sp.wait_ge(wls.sem, wls.at(e - 1, 2 * third + 2))
                    load_third(sp, io, raw, e, third, w_in.sem(third))

        @block.gpsimd
        def _(pool):
            def gather():
                pool.indirect_dma_start(xb[:], None, dram["h2"], bass.IndirectOffsetOnAxis(ap=ids[:, 0:1], axis=0)).then_inc(x_in.sem(0), 16)

            def load(b, row, following):
                pool.wait_ge(xTt.sem, xTt.at(b - 1))
                pool.sem_inc(junk.sem, 1)
                pool.dma_start(ids[:], dram["ids"][bass.ds(row, P), :]).then_inc(ids_in.sem(0), 16)
                pool.wait_ge(ids_in.sem(0), ids_in.at(b))
                pool.sem_inc(junk.sem, 1)
                gather()
            count = over_blocks(pool, load)
            b = pool.snap(count, min_val=0, max_val=2 * NE)
            pool.wait_ge(xTt.sem, xTt.at(b - 1))
            pool.sem_inc(junk.sem, 1)
            gather()

        @block.tensor
        def _(pe):
            for x_ in (xTt, prodG, hTt, prodY):
                pe.sem_inc(x_.sem, x_.credit)
            ident = g["ident"][:, :]

            def turn_x(b):
                pe.wait_ge(x_in.sem(0), x_in.at(b))
                pe.wait_ge(xTl.sem, xTl.at(b - 1))
                for k in range(KD):
                    m = nc.tensor.transpose(pX[:, k], xb[:, k * P:(k + 1) * P], ident)
                m.then_inc(xTt.sem, 1)

            def turn_h(b, half):
                pe.wait_ge(hids.sem, hids.at(b, half + 1))
                pe.wait_ge(hTl.sem, hTl.at(b - 1, half + 1))
                for c in range(2):
                    m = nc.tensor.transpose(pH[:, half, c], hid[:, (2 * half + c) * P:(2 * half + c + 1) * P], ident)
                m.then_inc(hTt.sem, 1)

            def body(b, row, following, e=None):
                for half in range(2):
                    pe.wait_ge(hids.sem, hids.at(b - 1, half + 1))
                    pe.wait_ge(xTs.sem, xTs.at(b))
                    pe.wait_ge(wls.sem, wls.at(expert_of[0], 2 * half + 2))
                    for k in range(KD):
                        w = slice(k * 512, (k + 1) * 512)
                        nc.tensor.matmul(pG[:, half], xT[:, 0, k], wh[:, half, w], start=(k == 0), stop=False)
                        nc.tensor.matmul(pG[:, half], xT[:, 0, k], wl[:, half, w], start=False, stop=False)
                    pe.wait_ge(xTl.sem, xTl.at(b))
                    for k in range(KD):
                        m = nc.tensor.matmul(pG[:, half], xT[:, 1, k], wh[:, half, k * 512:(k + 1) * 512], start=False, stop=(k == KD - 1))
                    m.then_inc(prodG.sem, 1)
                turn_h(b, 0)
                turn_x(b + 1)
                turn_h(b, 1)
                pe.wait_ge(ya.sem, ya.at(b - 1))
                pe.wait_ge(yd.sem, yd.at(b - 1))
                pe.wait_ge(wls.sem, wls.at(expert_of[0], 6))
                for k in range(DE // P):
                    for part, with_ in ((0, wh), (0, wl), (1, wh)):
                        if k % 2 == 0:
                            part_ready = hTl if part else hTs
                            pe.wait_ge(part_ready.sem, part_ready.at(b, k // 2 + 1))
                        for n in range(2):
                            c0 = k * D + n * 512
                            m = nc.tensor.matmul(pY[:, n], hT[:, part, k], with_[:, 2, c0:c0 + 512], start=(k == 0 and part == 0 and with_ is wh),
                                                 stop=(k == DE // P - 1 and part == 1))
                m.then_inc(prodY.sem, 1)

            expert_of = [None]

            def enter(e):
                expert_of[0] = e
            turn_x(0)
            over_blocks(pe, body, enter)

        @block.scalar
        def _(act):
            for x_ in (xTs, sgs, hTs, ya):
                act.sem_inc(x_.sem, x_.credit)
            act.sem_inc(y_out.sem(0), 16)

            def xT_copy(b):
                act.wait_ge(xTt.sem, xTt.at(b))
                act.wait_ge(prodG.sem, prodG.at(b - 1))
                nc.scalar.activation(xT[:, 0], pX[:], ACT.Copy).then_inc(xTs.sem, 1)

            def high(e, third):
                act.wait_ge(w_in.sem(third), w_in.at(e - 1))
                for n in range(2):
                    part = slice(n * HALF, (n + 1) * HALF)
                    nc.scalar.activation(wh[:, third, part], raw[:, third, part], ACT.Copy).then_inc(whs.sem, 1)

            def body(b, row, following):
                for half in range(2):
                    act.wait_ge(prodG.sem, prodG.at(b, half + 1))
                    nc.scalar.activation(sg[:, half], pG[:, half, 0], ACT.Silu).then_inc(sgs.sem, 1)
                    if following is not None and half == 0:
                        high(following, 0)
                for half in range(2):
                    act.wait_ge(hTt.sem, hTt.at(b, half + 1))
                    act.wait_ge(prodY.sem, prodY.at(b - 1))
                    nc.scalar.activation(hT[:, 0, 2 * half:2 * half + 2], pH[:, half, 0:2], ACT.Copy).then_inc(hTs.sem, 1)
                    if half == 0:
                        xT_copy(b + 1)
                if following is not None:
                    high(following, 1)
                act.wait_ge(prodY.sem, prodY.at(b))
                act.wait_ge(y_out.sem(0), b * 16 + 16)
                nc.scalar.activation(y[:, 0:512], pY[:, 0], ACT.Copy).then_inc(ya.sem, 1)
                act.wait_ge(ya.sem, ya.at(b))
                act.wait_ge(yd.sem, yd.at(b))
                act.dma_start(dram["ys"][bass.ds(row, P), :], y[:]).then_inc(y_out.sem(0), 16)
                if following is not None:
                    high(following, 2)
            xT_copy(0)
            count = over_blocks(act, body)
            b = act.snap(count, min_val=0, max_val=2 * NE)
            act.wait_ge(y_out.sem(0), b * 16 + 16)
            act.sem_inc(junk.sem, 1)

        @block.vector
        def _(dve):
            for x_ in (xTl, hids, hTl, yd, wls):
                dve.sem_inc(x_.sem, x_.credit)

            def xT_low(b):
                dve.wait_ge(xTs.sem, xTs.at(b))
                nc.vector.tensor_tensor(xT[:, 1], pX[:], xT[:, 0].bitcast(F32), ALU.subtract).then_inc(xTl.sem, 1)

            def low(e, third):
                for n in range(2):
                    part = slice(n * HALF, (n + 1) * HALF)
                    dve.wait_ge(whs.sem, whs.at(e - 1, 2 * third + n + 1))
                    nc.vector.tensor_tensor(wl[:, third, part], raw[:, third, part], wh[:, third, part].bitcast(F32), ALU.subtract).then_inc(wls.sem, 1)

            def body(b, row, following):
                for half in range(2):
                    dve.wait_ge(sgs.sem, sgs.at(b, half + 1))
                    dve.wait_ge(hTt.sem, hTt.at(b - 1, half + 1))
                    nc.vector.tensor_tensor(hid[:, half * 256:(half + 1) * 256], sg[:, half], pG[:, half, 1], ALU.mult).then_inc(hids.sem, 1)
                    if following is not None and half == 0:
                        low(following, 0)
                for half in range(2):
                    dve.wait_ge(hTs.sem, hTs.at(b, half + 1))
                    nc.vector.tensor_tensor(hT[:, 1, 2 * half:2 * half + 2], pH[:, half, 0:2], hT[:, 0, 2 * half:2 * half + 2].bitcast(F32), ALU.subtract).then_inc(hTl.sem, 1)
                    if half == 0:
                        xT_low(b + 1)
                if following is not None:
                    low(following, 1)
                dve.wait_ge(prodY.sem, prodY.at(b))
                dve.wait_ge(y_out.sem(0), b * 16 + 16)
                nc.vector.tensor_copy(y[:, 512:D], pY[:, 1]).then_inc(yd.sem, 1)
                if following is not None:
                    low(following, 2)
            dve.sem_inc(wls.sem, wls.credit)
            xT_low(0)
            over_blocks(dve, body)


def combine(nc, kit, io, g, dram):
    B = 3
    with ExitStack() as st:
        yy = kit.sb("c_yy", [P, B, 2, D], stack=st)
        x1 = kit.sb("c_x1", [P, B, D], stack=st)
        v = kit.sb("c_v", [P, B, D], stack=st)
        sq = kit.sb("c_sq", [P, B, D], stack=st)
        ss = kit.sb("c_ss", [P, B, 2], stack=st)
        y_in = kit.landing("c_y_in", B, dmas=2)
        x_in = kit.landing("c_x_in", B)
        o_out = kit.landing("c_out", B)
        summed = kit.counter("c_summed", 2)
        ssq = kit.counter("c_ssq")
        eps_added = kit.counter("c_eps_added")
        rstd = kit.counter("c_rstd")
        outs = kit.counter("c_out_ready", 2)
        block = st.enter_context(nc.Block())

        @block.gpsimd
        def _(pool):
            def gather(t):
                if t >= B:
                    pool.wait_ge(summed.sem, summed.at(t - B))
                for k in range(2):
                    pool.indirect_dma_start(yy[:, t % B, k], None, dram["ys"], bass.IndirectOffsetOnAxis(ap=g["slots"][:, k, t:t + 1], axis=0)).then_inc(y_in.sem(t % B), 16)

            def root(t):
                pool.wait_ge(ssq.sem, ssq.at(t))
                rstd_root(nc, g, pool, eps_added, t, 1, ss[:, t % B, 1:2], ss[:, t % B, 0:1], D).then_inc(rstd.sem, 1)
            for t in range(NL + 2):
                if t < NL:
                    gather(t)
                if t >= 2:
                    root(t - 2)

        @block.sync
        def _(sp):
            def load(t):
                if t >= B:
                    sp.wait_ge(outs.sem, outs.at(t - B))
                sp.dma_start(x1[:, t % B], dram["x1"][t]).then_inc(x_in.sem(t % B), 16)

            def store(t):
                sp.wait_ge(outs.sem, outs.at(t))
                sp.dma_start(io["out0"][0, t * P:(t + 1) * P, :], v[:, t % B]).then_inc(o_out.sem(t % B), 16)
            for t in range(NL + B - 1):
                if t >= B - 1:
                    store(t - B + 1)
                if t < NL:
                    load(t)
            for s in range(B):
                sp.wait_ge(o_out.sem(s), 16 * len(range(s, NL, B)))

        @block.scalar
        def _(act):
            for t in range(NL):
                act.wait_ge(summed.sem, summed.at(t))
                if t >= B:
                    act.wait_ge(outs.sem, outs.at(t - B))
                nc.scalar.activation(sq[:, t % B], v[:, t % B], ACT.Square, accum_out=ss[:, t % B, 0:1]).then_inc(ssq.sem, 1)

        @block.vector
        def _(dve):
            def add(t):
                s = t % B
                dve.wait_ge(y_in.sem(s), y_in.at(t // B))
                if t >= B:
                    dve.wait_ge(o_out.sem(s), 16 * (t // B))
                nc.vector.tensor_scalar(v[:, s], yy[:, s, 0], g["wtop"][:, 0, t:t + 1], None, ALU.mult).then_inc(summed.sem, 1)
                dve.wait_ge(summed.sem, summed.at(t, 1))
                nc.vector.scalar_tensor_tensor(out=v[:, s], in0=yy[:, s, 1], scalar=g["wtop"][:, 1, t:t + 1], in1=v[:, s], op0=ALU.mult, op1=ALU.add).then_inc(summed.sem, 1)

            def finish(t):
                s = t % B
                dve.wait_ge(rstd.sem, rstd.at(t))
                nc.vector.scalar_tensor_tensor(out=v[:, s], in0=v[:, s], scalar=ss[:, s, 1:2], in1=g["mod"][:, 3], op0=ALU.mult, op1=ALU.mult).then_inc(outs.sem, 1)
                dve.wait_ge(outs.sem, outs.at(t, 1))
                dve.wait_ge(x_in.sem(s), x_in.at(t // B))
                nc.vector.tensor_tensor(v[:, s], v[:, s], x1[:, s], ALU.add).then_inc(outs.sem, 1)
            for t in range(NL + 1):
                if t < NL:
                    add(t)
                if t >= 1:
                    finish(t - 1)


def program(nc, io):
    kit = Kit(nc)
    g = globals_of(kit)

    def scratch(name, shape):
        return nc.dram_tensor(name, shape, F32).ap()
    dram = {
        "tok": scratch("by_token", (NT, P, NTOK)),
        "ch": scratch("by_channel", (NCH, P, NT * P)),
        "u": scratch("convolved", (NCH, P, NT * P)),
        "sb": scratch("backward_states", (NT, P, D)),
        "y": scratch("mixed", (NT, P, D)),
        "x1": scratch("after_mixing", (NL, P, D)),
        "h2": scratch("second_norm", (SEQ, D)),
        "ids": nc.dram_tensor("tokens_sorted", (ROWS, 1), I32).ap(),
        "ys": scratch("rows_done", (ROWS, D)),
    }
    first_only = ExitStack()
    for part in ("w_high", "w_low"):
        g[part] = kit.sb(part, [P, 4, KD, 512], F32R, stack=first_only)
    for stage in (modulation, projection, convolution, states, mixing, residual, routing, experts, combine):
        if stage is convolution:
            first_only.close()
            g.update(routing_globals_of(kit))
            mixing_only = ExitStack()
            g.update(mixing_globals_of(kit, mixing_only))
        if stage is mixing:
            g["w_out"] = kit.sb("w_out_sb", [P, KD, D], stack=mixing_only)
        if stage is residual or stage is routing:
            kit.retire()
        if stage is routing:
            mixing_only.close()
            experts_only = ExitStack()
            g["e_raw"] = kit.sb("e_w_whole", [P, 3, THIRD], stack=experts_only)
            g["e_high"] = kit.sb("e_w_high", [P, 3, THIRD], F32R, stack=experts_only)
            g["e_low"] = kit.sb("e_w_low", [P, 3, THIRD], F32R, stack=experts_only)
        if stage is combine:
            experts_only.close()
        stage(nc, kit, io, g, dram)
    kit.keep.close()


_INS = ['x', 'c', 'ctx', 'c_ctx', 'w_mod', 'b_mod', 'norm_pre_mix', 'norm_post_mix', 'norm_pre_ffn',
        'norm_post_ffn', 'w_in', 'w_out', 'ret_decay_f', 'ret_decay_b', 'ret_gn_w', 'ssd_conv_w',
        'ssd_conv_b', 'ssd_dt_bias_f', 'ssd_dt_bias_b', 'ssd_a_log_f', 'ssd_a_log_b', 'ssd_d',
        'ssd_norm_w', 'moe_w_rg', 'moe_b_rg', 'moe_w_re', 'moe_b_re', 'moe_w_gate', 'moe_w_up', 'moe_w_down']
_OUTS = [((1, SEQ, D), 'float32')]


def constants():
    f = np.float32
    quarter = P // 4
    freq = 10000.0 ** (-np.arange(quarter) / quarter)
    t = np.arange(SEQ)
    ang = np.stack([(t // 64)[:, None] * freq, (t % 64)[:, None] * freq], 1)
    cos = np.repeat(np.cos(ang)[:, :, None], 2, 2).reshape(SEQ, P)
    sin = np.stack([-np.sin(ang), np.sin(ang)], 2).reshape(SEQ, P)
    cos = np.concatenate([np.ones((CTX, P)), cos])
    sin = np.concatenate([np.zeros((CTX, P)), sin])
    s = float(P) ** -0.5
    rope = np.stack([cos, sin, cos * s, sin * s], 1).reshape(NT, P, 4 * P).astype(f)
    i = np.arange(P)
    rel = i[None, :] - i[:, None]
    return {
        "rope": rope,
        "ident": np.eye(P, dtype=f),
        "tri": np.stack([rel >= 0, rel < 0, rel <= 0, rel > 0, rel < 9999], 1).astype(f),
        "rel": np.stack([np.maximum(rel, 0), np.maximum(-rel, 0), np.tile(i + 1, (P, 1)), np.tile(P - i, (P, 1))], 1).astype(f),
        "relk": np.stack([P - 1 - i, i], 1).astype(f),
        "iota8": np.tile(np.arange(EPG).astype(f), (P, 1)),
        "tokens": (np.arange(NL)[None, :] * P + i[:, None]).astype(np.int32),
        "multiples": np.tile(np.arange(1, NL).astype(f) * P, (P, 1)),
    }


def kernel(**inputs):
    import concourse.bacc as _bacc
    from concourse import mybir as _mybir
    from concourse.bass_utils import run_bass_kernel_spmd as _run

    nc = _bacc.Bacc("TRN2", target_bir_lowering=False, num_devices=1)
    arrays, io = {}, {}
    given = {name: np.ascontiguousarray(inputs[name]) for name in _INS}
    for name, a in {**given, **constants()}.items():
        arrays[f"in_{name}_dram"] = a
        io[name] = nc.dram_tensor(f"in_{name}_dram", a.shape, _mybir.dt.from_np(a.dtype), kind="ExternalInput").ap()
    for i, (shape, dtype) in enumerate(_OUTS):
        dt = _mybir.dt.from_np(np.dtype(dtype))
        io[f"out{i}"] = nc.dram_tensor(f"out_{i}_dram", shape, dt, kind="ExternalOutput").ap()
    program(nc, io)
    r = _run(nc, [arrays], core_ids=[0])
    got = tuple(r.results[0][f"out_{i}_dram"] for i in range(len(_OUTS)))
    return got[0]
```
